# Optimizing a Trainium2 kernel written in Bass

```python
import jax, jax.numpy as jnp
from jax import lax
import numpy as np
import math

D_MODEL = 1024
BATCH = 1
SEQ = 512
DEPTH = 1

CHUNK = 64
LEFT_CHUNKS = 8
BAND = (LEFT_CHUNKS + 1) * CHUNK
N_HEADS = 8
HEAD_DIM = 64
D_ATTN = N_HEADS * HEAD_DIM
REL_CLIP = 128
D_CONV = 512
CONV_WIDTH = 31
N_BRANCH = 2
D_IN = 3 * D_ATTN + 2 * D_CONV + N_BRANCH * D_MODEL
D_FF = 2816
EPS = 1e-6


def rms_norm(x, g):
    xf = x.astype(jnp.float32)
    y = xf * lax.rsqrt(jnp.mean(xf * xf, axis=-1, keepdims=True) + EPS)
    return (y * g.astype(jnp.float32)).astype(x.dtype)

def layer_norm(x, g, b):
    xf = x.astype(jnp.float32)
    mu = jnp.mean(xf, axis=-1, keepdims=True)
    var = jnp.mean(jnp.square(xf - mu), axis=-1, keepdims=True)
    y = (xf - mu) * lax.rsqrt(var + EPS)
    return (y * g.astype(jnp.float32) + b.astype(jnp.float32)).astype(x.dtype)

def swiglu(x, w_gate, w_up, w_down):
    return (jax.nn.silu(x @ w_gate) * (x @ w_up)) @ w_down

def chunked_attention(q, k, v, rel_table):
    B, S, H, Dh = q.shape
    nc = S // CHUNK
    qc = q.reshape(B, nc, CHUNK, H, Dh)
    pad = ((0, 0), (LEFT_CHUNKS, 0), (0, 0), (0, 0), (0, 0))
    kp = jnp.pad(k.reshape(B, nc, CHUNK, H, Dh), pad)
    vp = jnp.pad(v.reshape(B, nc, CHUNK, H, Dh), pad)
    k_band = jnp.concatenate([kp[:, j:j + nc] for j in range(LEFT_CHUNKS + 1)], axis=2)
    v_band = jnp.concatenate([vp[:, j:j + nc] for j in range(LEFT_CHUNKS + 1)], axis=2)
    scores = jnp.einsum('bnqhd,bnkhd->bnhqk', qc, k_band).astype(jnp.float32) * (HEAD_DIM ** -0.5)
    qi = jnp.arange(CHUNK)[:, None]
    kj = jnp.arange(BAND)[None, :]
    dist = qi + LEFT_CHUNKS * CHUNK - kj
    idx = jnp.clip(dist, -REL_CLIP, REL_CLIP) + REL_CLIP
    bias = rel_table.astype(jnp.float32)[:, idx]
    scores = scores + bias[None, None]
    key_chunk = jnp.arange(nc)[:, None] + (jnp.arange(BAND) // CHUNK)[None, :] - LEFT_CHUNKS
    valid = (key_chunk >= 0)[None, :, None, None, :]
    scores = jnp.where(valid, scores, jnp.float32(-1e30))
    p = jax.nn.softmax(scores, axis=-1).astype(v.dtype)
    out = jnp.einsum('bnhqk,bnkhd->bnqhd', p, v_band)
    return out.reshape(B, S, H * Dh)

def conv_module(c_in, glu_bias, dw_w, dw_b, ln_g, ln_b, w_out):
    c = c_in + glu_bias
    c = c[..., :D_CONV] * jax.nn.sigmoid(c[..., D_CONV:])
    c = lax.conv_general_dilated(
        c, dw_w.astype(c.dtype), window_strides=(1,), padding=((CONV_WIDTH - 1, 0),),
        dimension_numbers=('NWC', 'WIO', 'NWC'), feature_group_count=D_CONV) + dw_b
    c = jax.nn.silu(layer_norm(c, ln_g, ln_b))
    return c @ w_out

def hybrid_mixer(u, w_in, gate_bias, rel_table, w_attn_out, conv_glu_bias, conv_dw_w,
                 conv_dw_b, conv_ln_g, conv_ln_b, conv_w_out, w_out):
    B, S, _ = u.shape
    proj = u @ w_in
    q, k, v, c_in, g = jnp.split(
        proj, [D_ATTN, 2 * D_ATTN, 3 * D_ATTN, 3 * D_ATTN + 2 * D_CONV], axis=-1)
    shp = (B, S, N_HEADS, HEAD_DIM)
    y_a = chunked_attention(q.reshape(shp), k.reshape(shp), v.reshape(shp), rel_table) @ w_attn_out
    y_b = conv_module(c_in, conv_glu_bias, conv_dw_w, conv_dw_b, conv_ln_g, conv_ln_b, conv_w_out)
    gates = jax.nn.sigmoid(g + gate_bias)
    merged = gates[..., :D_MODEL] * y_a + gates[..., D_MODEL:] * y_b
    return merged @ w_out

def first_inputs(seed: int = 0) -> dict:
    key = jax.random.key(seed)
    ks = jax.random.split(key, 32)
    L, D = DEPTH, D_MODEL

    def w(k, shape, fan_in):
        return jax.random.normal(k, shape, jnp.float32) * (fan_in ** -0.5)

    def gain(k, shape):
        return 1.0 + 0.05 * jax.random.normal(k, shape, jnp.float32)

    def small(k, shape, s=0.02):
        return s * jax.random.normal(k, shape, jnp.float32)

    return {
        "x": jax.random.normal(ks[0], (BATCH, SEQ, D), jnp.float32),
        "ffn1_norm_pre": gain(ks[1], (L, D)),
        "ffn1_w_gate": w(ks[2], (L, D, D_FF), D),
        "ffn1_w_up": w(ks[3], (L, D, D_FF), D),
        "ffn1_w_down": w(ks[4], (L, D_FF, D), D_FF),
        "ffn1_norm_post": gain(ks[5], (L, D)),
        "mix_norm_pre": gain(ks[6], (L, D)),
        "w_in": w(ks[7], (L, D, D_IN), D),
        "gate_bias": small(ks[8], (L, N_BRANCH * D), 0.1),
        "rel_table": small(ks[9], (L, N_HEADS, 2 * REL_CLIP + 1), 0.5),
        "w_attn_out": w(ks[10], (L, D_ATTN, D), D_ATTN),
        "conv_glu_bias": small(ks[11], (L, 2 * D_CONV)),
        "conv_dw_w": w(ks[12], (L, CONV_WIDTH, 1, D_CONV), CONV_WIDTH),
        "conv_dw_b": small(ks[13], (L, D_CONV)),
        "conv_ln_g": gain(ks[14], (L, D_CONV)),
        "conv_ln_b": small(ks[15], (L, D_CONV)),
        "conv_w_out": w(ks[16], (L, D_CONV, D), D_CONV),
        "w_out": w(ks[17], (L, D, D), D),
        "mix_norm_post": gain(ks[18], (L, D)),
        "ffn2_norm_pre": gain(ks[19], (L, D)),
        "ffn2_w_gate": w(ks[20], (L, D, D_FF), D),
        "ffn2_w_up": w(ks[21], (L, D, D_FF), D),
        "ffn2_w_down": w(ks[22], (L, D_FF, D), D_FF),
        "ffn2_norm_post": gain(ks[23], (L, D)),
    }

def first_block(x, ffn1_norm_pre, ffn1_w_gate, ffn1_w_up, ffn1_w_down, ffn1_norm_post,
              mix_norm_pre, w_in, gate_bias, rel_table, w_attn_out, conv_glu_bias,
              conv_dw_w, conv_dw_b, conv_ln_g, conv_ln_b, conv_w_out, w_out, mix_norm_post,
              ffn2_norm_pre, ffn2_w_gate, ffn2_w_up, ffn2_w_down, ffn2_norm_post):
    h = x
    for l in range(DEPTH):
        f = swiglu(rms_norm(h, ffn1_norm_pre[l]), ffn1_w_gate[l], ffn1_w_up[l], ffn1_w_down[l])
        h = h + 0.5 * rms_norm(f, ffn1_norm_post[l])
        m = hybrid_mixer(rms_norm(h, mix_norm_pre[l]), w_in[l], gate_bias[l], rel_table[l],
                         w_attn_out[l], conv_glu_bias[l], conv_dw_w[l], conv_dw_b[l],
                         conv_ln_g[l], conv_ln_b[l], conv_w_out[l], w_out[l])
        h = h + rms_norm(m, mix_norm_post[l])
        f = swiglu(rms_norm(h, ffn2_norm_pre[l]), ffn2_w_gate[l], ffn2_w_up[l], ffn2_w_down[l])
        h = h + 0.5 * rms_norm(f, ffn2_norm_post[l])
    return h


DEPTH_2 = 2

Q_BLOCK = 128
N_MIXERS = 2
N_RET_LAYERS = (DEPTH_2 + 1) // 2
N_DIFF_LAYERS = DEPTH_2 // 2
MIX_WIDTH = D_MODEL
MEM_LEN = 256
MEM_HEADS = 4
MEM_HEAD_DIM = 64
MEM_WIDTH = MEM_HEADS * MEM_HEAD_DIM
MAIN_WIDTH = MIX_WIDTH - MEM_WIDTH
RET_HEADS = 6
RET_V_DIM = MAIN_WIDTH // RET_HEADS
RET_QK_DIM = RET_V_DIM // 2
DIFF_HEADS = 6
DIFF_HEAD_DIM = MAIN_WIDTH // (2 * DIFF_HEADS)
DIFF_V_DIM = 2 * DIFF_HEAD_DIM
IN_WIDTH = 3 * MAIN_WIDTH + MEM_WIDTH
FFN_DIM = -(-8 * D_MODEL // (3 * 256)) * 256


def rms_norm_2(x, w):
    x32 = x.astype(jnp.float32)
    y = x32 * lax.rsqrt(jnp.mean(x32 * x32, axis=-1, keepdims=True) + EPS)
    return (y * w.astype(jnp.float32)).astype(x.dtype)

def retention(q, k, v):
    B, S, H, dk = q.shape
    dv = v.shape[-1]
    nc = S // CHUNK
    dt = q.dtype
    log_gamma = jnp.log(1.0 - 2.0 ** (-5.0 - jnp.arange(H, dtype=jnp.float32)))
    k = k * (dk ** -0.5)
    q = q.reshape(B, nc, CHUNK, H, dk)
    k = k.reshape(B, nc, CHUNK, H, dk)
    v = v.reshape(B, nc, CHUNK, H, dv)
    pos = jnp.arange(CHUNK, dtype=jnp.float32)
    d_in = jnp.exp(log_gamma[:, None, None] * jnp.abs(pos[:, None] - pos[None, :])).astype(dt)
    s_in = jnp.einsum('bnihd,bnjhd->bnhij', q, k) * d_in
    o_in = jnp.einsum('bnhij,bnjhe->bnihe', s_in, v)
    k_dec = jnp.exp(log_gamma[:, None] * (CHUNK - 1 - pos)[None, :]).astype(dt)
    kv = jnp.einsum('bnjhd,hj,bnjhe->bnhde', k, k_dec, v)
    chunk_dec = jnp.exp(log_gamma * CHUNK).astype(dt)[:, None, None]

    def step(state, kv_c):
        return state * chunk_dec + kv_c, state

    init = jnp.zeros((B, H, dk, dv), dtype=kv.dtype)
    _, prev = lax.scan(step, init, jnp.moveaxis(kv, 1, 0))
    prev = jnp.moveaxis(prev, 0, 1)
    q_dec = jnp.exp(log_gamma[:, None] * (pos + 1.0)[None, :]).astype(dt)
    o_x = jnp.einsum('bnihd,hi,bnhde->bnihe', q, q_dec, prev)
    return (o_in + o_x).reshape(B, S, H, dv)

def diff_attention(q, k, v, lam):
    B, S, H, _, d = q.shape
    nb = S // Q_BLOCK
    slopes = 2.0 ** (-8.0 * jnp.arange(1, H + 1, dtype=jnp.float32) / H)
    s_pos = jnp.arange(S)
    s_chunk = s_pos // CHUNK
    qb = jnp.moveaxis(q.reshape(B, nb, Q_BLOCK, H, 2, d), 1, 0)
    starts = jnp.arange(nb, dtype=jnp.int32) * Q_BLOCK
    scale = d ** -0.5

    def block(args):
        qblk, t0 = args
        t = t0 + jnp.arange(Q_BLOCK)
        sc = jnp.einsum('bihcd,bjhcd->bhcij', qblk, k).astype(jnp.float32) * scale
        dist = jnp.abs(t[:, None] - s_pos[None, :]).astype(jnp.float32)
        bias = -slopes[:, None, None] * dist[None]
        allowed = s_chunk[None, :] <= (t // CHUNK)[:, None]
        sc = jnp.where(allowed, sc + bias[None, :, None], -jnp.inf)
        p = jax.nn.softmax(sc, axis=-1)
        a = p[:, :, 0] - lam * p[:, :, 1]
        return jnp.einsum('bhij,bjhe->bihe', a.astype(v.dtype), v)

    o = lax.map(block, (qb, starts))
    return jnp.moveaxis(o, 0, 1).reshape(B, S, H, v.shape[-1])

def memory_attention(qc, mk, mv):
    sc = jnp.einsum('bshd,bmhd->bhsm', qc, mk).astype(jnp.float32) * (qc.shape[-1] ** -0.5)
    p = jax.nn.softmax(sc, axis=-1).astype(mv.dtype)
    return jnp.einsum('bhsm,bmhd->bshd', p, mv)

def second_inputs(seed: int = 0) -> dict:
    key = jax.random.key(seed)
    ks = jax.random.split(key, 24)
    n = jax.random.normal
    f = jnp.float32

    def gain(k, shape):
        return 1.0 + 0.02 * n(k, shape, f)

    return {
        'x': n(ks[0], (BATCH, SEQ, D_MODEL), f),
        'mem': n(ks[1], (BATCH, MEM_LEN, D_MODEL), f),
        'attn_norm_w': gain(ks[2], (DEPTH_2, D_MODEL)),
        'w_in': n(ks[3], (DEPTH_2, D_MODEL, IN_WIDTH), f) * D_MODEL ** -0.5,
        'w_out': n(ks[4], (DEPTH_2, MIX_WIDTH, D_MODEL), f) * MIX_WIDTH ** -0.5,
        'mem_norm_w': gain(ks[5], (D_MODEL,)),
        'w_mem_kv': n(ks[6], (DEPTH_2, D_MODEL, 2 * MEM_WIDTH), f) * D_MODEL ** -0.5,
        'mem_q_norm_w': gain(ks[7], (DEPTH_2, MEM_HEAD_DIM)),
        'mem_k_norm_w': gain(ks[8], (DEPTH_2, MEM_HEAD_DIM)),
        'ret_gn_w': gain(ks[9], (N_RET_LAYERS, RET_HEADS, RET_V_DIM)),
        'diff_q_norm_w': gain(ks[10], (N_DIFF_LAYERS, DIFF_HEAD_DIM)),
        'diff_k_norm_w': gain(ks[11], (N_DIFF_LAYERS, DIFF_HEAD_DIM)),
        'diff_lambda_q1': 0.1 * n(ks[12], (N_DIFF_LAYERS, DIFF_HEAD_DIM), f),
        'diff_lambda_k1': 0.1 * n(ks[13], (N_DIFF_LAYERS, DIFF_HEAD_DIM), f),
        'diff_lambda_q2': 0.1 * n(ks[14], (N_DIFF_LAYERS, DIFF_HEAD_DIM), f),
        'diff_lambda_k2': 0.1 * n(ks[15], (N_DIFF_LAYERS, DIFF_HEAD_DIM), f),
        'diff_subln_w': gain(ks[16], (N_DIFF_LAYERS, DIFF_V_DIM)),
        'ffn_norm_w': gain(ks[17], (DEPTH_2, D_MODEL)),
        'w_gate_up': n(ks[18], (DEPTH_2, D_MODEL, 2 * FFN_DIM), f) * D_MODEL ** -0.5,
        'w_down': n(ks[19], (DEPTH_2, FFN_DIM, D_MODEL), f) * FFN_DIM ** -0.5,
    }

def second_block(x, mem, attn_norm_w, w_in, w_out, mem_norm_w, w_mem_kv, mem_q_norm_w,
              mem_k_norm_w, ret_gn_w, diff_q_norm_w, diff_k_norm_w, diff_lambda_q1,
              diff_lambda_k1, diff_lambda_q2, diff_lambda_k2, diff_subln_w, ffn_norm_w,
              w_gate_up, w_down):
    B, S, _ = x.shape
    M = mem.shape[1]
    memn = rms_norm_2(mem, mem_norm_w)
    for layer in range(DEPTH_2):
        h = rms_norm_2(x, attn_norm_w[layer])
        u = h @ w_in[layer]
        j = layer // N_MIXERS
        if layer % N_MIXERS == 0:
            nqk = RET_HEADS * RET_QK_DIM
            q = u[..., :nqk].reshape(B, S, RET_HEADS, RET_QK_DIM)
            k = u[..., nqk:2 * nqk].reshape(B, S, RET_HEADS, RET_QK_DIM)
            v = u[..., 2 * nqk:2 * nqk + MAIN_WIDTH].reshape(B, S, RET_HEADS, RET_V_DIM)
            g = u[..., 2 * nqk + MAIN_WIDTH:3 * MAIN_WIDTH]
            o = rms_norm_2(retention(q, k, v), ret_gn_w[j])
            o_main = jax.nn.silu(g) * o.reshape(B, S, MAIN_WIDTH)
        else:
            q = u[..., :MAIN_WIDTH].reshape(B, S, DIFF_HEADS, 2, DIFF_HEAD_DIM)
            k = u[..., MAIN_WIDTH:2 * MAIN_WIDTH].reshape(B, S, DIFF_HEADS, 2, DIFF_HEAD_DIM)
            v = u[..., 2 * MAIN_WIDTH:3 * MAIN_WIDTH].reshape(B, S, DIFF_HEADS, DIFF_V_DIM)
            q = rms_norm_2(q, diff_q_norm_w[j])
            k = rms_norm_2(k, diff_k_norm_w[j])
            lambda_init = 0.8 - 0.6 * math.exp(-0.3 * layer)
            lq1 = diff_lambda_q1[j].astype(jnp.float32)
            lk1 = diff_lambda_k1[j].astype(jnp.float32)
            lq2 = diff_lambda_q2[j].astype(jnp.float32)
            lk2 = diff_lambda_k2[j].astype(jnp.float32)
            lam = jnp.exp(jnp.sum(lq1 * lk1)) - jnp.exp(jnp.sum(lq2 * lk2)) + lambda_init
            o = rms_norm_2(diff_attention(q, k, v, lam), diff_subln_w[j]) * (1.0 - lambda_init)
            o_main = o.reshape(B, S, MAIN_WIDTH)
        qc = rms_norm_2(u[..., 3 * MAIN_WIDTH:].reshape(B, S, MEM_HEADS, MEM_HEAD_DIM), mem_q_norm_w[layer])
        mkv = memn @ w_mem_kv[layer]
        mk = rms_norm_2(mkv[..., :MEM_WIDTH].reshape(B, M, MEM_HEADS, MEM_HEAD_DIM), mem_k_norm_w[layer])
        mv = mkv[..., MEM_WIDTH:].reshape(B, M, MEM_HEADS, MEM_HEAD_DIM)
        o_mem = memory_attention(qc, mk, mv).reshape(B, S, MEM_WIDTH)
        x = x + jnp.concatenate([o_main, o_mem], axis=-1) @ w_out[layer]
        h = rms_norm_2(x, ffn_norm_w[layer])
        gu = h @ w_gate_up[layer]
        x = x + (jax.nn.silu(gu[..., :FFN_DIM]) * gu[..., FFN_DIM:]) @ w_down[layer]
    return x


def setup_inputs(seed=0):
    out = dict(first_inputs(seed))
    for name, value in second_inputs(seed + 1).items():
        if name != "x":
            out[name + "_2"] = value
    return out


def reference(
    x, ffn1_norm_pre, ffn1_w_gate, ffn1_w_up, ffn1_w_down, ffn1_norm_post, mix_norm_pre, w_in,
    gate_bias, rel_table, w_attn_out, conv_glu_bias, conv_dw_w, conv_dw_b, conv_ln_g, conv_ln_b,
    conv_w_out, w_out, mix_norm_post, ffn2_norm_pre, ffn2_w_gate, ffn2_w_up, ffn2_w_down,
    ffn2_norm_post, mem_2, attn_norm_w_2, w_in_2, w_out_2, mem_norm_w_2, w_mem_kv_2,
    mem_q_norm_w_2, mem_k_norm_w_2, ret_gn_w_2, diff_q_norm_w_2, diff_k_norm_w_2,
    diff_lambda_q1_2, diff_lambda_k1_2, diff_lambda_q2_2, diff_lambda_k2_2, diff_subln_w_2,
    ffn_norm_w_2, w_gate_up_2, w_down_2,
):
    x = first_block(
        x, ffn1_norm_pre, ffn1_w_gate, ffn1_w_up, ffn1_w_down, ffn1_norm_post, mix_norm_pre,
        w_in, gate_bias, rel_table, w_attn_out, conv_glu_bias, conv_dw_w, conv_dw_b, conv_ln_g,
        conv_ln_b, conv_w_out, w_out, mix_norm_post, ffn2_norm_pre, ffn2_w_gate, ffn2_w_up,
        ffn2_w_down, ffn2_norm_post,
    )
    return second_block(
        x, mem_2, attn_norm_w_2, w_in_2, w_out_2, mem_norm_w_2, w_mem_kv_2, mem_q_norm_w_2,
        mem_k_norm_w_2, ret_gn_w_2, diff_q_norm_w_2, diff_k_norm_w_2, diff_lambda_q1_2,
        diff_lambda_k1_2, diff_lambda_q2_2, diff_lambda_k2_2, diff_subln_w_2, ffn_norm_w_2,
        w_gate_up_2, w_down_2,
    )


_drawn_inputs = setup_inputs


def setup_inputs(seed=0):
    import zlib

    import numpy as np

    out = dict(_drawn_inputs(seed))
    spreads = {}
    factors = {'ffn2_norm_post': 2.824,
     'attn_norm_w_2': 3.184,
     'mem_norm_w_2': 8.0,
     'mem_q_norm_w_2': 8.0,
     'mem_k_norm_w_2': 8.0,
     'ret_gn_w_2': 8.0,
     'diff_q_norm_w_2': 8.0,
     'diff_k_norm_w_2': 8.0,
     'diff_lambda_q2_2': 8.0,
     'diff_lambda_k2_2': 8.0,
     'diff_subln_w_2': 181.729,
     'ffn_norm_w_2': 4.082,
     'diff_lambda_q1_2': 3.849}
    for name, (base, spread) in spreads.items():
        noise = np.random.default_rng([zlib.crc32(name.encode()), seed]).standard_normal(out[name].shape)
        drawn = base * np.exp(spread * noise) if base else spread * noise
        out[name] = __import__('jax').numpy.asarray(drawn.astype(out[name].dtype))
    for name, factor in factors.items():
        out[name] = (out[name] * factor).astype(out[name].dtype)
    return out
```

```python
from contextlib import ExitStack
import math

import numpy as np
import concourse.bass as bass
from concourse import mybir

F32 = mybir.dt.float32
F32R = mybir.dt.float32r
ALU = mybir.AluOpType
ACT = mybir.ActivationFunctionType
AX_X = mybir.AxisListType.X

P = 128
S = 512
D = 1024
ND = D // P
TT = S // P
FF = 2816
NF = FF // P
EPS = 1e-6
MEM = 256
NMT = MEM // P
NEG = -1e30

HEADS, HD = 8, 64
CH = 512 // P
TAPS = 31
PAD = TAPS - 1
RET_H, DIFF_H, MEM_H = 6, 6, 4
MAIN = 768
NM = MAIN // P
W_IN2 = 3 * MAIN + 256
N_IN2 = W_IN2 // P
N_IN1 = 4608 // P
LAMBDA_INIT = 0.8 - 0.6 * math.exp(-0.3)

RING = 4
AHEAD = 3

GU = 2 * NF
F1_GU = 0
F1_DN = F1_GU + GU
MX_IN = F1_DN + NF
MX_CO = MX_IN + N_IN1
MX_AO = MX_CO + 4
MX_OUT = MX_AO + 4
F2_GU = MX_OUT + ND
F2_DN = F2_GU + GU
LAYER0 = F2_DN + NF
LAYER_UNITS = 4 + N_IN2 + ND + GU + NF
UNITS = LAYER0 + 2 * LAYER_UNITS

COLS = {}


def _columns():
    at = 0
    for name, n in (
        ("f1_pre", ND), ("f1_post", ND), ("mx_pre", ND), ("gate_bias", 2 * ND), ("glu_bias", 2 * CH),
        ("dw_b", CH), ("ln_g", CH), ("ln_b", CH), ("mx_post", ND), ("f2_pre", ND), ("f2_post", ND),
        ("dw_w", CH * TAPS), ("attn0", ND), ("attn1", ND), ("mem", ND), ("mq0", 1), ("mq1", 1),
        ("mk0", 1), ("mk1", 1), ("ret_gn", RET_H), ("dq", 1), ("dk", 1), ("subln", 1),
        ("ffn0", ND), ("ffn1", ND), ("lq1", 1), ("lk1", 1), ("lq2", 1), ("lk2", 1),
    ):
        COLS[name] = (at, n)
        at += n
    return at


NCOLS = _columns()

SEL64_AT, SEL64_W = 2 * P, 22
SEL128_AT, SEL128_W = 2 * P + 22, 11
NCONST = 2 * P + 22 + 11


def shape_constants():
    p = np.arange(P)
    const = np.zeros((P, NCONST), np.float32)
    const[p, p] = 1.0
    const[:, P:2 * P] = 1.0
    const[:64, SEL64_AT + 10] = 1.0
    const[64:, SEL64_AT + 11] = 1.0
    const[:, SEL128_AT + 5] = 1.0
    spread64 = np.zeros((12, 6, P), np.float32)
    spread128 = np.zeros((6, 6, P), np.float32)
    for i in range(6):
        spread64[2 * i, i, :64] = 1.0
        spread64[2 * i + 1, i, 64:] = 1.0
        spread128[i, i, :] = 1.0
    log_gamma = np.log(np.float32(1.0) - np.float32(2.0) ** (np.float32(-5.0) - np.arange(RET_H, dtype=np.float32)))
    u = np.arange(S)
    dist = np.abs(u[None, :] - p[:, None]).astype(np.float32)
    seen = (u[None, :] // 64) >= (p[:, None] // 64)
    decay = np.where(seen[None], np.exp(log_gamma[:, None, None] * dist[None]), 0.0).astype(np.float32)
    decay *= np.float32(0.125)
    slopes = (2.0 ** (-8.0 * np.arange(1, DIFF_H + 1, dtype=np.float32) / DIFF_H)).astype(np.float32)
    rel = u - 384
    dist = np.abs(p[:, None] - rel[None, :]).astype(np.float32)
    seen = np.floor_divide(rel[None, :], 64) <= (p[:, None] // 64)
    alibi = np.where(seen[None], -slopes[:, None, None] * dist[None], np.float32(NEG)).astype(np.float32)
    return {
        "const": const,
        "spread64": spread64.reshape(12, 6 * P),
        "spread128": spread128.reshape(6, 6 * P),
        "decay": np.ascontiguousarray(decay.transpose(1, 0, 2)),
        "alibi": np.ascontiguousarray(alibi.transpose(1, 0, 2)),
    }


class Attention:

    def __init__(self, name, steps, maps, per_group, first_step, first_group):
        self.name, self.steps, self.maps, self.per_group = name, steps, maps, per_group
        self.s0, self.g0 = first_step, first_group
        self.m0 = None


def build(nc, d, out):
    with ExitStack() as ctx:
        ctx.enter_context(nc.sbuf_tensor("fence", [P, 53200], F32))
        FENCE = FENCE_AT
        taken = [FENCE]

        def place(name, shape, dt, at=None):
            size = 4 * int(np.prod(shape[1:]))
            if at is None:
                at = taken[0]
                taken[0] += (size + 31) // 32 * 32
            return nc.alloc_sbuf_tensor_at(name, shape, dt, offset=at)

        def sem(name):
            return ctx.enter_context(nc.semaphore(name))

        H = place("H", [P, ND, S], F32)
        XH = place("XH", [P, ND, S], F32R)
        XL = place("XL", [P, ND, S], F32R)
        RAW = place("RAW", [P, RING, D], F32)
        WHI = place("WHI", [P, RING, D], F32R)
        WLO = place("WLO", [P, RING, D], F32R)
        R = place("R", [P, S], F32)
        ACC = place("ACC", [P, S], F32)
        SQ = place("SQ", [P, 2, S], F32)
        tmp_at = taken[0]
        TMP = place("TMP", [P, 4, S], F32)
        MTOK = place("MTOK", [P, NMT, D], F32, tmp_at)
        COL = place("COL", [P, NCOLS], F32)
        CONST = place("CONST", [P, NCONST], F32)
        EPSC = place("EPSC", [P, 2], F32)
        STAT = place("STAT", [P, 32], F32)
        LAM = place("LAM", [P, 8], F32)
        arena = taken[0]
        IDENT, ONES = CONST[:, 0:P], CONST[:, P:2 * P]

        KB = 2048
        AH = place("AH", [P, NF, S], F32R, arena)
        AL = place("AL", [P, NF, S], F32R, arena + NF * KB)
        FG = place("FG", [P, ND, S], F32, arena)
        XTOK = place("XTOK", [P, TT, D], F32, arena)
        U = place("U", [P, N_IN1, S], F32, arena)
        CO = place("CO", [P, CH, S], F32, arena)
        V1 = place("V1", [P, TT, 512], F32, arena + 4 * KB)
        SB1 = place("SB1", [P, 3, S], F32, arena + 16 * KB)
        CPAD = 544
        C = place("C", [P, CH, CPAD], F32, arena + 36 * KB)
        BIAS1 = place("BIAS1", [P, HEADS, 256], F32, arena + 36 * KB)
        PT1 = place("PT1", [P, 2, S], F32, arena + 36 * KB + CH * CPAD * 4)
        V2 = place("V2", [P, TT, MAIN], F32, arena + 20 * KB)
        TAB = place("TAB", [P, 6, S], F32, arena + 26 * KB)
        SB2 = place("SB2", [P, 6, S], F32, arena + 32 * KB)
        PT2 = place("PT2", [P, 2, S], F32, arena + 38 * KB)
        MKT = place("MKT", [P, NMT, MEM], F32, arena + 40 * KB)
        MV = place("MV", [P, NMT, MEM], F32, arena + 41 * KB)
        SP64 = place("SP64", [P, 6, P], F32, arena + 42 * KB)
        SP128 = place("SP128", [P, 6, P], F32, arena + 42 * KB + 3072)
        MVT = place("MVT", [P, NMT, MEM], F32, arena + 38 * KB)
        MH = place("MH", [P, ND, MEM], F32R, arena + 20 * KB)
        ML = place("ML", [P, ND, MEM], F32R, arena + 24 * KB)
        YH = place("YH", [P, ND, S], F32R, arena)
        YL = place("YL", [P, ND, S], F32R, arena + 20 * KB)
        O2 = place("O2", [P, 6, S], F32, arena + 12 * KB)
        O2R = place("O2R", [P, 6, S], F32, arena + 6 * KB)

        bank = [ctx.enter_context(nc.psum_tensor(f"bank{i}", [P, S], F32)) for i in range(8)]

        const_in = sem("const_in")
        eps_set = sem("eps_set")
        x_in = sem("x_in")
        raw_in = [sem(f"raw_in{i}") for i in range(RING)]
        hi_ready, lo_ready, unit_done = sem("hi_ready"), sem("lo_ready"), sem("unit_done")
        tile_ready = sem("tile_ready")
        xT_done = sem("xT_done")
        h_new, xh_ready, x_ready = sem("h_new"), sem("xh_ready"), sem("x_ready")
        sq_ready, acc_done = sem("sq_ready"), sem("acc_done")
        stat_done, root_done, rstd_done = sem("stat_done"), sem("root_done"), sem("rstd_done")
        g_scaled, silu_done, u_scaled = sem("g_scaled"), sem("silu_done"), sem("u_scaled")
        a_done, ah_ready, al_ready = sem("a_done"), sem("ah_ready"), sem("al_ready")
        fsq_done, fg_done, fstat_done = sem("fsq_done"), sem("fg_done"), sem("fstat_done")
        froot_done, frstd_done, f_scaled = sem("froot_done"), sem("frstd_done"), sem("f_scaled")
        ev = sem("ev")
        glu_sig, c_done, gate_done = sem("glu_sig"), sem("c_done"), sem("gate_done")
        pad_zero = sem("pad_zero")
        tap_done, ptap_mul, ptap_done = sem("tap_done"), sem("ptap_mul"), sem("ptap_done")
        ln_sum, ln_cent, ln_sq, ln_var = sem("ln_sum"), sem("ln_cent"), sem("ln_sq"), sem("ln_var")
        ln_root, ln_rstd, ln_norm = sem("ln_root"), sem("ln_rstd"), sem("ln_norm")
        ln_silu, ln_hi, ln_lo = sem("ln_silu"), sem("ln_hi"), sem("ln_lo")
        yb_done, ya_done, m_done = sem("yb_done"), sem("ya_done"), sem("m_done")
        mh_done, mx_ready = sem("mh_done"), sem("mx_ready")
        v_turned, v_ready = sem("v_turned"), sem("v_ready")
        bias_in, bias_masked = sem("bias_in"), sem("bias_masked")
        qk_done, sb_done, nmax_done = sem("qk_done"), sem("sb_done"), sem("nmax_done")
        exp_done, rinv_done, p_done = sem("exp_done"), sem("rinv_done"), sem("p_done")
        p_turned, pt_ready, pv_done = sem("p_turned"), sem("pt_ready"), sem("pv_done")
        oh_done, ol_done = sem("oh_done"), sem("ol_done")
        mem_in, mem_ss, mem_root = sem("mem_in"), sem("mem_ss"), sem("mem_root")
        mem_rec, mem_norm, mem_turned = sem("mem_rec"), sem("mem_norm"), sem("mem_turned")
        memh_done, meml_done, mem_ev = sem("memh_done"), sem("meml_done"), sem("mem_ev")
        mv_turned, mv_ready = sem("mv_turned"), sem("mv_ready")
        gn_sq, gn_stat, gn_root = sem("gn_sq"), sem("gn_stat"), sem("gn_root")
        gn_rec, gn_spread, gn_out = sem("gn_rec"), sem("gn_spread"), sem("gn_out")
        tab_in = sem("tab_in")
        sg_done, ret_qk, ret_decayed, ret_pv, ret_ev = sem("sg_done"), sem("ret_qk"), sem("ret_decayed"), sem("ret_pv"), sem("ret_ev")
        og_gated = sem("og_gated")
        lam_prod, lam_sum, lam_exp, lam_set = sem("lam_prod"), sem("lam_sum"), sem("lam_exp"), sem("lam_set")
        y_turned, y_ready, y_out = sem("y_turned"), sem("y_ready"), sem("y_out")

        def col(name, i=0, rows=slice(None)):
            at, n = COLS[name]
            return COL[rows, at + i:at + i + 1]

        def view(ap):
            return ap.bitcast(F32)

        SITES = ["f1_pre", "mx_pre", "f2_pre", "attn0", "ffn0", "attn1", "ffn1"]
        b1_steps = [(h, i) for h in range(HEADS) for i in range(TT)]
        mem_steps = [(h, i) for h in range(MEM_H) for i in range(TT)]
        diff_steps = [(h, i) for h in range(DIFF_H) for i in range(TT)]
        atts, s0, g0, m0 = {}, 0, 0, 0
        for name, steps, maps, per in (("b1", b1_steps, 1, 8), ("mem0", mem_steps, 1, 8),
                                       ("diff", diff_steps, 2, 4), ("mem1", mem_steps, 1, 8)):
            A = Attention(name, steps, maps, per, s0, g0)
            A.m0 = m0
            atts[name] = A
            s0, g0, m0 = s0 + len(steps), g0 + len(steps) // per, m0 + maps * len(steps)

        def att_width(A, s):
            h, i = A.steps[s]
            return MEM if A.name.startswith("mem") else P * (i + 1)

        def att_q(A, s, c):
            h, i = A.steps[s]
            tok = slice(P * i, P * i + P)
            if A.name == "b1":
                return U[64 * (h % 2):64 * (h % 2) + 64, 8 + h // 2, tok]
            if A.name == "diff":
                return U[64 * c:64 * c + 64, h, tok]
            return U[64 * (h % 2):64 * (h % 2) + 64, 18 + h // 2, tok]

        def att_k(A, s, c):
            h, i = A.steps[s]
            w = att_width(A, s)
            if A.name == "b1":
                return U[64 * (h % 2):64 * (h % 2) + 64, 12 + h // 2, 0:w]
            if A.name == "diff":
                return U[64 * c:64 * c + 64, 6 + h, 0:w]
            return MKT[64 * (h % 2):64 * (h % 2) + 64, h // 2, 0:w]

        def att_v(A, s, j):
            h, i = A.steps[s]
            if A.name == "b1":
                return V1[:, j, 64 * h:64 * h + 64]
            if A.name == "diff":
                return V2[:, j, P * h:P * h + P]
            return MV[:, j, 64 * h:64 * h + 64]

        def att_sb(A, s, c):
            return (SB1[:, s % 3, :] if A.name == "b1" else SB2[:, (s % 3) * A.maps + c, :])

        def att_pt(A, s):
            return PT1[:, s % 2, :] if A.name == "b1" else PT2[:, s % 2, :]

        def att_group_rows(A, s):
            h, i = A.steps[s]
            return slice(0, P) if A.name == "diff" else slice(64 * (h % 2), 64 * (h % 2) + 64)

        def stat_cols(A, s, c):
            k = (s % 3) * A.maps + c
            return STAT[:, k:k + 1], STAT[:, 8 + k:9 + k], STAT[:, 16 + k:17 + k]

        gns, t0 = {}, 0
        for k, (name, n, size, groups, width) in enumerate((
                ("qc0", 2, 64, 4, S), ("mk0", 2, 64, 4, MEM), ("o0", 6, 128, 6, S),
                ("q1", 6, 64, 12, S), ("k1", 6, 64, 12, S), ("qc1", 2, 64, 4, S),
                ("mk1", 2, 64, 4, MEM), ("o1", 6, 128, 6, S))):
            gns[name] = (n, size, groups, width, t0, k)
            t0 += n

        def gn_tile(name, i):
            return {"qc0": lambda: U[:, 18 + i, :], "qc1": lambda: U[:, 18 + i, :],
                    "mk0": lambda: MKT[:, i, :], "mk1": lambda: MKT[:, i, :],
                    "o0": lambda: O2R[:, i, :], "o1": lambda: O2[:, i, :],
                    "q1": lambda: U[:, i, :], "k1": lambda: U[:, 6 + i, :]}[name]()

        def gn_gain(name, i):
            return {"qc0": lambda: col("mq0"), "qc1": lambda: col("mq1"), "mk0": lambda: col("mk0"),
                    "mk1": lambda: col("mk1"), "o0": lambda: col("ret_gn", i), "o1": lambda: LAM[:, 5:6],
                    "q1": lambda: col("dq"), "k1": lambda: col("dk")}[name]()

        block = ctx.enter_context(nc.Block())

        @block.sync
        def _(sp):
            sp.dma_start(COL[:, :], d["cols"]).then_inc(const_in, 16)
            sp.dma_start(CONST[:, :], d["const"]).then_inc(const_in, 16)
            sp.dma_start(XTOK[:, :, :], d["x"][0].rearrange("(t p) n -> p t n", p=P)).then_inc(x_in, 16)

            def load(u, j, src):
                if not isinstance(u, int) or u >= RING:
                    sp.wait_ge(lo_ready, u - RING + 1)
                slot = RAW[:, j, :]
                if len(src.shape) == 3:
                    slot = slot.rearrange("p (t n) -> p t n", n=src.shape[2])
                sp.dma_start(slot, src).then_inc(raw_in[j], 16)

            def tile_src(w, n):
                return w.rearrange("(t p) n -> p t n", p=P)[:, :, bass.ts(n, P)]

            def tiles(w, n0, count, u0):
                done = 0
                if u0 < RING:
                    for k in range(4):
                        load(u0 + k, (u0 + k) % RING, tile_src(w, n0 + k))
                    done = 4
                if count - done >= 4:
                    with sp.Fori(done // 4, count // 4) as i:
                        for k in range(4):
                            load(u0 + i * 4 + k, (u0 + k) % RING, tile_src(w, n0 + i * 4 + k))
                for k in range(count // 4 * 4, count):
                    load(u0 + k, (u0 + k) % RING, tile_src(w, n0 + k))

            def ffn(wg, wu, up0, wd, u0):
                def body(i, first):
                    for k in range(4):
                        w, off = (wg, 0) if k % 2 == 0 else (wu, up0)
                        load(u0 + i * 4 + k, (u0 + k) % RING, tile_src(w, off + i * 2 + k // 2))
                lo = 0
                if u0 == 0:
                    body(0, True)
                    lo = 1
                with sp.Fori(lo, NF // 2) as i:
                    body(i, False)
                v0 = u0 + GU
                rows = wd.rearrange("(t p) n -> t p n", p=P)
                with sp.Fori(0, NF // 4) as i:
                    for k in range(4):
                        load(v0 + i * 4 + k, (v0 + k) % RING, rows[i * 4 + k])
                for k in range(NF // 4 * 4, NF):
                    load(v0 + k, (v0 + k) % RING, rows[k])

            def half_rows(w, u0):
                for k in range(4):
                    load(u0 + k, (u0 + k) % RING, w.rearrange("(t p) n -> p t n", p=P)[:, :, 256 * k:256 * k + 256])

            ffn(d["ffn1_w_gate"], d["ffn1_w_up"], 0, d["ffn1_w_down"], F1_GU)
            tiles(d["w_in"], 12, 8, MX_IN)
            tiles(d["w_in"], 0, 12, MX_IN + 8)
            tiles(d["w_in"], 20, 16, MX_IN + 20)
            half_rows(d["conv_w_out"], MX_CO)
            sp.wait_ge(tap_done, 3 * TAPS)
            sp.wait_ge(ptap_done, TAPS)
            sp.dma_start(BIAS1[:, :, :], d["rel"]).then_inc(bias_in, 16)
            half_rows(d["w_attn_out"], MX_AO)
            tiles(d["w_out"], 0, ND, MX_OUT)
            ffn(d["ffn2_w_gate"], d["ffn2_w_up"], 0, d["ffn2_w_down"], F2_GU)
            for layer in range(2):
                u0 = LAYER0 + layer * LAYER_UNITS
                tiles(d["w_mem_kv_2"][layer], 0, 4, u0)
                tiles(d["w_in_2"][layer], 0, N_IN2, u0 + 4)
                sp.wait_ge(unit_done, u0 + 4)
                sp.dma_start(TAB[:, :, :], d["decay" if layer == 0 else "alibi"]).then_inc(tab_in, 16)
                sp.dma_start(SP64[0:12, :, :], d["spread64"].rearrange("g (i p) -> g i p", p=P)).then_inc(tab_in, 16)
                sp.dma_start(SP128[0:6, :, :], d["spread128"].rearrange("g (i p) -> g i p", p=P)).then_inc(tab_in, 16)
                tiles(d["w_out_2"][layer], 0, ND, u0 + 4 + N_IN2)
                ffn(d["w_gate_up_2"][layer], d["w_gate_up_2"][layer], NF, d["w_down_2"][layer], u0 + 4 + N_IN2 + ND)
            for n in range(0, ND, 2):
                sp.wait_ge(y_ready, n + 2)
                sp.dma_start(out[0].rearrange("(t p) n -> p t n", p=P)[:, :, n * P:(n + 2) * P],
                             XTOK[:, :, n * P:(n + 2) * P]).then_inc(y_out, 16)
            sp.wait_ge(y_out, 16 * (ND // 2))

        @block.gpsimd
        def _(pool):
            nc.gpsimd.memset(EPSC[:, 0:1], EPS).then_inc(eps_set, 1)
            nc.gpsimd.memset(EPSC[:, 1:2], 4 * EPS).then_inc(eps_set, 1)

            def site_sums(s):
                for n in range(1, ND):
                    pool.wait_ge(sq_ready, ND * s + n + 1)
                    if n >= 2:
                        pool.wait_ge(acc_done, (ND - 1) * s + n - 1)
                    nc.gpsimd.tensor_tensor(ACC[:, :], ACC[:, :], SQ[:, n % 2, :], ALU.add).then_inc(acc_done, 1)

            site_sums(0)
            pool.wait_ge(unit_done, MX_IN)
            nc.gpsimd.memset(C[:, :, 0:PAD], 0.0).then_inc(pad_zero, 1)
            site_sums(1)
            pool.wait_ge(c_done, CH)
            pool.wait_ge(pad_zero, 1)
            pool.wait_ge(stat_done, 2)
            t = CH - 1
            for tap in range(TAPS):
                w = col("dw_w", t * TAPS + tap)
                if tap == 0:
                    nc.gpsimd.tensor_scalar(CO[:, t, :], C[:, t, 0:S], w, col("dw_b", t), ALU.mult, ALU.add).then_inc(ptap_done, 1)
                    continue
                if tap >= 3:
                    pool.wait_ge(ptap_done, tap - 1)
                nc.gpsimd.tensor_scalar(SQ[:, tap % 2, :], C[:, t, tap:tap + S], w, 0.0, ALU.mult, ALU.add).then_inc(ptap_mul, 1)
                pool.wait_ge(ptap_mul, tap)
                pool.wait_ge(ptap_done, tap)
                nc.gpsimd.tensor_tensor(CO[:, t, :], CO[:, t, :], SQ[:, tap % 2, :], ALU.add).then_inc(ptap_done, 1)
            for s in range(2, 7):
                site_sums(s)

        @block.scalar
        def _(act):
            def hi(u, j=None):
                if isinstance(u, int):
                    if u >= UNITS:
                        return
                    j = u % RING
                    act.wait_ge(raw_in[j], 16 * (u // RING + 1))
                    if u >= RING:
                        act.wait_ge(unit_done, u - RING + 1)
                nc.scalar.activation(WHI[:, j, :], RAW[:, j, :], ACT.Copy).then_inc(hi_ready, 1)

            def hi_loop(u0, i, k):
                j = (u0 + k) % RING
                act.wait_ge(raw_in[j], (i * 16) + 16 * ((u0 + k) // RING + 1))
                act.wait_ge(unit_done, i * 4 + (u0 + k - RING + 1))
                hi(None, j)

            def hi_any(u0, i, k):
                if isinstance(i, int):
                    hi(u0 + 4 * i + k)
                else:
                    hi_loop(u0, i, k)

            def site_act(s, n):
                act.wait_ge(h_new, ND * s + n + 1)
                nc.scalar.mul(XH[:, n, :], H[:, n, :], col(SITES[s], n)).then_inc(xh_ready, 1)
                if n >= 3:
                    act.wait_ge(acc_done, (ND - 1) * s + n - 2)
                nc.scalar.activation(ACC[:, :] if n == 0 else SQ[:, n % 2, :], H[:, n, :], ACT.Square).then_inc(sq_ready, 1)

            def site_root(s):
                act.wait_ge(stat_done, s + 1)
                nc.scalar.activation(R[:, :], bank[7][:, :], ACT.Sqrt, scale=1.0 / D, bias=EPSC[:, 0:1]).then_inc(root_done, 1)

            def ffn_act(f, s, u0, after_gu=None, in_down=None):
                T0 = NF * f

                def body(i):
                    for t in range(2):
                        hi_any(u0 + AHEAD, i, 2 * t)
                        if t == 0 and isinstance(i, int) and i == 0:
                            site_root(s)
                        act.wait_ge(g_scaled, i * 2 + (T0 + t + 1))
                        nc.scalar.activation(TMP[:, t, :], TMP[:, t, :], ACT.Silu).then_inc(silu_done, 1)
                        hi_any(u0 + AHEAD, i, 2 * t + 1)
                        act.wait_ge(a_done, i * 2 + (T0 + t + 1))
                        nc.scalar.activation(AH[:, i * 2 + t, :], TMP[:, 2 + t, :], ACT.Copy).then_inc(ah_ready, 1)
                body(0)
                with act.Fori(1, NF // 2) as i:
                    body(i)
                if after_gu:
                    after_gu()
                v0 = u0 + GU
                with act.Fori(0, 4) as i:
                    for k in range(4):
                        hi_loop(v0 + AHEAD, i, k)
                if in_down:
                    in_down()
                for k in range(16, NF):
                    hi(v0 + k + AHEAD)

            def post_square(p, n, wait):
                wait(act, n)
                if n >= 2:
                    act.wait_ge(fstat_done, ND * p + n - 1)
                nc.scalar.activation(SQ[:, n % 2, :], bank[n if p != 1 else n % 4][:, :], ACT.Square).then_inc(fsq_done, 1)

            def post_root(p):
                four = 1 if p == 1 else 4
                act.wait_ge(fstat_done, ND * (p + 1))
                nc.scalar.activation(R[:, :], bank[7 if p == 1 else 0][:, :], ACT.Sqrt, scale=four / D,
                                     bias=EPSC[:, four // 4:four // 4 + 1]).then_inc(froot_done, 1)

            def down_wait(e, t8):
                def wait(eng, n):
                    if n < ND - 1:
                        eng.wait_ge(tile_ready, (ND - 1) * t8 + n + 1)
                    else:
                        eng.wait_ge(unit_done, e)
                return wait

            def attention_act(A):
                n = len(A.steps)
                for it in range(n + 3):
                    if it < n:
                        w = att_width(A, it)
                        for c in range(A.maps):
                            nmax, total, _ = stat_cols(A, it, c)
                            act.wait_ge(nmax_done, A.m0 + it * A.maps + c + 1)
                            src = att_sb(A, it, c)[:, 0:w]
                            if A.name.startswith("mem"):
                                if it >= 3:
                                    act.wait_ge(p_turned, A.s0 + it - 2)
                                nc.scalar.activation(src, bank[it % 2][:, 0:w], ACT.Exp, scale=0.125, bias=nmax,
                                                     accum_out=total).then_inc(exp_done, 1)
                            else:
                                nc.scalar.activation(src, src, ACT.Exp, bias=nmax, accum_out=total).then_inc(exp_done, 1)
                    s = it - 2
                    if 0 <= s < n:
                        w = att_width(A, s)
                        act.wait_ge(p_turned, A.s0 + s + 1)
                        if s >= 2:
                            act.wait_ge(pv_done, A.s0 + s - 1)
                        nc.scalar.activation(att_pt(A, s)[:, 0:w], bank[2 + s % 2][:, 0:w], ACT.Copy).then_inc(pt_ready, 1)
                    s = it - 3
                    if s >= 0 and s % A.per_group == A.per_group - 1:
                        g = s // A.per_group
                        act.wait_ge(pv_done, A.s0 + s + 1)
                        src = bank[4 + g % 2][:, :]
                        if A.name == "diff":
                            nc.scalar.activation(O2[:, g, :], src, ACT.Copy).then_inc(oh_done, 1)
                        else:
                            dst = XH[:, 4 + g, :] if A.name == "b1" else YH[:, 6 + g, :]
                            nc.scalar.activation(dst, src, ACT.Copy).then_inc(oh_done, 1)

            def gn_act(name):
                n, size, groups, width, t0, k = gns[name]
                for i in range(n):
                    if i >= 2:
                        act.wait_ge(gn_stat, t0 + i - 1)
                    nc.scalar.activation(SQ[:, i % 2, 0:width], gn_tile(name, i), ACT.Square).then_inc(gn_sq, 1)
                act.wait_ge(gn_stat, t0 + n)
                if k:
                    act.wait_ge(gn_spread, t0)
                nc.scalar.activation(ACC[0:groups, 0:width], bank[7][0:groups, 0:width], ACT.Sqrt, scale=1.0 / size,
                                     bias=EPSC[0:groups, 0:1]).then_inc(gn_root, 1)

            for u in range(AHEAD):
                hi(u)
            act.wait_ge(const_in, 32)
            act.wait_ge(eps_set, 2)
            for n in range(ND):
                site_act(0, n)
            ffn_act(0, 0, F1_GU)
            wait = down_wait(MX_IN, 0)
            for n in range(ND):
                post_square(0, n, wait)
            post_root(0)
            for n in range(ND):
                site_act(1, n)

            def mx_body(i, gates):
                for k in range(4):
                    hi_any(MX_IN + AHEAD, i, k)
                    if isinstance(i, int) and i == 0 and k == 0:
                        site_root(1)
                    if gates:
                        act.wait_ge(ev, i * 4 + (k + 1))
                        nc.scalar.activation(U[:, i * 4 + k, :], U[:, i * 4 + k, :], ACT.Sigmoid,
                                             bias=COL[:, bass.ds(i * 4 + (k - 20 + COLS["gate_bias"][0]), 1)]).then_inc(gate_done, 1)
            mx_body(0, False)
            mx_body(1, False)
            for a in range(CH):
                act.wait_ge(ev, 5 + a)
                nc.scalar.activation(U[:, 4 + a, :], U[:, 4 + a, :], ACT.Sigmoid, bias=col("glu_bias", CH + a)).then_inc(glu_sig, 1)
            with act.Fori(2, 5) as i:
                mx_body(i, False)
            act.wait_ge(c_done, CH)
            for a in range(4):
                act.wait_ge(v_turned, a + 1)
                nc.scalar.activation(V1[:, :, P * a:P * a + P], bank[4 + a % 2][:, :].rearrange("p (t f) -> p t f", f=P),
                                     ACT.Copy).then_inc(v_ready, 1)
            with act.Fori(5, 9) as i:
                mx_body(i, True)

            for t in range(CH):
                act.wait_ge(ln_cent, t + 1)
                if t >= 2:
                    act.wait_ge(ln_var, t - 1)
                nc.scalar.activation(SQ[:, t % 2, :], CO[:, t, :], ACT.Square).then_inc(ln_sq, 1)
            act.wait_ge(ln_var, CH)
            nc.scalar.activation(ACC[:, :], bank[6][:, :], ACT.Sqrt, scale=1.0 / 512, bias=EPSC[:, 0:1]).then_inc(ln_root, 1)
            act.wait_ge(unit_done, MX_CO)
            for t in range(CH):
                act.wait_ge(ln_norm, t + 1)
                nc.scalar.activation(CO[:, t, :], CO[:, t, :], ACT.Silu, scale=col("ln_g", t), bias=col("ln_b", t)).then_inc(ln_silu, 1)
                act.wait_ge(ln_silu, t + 1)
                nc.scalar.activation(XH[:, t, :], CO[:, t, :], ACT.Copy).then_inc(ln_hi, 1)
            for j in range(4):
                hi(MX_CO + j + AHEAD)
            attention_act(atts["b1"])
            for j in range(4):
                hi(MX_AO + j + AHEAD)
                if j < 2:
                    for n in (2 * j, 2 * j + 1):
                        act.wait_ge(m_done, n + 1)
                        nc.scalar.activation(XH[:, n, :], U[:, 20 + n, :], ACT.Copy).then_inc(mh_done, 1)
            act.wait_ge(unit_done, MX_OUT)
            for n in range(4, ND):
                act.wait_ge(m_done, n + 1)
                nc.scalar.activation(XH[:, n, :], U[:, 20 + n, :], ACT.Copy).then_inc(mh_done, 1)
            for n in range(ND):
                hi(MX_OUT + n + AHEAD)
                post_square(1, n, lambda eng, n: eng.wait_ge(unit_done, MX_OUT + n + 1))
            post_root(1)
            for n in range(ND):
                site_act(2, n)

            def mem_load(layer):
                act.wait_ge(al_ready, NF * (2 + layer))
                act.dma_start(MTOK[:, :, :], d["mem_2"][0].rearrange("(t p) n -> p t n", p=P)).then_inc(mem_in, 16)

            def mem_sums(layer):
                act.wait_ge(mem_in, 16 * (layer + 1))
                for t in range(NMT):
                    if t:
                        act.wait_ge(mem_ss, NMT * layer + t)
                    nc.scalar.activation(SQ[:, :, :].rearrange("p a n -> p (a n)"), MTOK[:, t, :], ACT.Square,
                                         accum_out=LAM[:, 6 + t:7 + t]).then_inc(mem_ss, 1)
                act.wait_ge(mem_ss, NMT * (layer + 1))
                nc.scalar.activation(LAM[:, 6:8], LAM[:, 6:8], ACT.Sqrt, scale=1.0 / D, bias=EPSC[:, 0:1]).then_inc(mem_root, 1)

            ffn_act(1, 2, F2_GU, lambda: mem_load(0), lambda: mem_sums(0))

            for layer in range(2):
                u0 = LAYER0 + layer * LAYER_UNITS
                if layer == 0:
                    wait = down_wait(LAYER0, 1)
                    for n in range(ND):
                        post_square(2, n, wait)
                for k in range(ND):
                    act.wait_ge(mem_turned, ND * layer + k + 1)
                    nc.scalar.mul(MH[:, k, :], bank[4 + k % 2][:, 0:MEM], col("mem", k)).then_inc(memh_done, 1)
                if layer == 0:
                    post_root(2)
                s = 3 + 2 * layer
                for n in range(ND):
                    site_act(s, n)
                for m in range(4):
                    hi(u0 + m + AHEAD)
                for b in range(NMT):
                    act.wait_ge(mv_turned, NMT * layer + b + 1)
                    nc.scalar.activation(MV[:, :, P * b:P * b + P], bank[4 + b][:, 0:MEM].rearrange("p (t f) -> p t f", f=P),
                                         ACT.Copy).then_inc(mv_ready, 1)

                def in_body(i):
                    for k in range(4):
                        hi_any(u0 + 4 + AHEAD, i, k)
                        if isinstance(i, int) and i == 0 and k == 0:
                            site_root(s)
                in_body(0)
                with act.Fori(1, N_IN2 // 4) as i:
                    in_body(i)
                for a in range(6):
                    act.wait_ge(v_turned, 4 + 6 * layer + a + 1)
                    nc.scalar.activation(V2[:, :, P * a:P * a + P], bank[4 + a % 2][:, :].rearrange("p (t f) -> p t f", f=P),
                                         ACT.Copy).then_inc(v_ready, 1)
                if layer == 0:
                    for n in range(6):
                        nc.scalar.activation(U[:, 12 + n, :], U[:, 12 + n, :], ACT.Silu).then_inc(sg_done, 1)
                    gn_act("qc0")
                    gn_act("mk0")
                    for h in range(RET_H):
                        act.wait_ge(ret_pv, TT * (h + 1))
                        nc.scalar.activation(O2R[:, h, :], bank[4 + h % 2][:, :], ACT.Copy).then_inc(ret_ev, 1)
                    act.wait_ge(unit_done, u0 + 4 + N_IN2)
                    act.wait_ge(ret_ev, RET_H)
                    gn_act("o0")
                    for h in range(RET_H):
                        act.wait_ge(og_gated, h + 1)
                        nc.scalar.activation(YH[:, h, :], O2R[:, h, :], ACT.Copy).then_inc(mh_done, 1)
                    attention_act(atts["mem0"])
                else:
                    act.wait_ge(lam_sum, 1)
                    nc.scalar.activation(LAM[:, 2:4], bank[6][:, 0:2], ACT.Exp).then_inc(lam_exp, 1)
                    gn_act("q1")
                    gn_act("k1")
                    gn_act("qc1")
                    gn_act("mk1")
                    attention_act(atts["diff"])
                    act.wait_ge(oh_done, atts["diff"].g0 + DIFF_H)
                    gn_act("o1")
                    for h in range(DIFF_H):
                        act.wait_ge(gn_out, gns["o1"][4] + h + 1)
                        nc.scalar.activation(YH[:, h, :], O2[:, h, :], ACT.Copy).then_inc(mh_done, 1)
                    attention_act(atts["mem1"])
                for n in range(ND):
                    hi(u0 + 4 + N_IN2 + n + AHEAD)
                    site_act(s + 1, n)
                if layer == 0:
                    ffn_act(2, s + 1, u0 + 4 + N_IN2 + ND, lambda: mem_load(1), lambda: mem_sums(1))
                else:
                    ffn_act(3, s + 1, u0 + 4 + N_IN2 + ND)
            for n in range(ND):
                act.wait_ge(y_turned, n + 1)
                nc.scalar.activation(XTOK[:, :, P * n:P * n + P], bank[n][:, :].rearrange("p (t f) -> p t f", f=P),
                                     ACT.Copy).then_inc(y_ready, 1)

        @block.vector
        def _(dve):
            def lo(u, j=None):
                if isinstance(u, int):
                    if u >= UNITS:
                        return
                    j = u % RING
                    dve.wait_ge(hi_ready, u + 1)
                nc.vector.tensor_tensor(WLO[:, j, :], RAW[:, j, :], view(WHI[:, j, :]), ALU.subtract).then_inc(lo_ready, 1)

            def lo_any(u0, i, k):
                if isinstance(i, int):
                    lo(u0 + 4 * i + k)
                else:
                    dve.wait_ge(hi_ready, i * 4 + (u0 + k + 1))
                    lo(None, (u0 + k) % RING)

            def site_dve(s, n):
                dve.wait_ge(xh_ready, ND * s + n + 1)
                nc.vector.scalar_tensor_tensor(out=XL[:, n, :], in0=H[:, n, :], scalar=col(SITES[s], n), in1=view(XH[:, n, :]),
                                               op0=ALU.mult, op1=ALU.subtract).then_inc(x_ready, 1)

            def site_rstd(s):
                dve.wait_ge(root_done, s + 1)
                nc.vector.reciprocal(R[:, :], R[:, :]).then_inc(rstd_done, 1)
                dve.wait_ge(rstd_done, s + 1)

            def ffn_dve(f, s, u0, in_down=None):
                T0 = NF * f

                def al(T, t):
                    dve.wait_ge(ah_ready, T + (T0 + 1))
                    nc.vector.tensor_tensor(AL[:, T, :], TMP[:, 2 + t, :], view(AH[:, T, :]), ALU.subtract).then_inc(al_ready, 1)

                def body(i):
                    first = isinstance(i, int)
                    for t in range(2):
                        lo_any(u0 + AHEAD, i, 2 * t)
                        dve.wait_ge(unit_done, i * 4 + (u0 + 2 * t + 1))
                        if first and t == 0:
                            site_rstd(s)
                        if not first:
                            dve.wait_ge(a_done, i * 2 + (T0 + t - 1))
                        nc.vector.tensor_tensor(TMP[:, t, :], bank[2 * t][:, :], R[:, :], ALU.mult).then_inc(g_scaled, 1)
                        if not first or t:
                            al(i * 2 + t - 1, 1 - t)
                        lo_any(u0 + AHEAD, i, 2 * t + 1)
                        dve.wait_ge(unit_done, i * 4 + (u0 + 2 * t + 2))
                        if not first:
                            dve.wait_ge(al_ready, i * 2 + (T0 + t - 1))
                        nc.vector.tensor_tensor(TMP[:, 2 + t, :], bank[2 * t + 1][:, :], R[:, :], ALU.mult).then_inc(u_scaled, 1)
                        dve.wait_ge(u_scaled, i * 2 + (T0 + t + 1))
                        dve.wait_ge(silu_done, i * 2 + (T0 + t + 1))
                        nc.vector.tensor_tensor(TMP[:, 2 + t, :], TMP[:, 2 + t, :], TMP[:, t, :], ALU.mult).then_inc(a_done, 1)
                body(0)
                with dve.Fori(1, NF // 2) as i:
                    body(i)
                al(NF - 1, 1)
                v0 = u0 + GU
                with dve.Fori(0, 4) as i:
                    for k in range(4):
                        lo_any(v0 + AHEAD, i, k)
                if in_down:
                    in_down()
                for k in range(16, NF):
                    lo(v0 + k + AHEAD)

            def post_gain(p, n, name):
                dve.wait_ge(fsq_done, ND * p + n + 1)
                nc.vector.tensor_scalar(FG[:, n, :], bank[n if p != 1 else n % 4][:, :], col(name, n), None, ALU.mult).then_inc(fg_done, 1)

            def post_update(p, s):
                dve.wait_ge(froot_done, p + 1)
                nc.vector.reciprocal(R[:, :], R[:, :]).then_inc(frstd_done, 1)
                dve.wait_ge(frstd_done, p + 1)
                dve.wait_ge(fg_done, ND * (p + 1))
                for n in range(ND):
                    nc.vector.tensor_tensor(FG[:, n, :], FG[:, n, :], R[:, :], ALU.mult).then_inc(f_scaled, 1)
                    dve.wait_ge(f_scaled, ND * p + n + 1)
                    nc.vector.tensor_tensor(H[:, n, :], H[:, n, :], FG[:, n, :], ALU.add).then_inc(h_new, 1)
                    if n:
                        site_dve(s, n - 1)
                site_dve(s, ND - 1)

            def down_ready(e, t8):
                def ready(n):
                    if n < ND - 1:
                        dve.wait_ge(tile_ready, (ND - 1) * t8 + n + 1)
                    else:
                        dve.wait_ge(unit_done, e)
                return ready

            def attention_dve(A):
                n = len(A.steps)
                is_mem = A.name.startswith("mem")
                for it in range(n + 3):
                    if it < n:
                        h, i = A.steps[it]
                        w = att_width(A, it)
                        for c in range(A.maps):
                            m = A.m0 + it * A.maps + c
                            nmax, total, rinv = stat_cols(A, it, c)
                            src = bank[(it * A.maps + c) % 2][:, 0:w]
                            dve.wait_ge(qk_done, m + 1)
                            if is_mem:
                                if it >= 3:
                                    dve.wait_ge(exp_done, m - 2)
                                nc.vector.tensor_reduce(nmax, src, AX_X, ALU.max, negate=True).then_inc(sb_done, 1)
                                dve.wait_ge(sb_done, m + 1)
                                nc.vector.tensor_scalar(nmax, nmax, 0.125, None, ALU.mult).then_inc(nmax_done, 1)
                                continue
                            sb = att_sb(A, it, c)
                            if it >= 3:
                                dve.wait_ge(p_turned, A.s0 + it - 2)
                            if A.name == "b1":
                                near = min(w, 256)
                                if w > near:
                                    nc.vector.tensor_scalar(sb[:, 0:w - near], src[:, 0:w - near], 0.125, BIAS1[:, h, 0:1],
                                                            ALU.mult, ALU.add)
                                nc.vector.scalar_tensor_tensor(out=sb[:, w - near:w], in0=src[:, w - near:w], scalar=0.125,
                                                               in1=BIAS1[:, h, 256 - near:256], op0=ALU.mult, op1=ALU.add).then_inc(sb_done, 1)
                            else:
                                nc.vector.scalar_tensor_tensor(out=sb[:, 0:w], in0=src, scalar=0.125, in1=TAB[:, h, S - w:S],
                                                               op0=ALU.mult, op1=ALU.add).then_inc(sb_done, 1)
                            dve.wait_ge(sb_done, m + 1)
                            nc.vector.tensor_reduce(nmax, sb[:, 0:w], AX_X, ALU.max, negate=True).then_inc(nmax_done, 1)
                    s = it - 1
                    if 0 <= s < n:
                        w = att_width(A, s)
                        m = A.m0 + s * A.maps
                        for c in range(A.maps):
                            _, total, rinv = stat_cols(A, s, c)
                            dve.wait_ge(exp_done, m + c + 1)
                            nc.vector.reciprocal(rinv, total).then_inc(rinv_done, 1)
                        dve.wait_ge(rinv_done, m + A.maps)
                        p0 = att_sb(A, s, 0)[:, 0:w]
                        _, _, r0 = stat_cols(A, s, 0)
                        if A.maps == 1:
                            nc.vector.tensor_scalar(p0, p0, r0, None, ALU.mult).then_inc(p_done, 1)
                        else:
                            _, _, r1 = stat_cols(A, s, 1)
                            nc.vector.tensor_scalar(r1, r1, LAM[:, 4:5], None, ALU.mult).then_inc(lam_prod, 1)
                            nc.vector.tensor_scalar(p0, p0, r0, None, ALU.mult).then_inc(lam_prod, 1)
                            dve.wait_ge(lam_prod, 2 + 2 * (s + 1))
                            nc.vector.scalar_tensor_tensor(out=p0, in0=att_sb(A, s, 1)[:, 0:w], scalar=r1, in1=p0,
                                                           op0=ALU.mult, op1=ALU.add).then_inc(p_done, 1)
                    s = it - 3
                    if s >= 0 and s % A.per_group == A.per_group - 1 and A.name != "diff":
                        g = s // A.per_group
                        high, low = (XH[:, 4 + g, :], XL[:, 4 + g, :]) if A.name == "b1" else (YH[:, 6 + g, :], YL[:, 6 + g, :])
                        dve.wait_ge(oh_done, A.g0 + g + 1)
                        nc.vector.tensor_tensor(low, bank[4 + g % 2][:, :], view(high), ALU.subtract).then_inc(ol_done, 1)

            def gn_rstd(name):
                n, size, groups, width, t0, k = gns[name]
                dve.wait_ge(gn_root, k + 1)
                nc.vector.reciprocal(ACC[0:groups, 0:width], ACC[0:groups, 0:width]).then_inc(gn_rec, 1)

            def gn_dve(name):
                n, size, groups, width, t0, k = gns[name]
                gn_rstd(name)
                for i in range(n):
                    dve.wait_ge(gn_spread, t0 + i + 1)
                    tile = gn_tile(name, i)
                    nc.vector.scalar_tensor_tensor(out=tile, in0=tile, scalar=gn_gain(name, i), in1=bank[5 + i % 2][:, 0:width],
                                                   op0=ALU.mult, op1=ALU.mult).then_inc(gn_out, 1)

            for u in range(AHEAD):
                lo(u)
            dve.wait_ge(const_in, 32)
            for n in range(ND):
                dve.wait_ge(xT_done, n + 1)
                nc.vector.tensor_copy(H[:, n, :], bank[n][:, :]).then_inc(h_new, 1)
                if n:
                    site_dve(0, n - 1)
            site_dve(0, ND - 1)
            ffn_dve(0, 0, F1_GU)
            for n in range(ND):
                post_gain(0, n, "f1_post")
            post_update(0, 1)

            def mx_body(i, taps=None):
                for k in range(4):
                    lo_any(MX_IN + AHEAD, i, k)
                    dve.wait_ge(unit_done, i * 4 + (MX_IN + k + 1))
                    if isinstance(i, int) and i == 0 and k == 0:
                        site_rstd(1)
                    nc.vector.tensor_tensor(U[:, i * 4 + k, :], bank[k][:, :], R[:, :], ALU.mult).then_inc(ev, 1)
                    if taps is not None:
                        for t in range(3):
                            tap = i * 4 + (k - 8 + 1)
                            dve.wait_ge(tap_done, i * 12 + (3 * (k - 8) + t + 1))
                            nc.vector.scalar_tensor_tensor(
                                out=CO[:, t, :], in0=C[:, t, bass.ds(tap, S)],
                                scalar=COL[:, bass.ds(tap + (COLS["dw_w"][0] + t * TAPS), 1)],
                                in1=CO[:, t, :], op0=ALU.mult, op1=ALU.add).then_inc(tap_done, 1)
            mx_body(0)
            mx_body(1)
            for a in range(CH):
                dve.wait_ge(glu_sig, a + 1)
                nc.vector.scalar_tensor_tensor(out=C[:, a, PAD:PAD + S], in0=U[:, a, :], scalar=col("glu_bias", a), in1=U[:, 4 + a, :],
                                               op0=ALU.add, op1=ALU.mult).then_inc(c_done, 1)
            dve.wait_ge(pad_zero, 1)
            dve.wait_ge(c_done, CH)
            for t in range(3):
                nc.vector.tensor_scalar(CO[:, t, :], C[:, t, 0:S], col("dw_w", t * TAPS), col("dw_b", t), ALU.mult, ALU.add).then_inc(tap_done, 1)
            with dve.Fori(2, 9) as i:
                mx_body(i, True)
            for tap in range(29, TAPS):
                for t in range(3):
                    dve.wait_ge(tap_done, 3 * (tap - 1) + t + 1)
                    nc.vector.scalar_tensor_tensor(out=CO[:, t, :], in0=C[:, t, tap:tap + S], scalar=col("dw_w", t * TAPS + tap),
                                                   in1=CO[:, t, :], op0=ALU.mult, op1=ALU.add).then_inc(tap_done, 1)
            dve.wait_ge(ln_sum, 1)
            for t in range(CH):
                nc.vector.scalar_tensor_tensor(out=CO[:, t, :], in0=bank[7][:, :], scalar=-1.0 / 512, in1=CO[:, t, :],
                                               op0=ALU.mult, op1=ALU.add).then_inc(ln_cent, 1)
            dve.wait_ge(ln_root, 1)
            nc.vector.reciprocal(ACC[:, :], ACC[:, :]).then_inc(ln_rstd, 1)
            dve.wait_ge(ln_rstd, 1)
            for t in range(CH):
                nc.vector.tensor_tensor(CO[:, t, :], CO[:, t, :], ACC[:, :], ALU.mult).then_inc(ln_norm, 1)
            for t in range(CH):
                dve.wait_ge(ln_hi, t + 1)
                nc.vector.tensor_tensor(XL[:, t, :], CO[:, t, :], view(XH[:, t, :]), ALU.subtract).then_inc(ln_lo, 1)
            dve.wait_ge(bias_in, 16)
            nc.vector.memset(BIAS1[0:64, :, 192:256], NEG).then_inc(bias_masked, 1)
            for j in range(4):
                lo(MX_CO + j + AHEAD)
                dve.wait_ge(unit_done, MX_CO + j + 1)
                dve.wait_ge(gate_done, 16)
                for n in (2 * j, 2 * j + 1):
                    nc.vector.tensor_tensor(U[:, 28 + n, :], bank[n % 4][:, :], U[:, 28 + n, :], ALU.mult).then_inc(yb_done, 1)
            dve.wait_ge(bias_masked, 1)
            attention_dve(atts["b1"])

            def m_lo(n):
                dve.wait_ge(mh_done, n + 1)
                nc.vector.tensor_tensor(XL[:, n, :], U[:, 20 + n, :], view(XH[:, n, :]), ALU.subtract).then_inc(mx_ready, 1)

            for j in range(4):
                lo(MX_AO + j + AHEAD)
                dve.wait_ge(unit_done, MX_AO + j + 1)
                for n in (2 * j, 2 * j + 1):
                    nc.vector.tensor_tensor(U[:, 20 + n, :], bank[n % 4][:, :], U[:, 20 + n, :], ALU.mult).then_inc(ya_done, 1)
                    dve.wait_ge(ya_done, n + 1)
                    dve.wait_ge(yb_done, n + 1)
                    nc.vector.tensor_tensor(U[:, 20 + n, :], U[:, 20 + n, :], U[:, 28 + n, :], ALU.add).then_inc(m_done, 1)
                if j < 2:
                    for n in (2 * j, 2 * j + 1):
                        m_lo(n)
            for n in range(4, ND):
                m_lo(n)
            for n in range(ND):
                lo(MX_OUT + n + AHEAD)
                post_gain(1, n, "mx_post")
            post_update(1, 2)

            def mem_scale(layer):
                dve.wait_ge(mem_root, layer + 1)
                nc.vector.reciprocal(LAM[:, 6:8], LAM[:, 6:8]).then_inc(mem_rec, 1)
                dve.wait_ge(mem_rec, layer + 1)
                for t in range(NMT):
                    nc.vector.tensor_scalar(MTOK[:, t, :], MTOK[:, t, :], LAM[:, 6 + t:7 + t], None, ALU.mult).then_inc(mem_norm, 1)

            ffn_dve(1, 2, F2_GU, lambda: mem_scale(0))

            for layer in range(2):
                u0 = LAYER0 + layer * LAYER_UNITS
                s = 3 + 2 * layer
                if layer == 0:
                    for n in range(ND):
                        post_gain(2, n, "f2_post")
                else:
                    ready = down_ready(u0, 2)
                    for n in range(ND):
                        ready(n)
                        nc.vector.tensor_tensor(H[:, n, :], H[:, n, :], bank[n][:, :], ALU.add).then_inc(h_new, 1)
                for k in range(ND):
                    dve.wait_ge(memh_done, ND * layer + k + 1)
                    nc.vector.scalar_tensor_tensor(out=ML[:, k, :], in0=bank[4 + k % 2][:, 0:MEM], scalar=col("mem", k), in1=view(MH[:, k, :]),
                                                   op0=ALU.mult, op1=ALU.subtract).then_inc(meml_done, 1)
                if layer == 0:
                    post_update(2, 3)
                else:
                    for n in range(ND):
                        site_dve(s, n)
                for m in range(4):
                    lo(u0 + m + AHEAD)
                    dve.wait_ge(unit_done, u0 + m + 1)
                    dst = MKT[:, m, :] if m < NMT else MVT[:, m - NMT, :]
                    nc.vector.tensor_copy(dst, bank[(1, 2, 3, 6)[m]][:, 0:MEM]).then_inc(mem_ev, 1)

                def in_body(i):
                    for k in range(4):
                        lo_any(u0 + 4 + AHEAD, i, k)
                        dve.wait_ge(unit_done, i * 4 + (u0 + 4 + k + 1))
                        if isinstance(i, int) and i == 0 and k == 0:
                            site_rstd(s)
                        nc.vector.tensor_tensor(U[:, i * 4 + k, :], bank[k][:, :], R[:, :], ALU.mult).then_inc(ev, 1)
                in_body(0)
                with dve.Fori(1, N_IN2 // 4) as i:
                    in_body(i)
                dve.wait_ge(tab_in, 48 * (layer + 1))
                if layer == 0:
                    gn_dve("qc0")
                    gn_dve("mk0")
                    k = 0
                    for h in range(RET_H):
                        for j in range(TT):
                            w = S - P * j
                            dve.wait_ge(ret_qk, k + 1)
                            if k >= 3:
                                dve.wait_ge(ret_pv, k - 2)
                            nc.vector.tensor_tensor(SB2[:, k % 3, 0:w], bank[k % 2][:, 0:w], TAB[:, h, 0:w], ALU.mult).then_inc(ret_decayed, 1)
                            k += 1
                    gn_rstd("o0")
                    for h in range(RET_H):
                        t0 = gns["o0"][4]
                        dve.wait_ge(gn_spread, t0 + h + 1)
                        nc.vector.scalar_tensor_tensor(out=O2R[:, h, :], in0=O2R[:, h, :], scalar=gn_gain("o0", h), in1=bank[5 + h % 2][:, :],
                                                       op0=ALU.mult, op1=ALU.mult).then_inc(gn_out, 1)
                        dve.wait_ge(gn_out, t0 + h + 1)
                        dve.wait_ge(sg_done, h + 1)
                        nc.vector.tensor_tensor(O2R[:, h, :], O2R[:, h, :], U[:, 12 + h, :], ALU.mult).then_inc(og_gated, 1)
                    for h in range(RET_H):
                        dve.wait_ge(mh_done, ND + h + 1)
                        nc.vector.tensor_tensor(YL[:, h, :], O2R[:, h, :], view(YH[:, h, :]), ALU.subtract).then_inc(mx_ready, 1)
                    attention_dve(atts["mem0"])
                else:
                    nc.vector.tensor_tensor(LAM[0:64, 0:1], col("lq1", 0, slice(0, 64)), col("lk1", 0, slice(0, 64)), ALU.mult).then_inc(lam_prod, 1)
                    nc.vector.tensor_tensor(LAM[0:64, 1:2], col("lq2", 0, slice(0, 64)), col("lk2", 0, slice(0, 64)), ALU.mult).then_inc(lam_prod, 1)
                    dve.wait_ge(lam_exp, 1)
                    nc.vector.tensor_tensor(LAM[:, 4:5], LAM[:, 3:4], LAM[:, 2:3], ALU.subtract).then_inc(lam_set, 1)
                    dve.wait_ge(lam_set, 1)
                    nc.vector.tensor_scalar(LAM[:, 4:5], LAM[:, 4:5], -LAMBDA_INIT, None, ALU.add).then_inc(lam_set, 1)
                    nc.vector.tensor_scalar(LAM[:, 5:6], col("subln"), 1.0 - LAMBDA_INIT, None, ALU.mult).then_inc(lam_set, 1)
                    dve.wait_ge(lam_set, 3)
                    gn_dve("q1")
                    gn_dve("k1")
                    gn_dve("qc1")
                    gn_dve("mk1")
                    attention_dve(atts["diff"])
                    gn_dve("o1")
                    for h in range(DIFF_H):
                        dve.wait_ge(mh_done, ND + RET_H + h + 1)
                        nc.vector.tensor_tensor(YL[:, h, :], O2[:, h, :], view(YH[:, h, :]), ALU.subtract).then_inc(mx_ready, 1)
                    attention_dve(atts["mem1"])
                w0 = u0 + 4 + N_IN2
                for n in range(ND):
                    lo(w0 + n + AHEAD)
                    dve.wait_ge(unit_done, w0 + n + 1)
                    nc.vector.tensor_tensor(H[:, n, :], H[:, n, :], bank[n][:, :], ALU.add).then_inc(h_new, 1)
                    if n:
                        site_dve(s + 1, n - 1)
                site_dve(s + 1, ND - 1)
                ffn_dve(2 + layer, s + 1, w0 + ND, (lambda: mem_scale(1)) if layer == 0 else None)
            ready = down_ready(UNITS, 3)
            for n in range(ND):
                ready(n)
                nc.vector.tensor_tensor(H[:, n, :], H[:, n, :], bank[n][:, :], ALU.add).then_inc(h_new, 1)

        @block.tensor
        def _(pe):
            def split_product(j, at, rhs_hi, rhs_lo, dst, start, stop):
                w = slice(at, at + P)
                nc.tensor.matmul(dst, WHI[:, j, w], rhs_hi, start=start, stop=False)
                nc.tensor.matmul(dst, WHI[:, j, w], rhs_lo, start=False, stop=False)
                return nc.tensor.matmul(dst, WLO[:, j, w], rhs_hi, start=False, stop=stop)

            def tile_unit(u, j, dst, xh, xl, before=None):
                pe.wait_ge(lo_ready, u + 1)
                for k in range(ND):
                    if before:
                        before(k)
                    mm = split_product(j, P * k, xh[:, k, :], xl[:, k, :], dst, k == 0, k == ND - 1)
                mm.then_inc(unit_done, 1)

            def site_stat(s):
                pe.wait_ge(acc_done, (ND - 1) * (s + 1))
                nc.tensor.matmul(bank[7][:, :], ONES, ACC[:, :], start=True, stop=True).then_inc(stat_done, 1)

            def ffn_pe(f, s, u0):
                T0 = NF * f

                def body(i):
                    first = isinstance(i, int)
                    for k in range(4):
                        if not first:
                            pe.wait_ge(g_scaled if k % 2 == 0 else u_scaled, i * 2 + (T0 + k // 2 - 1))
                        tile_unit(i * 4 + (u0 + k), (u0 + k) % RING, bank[k][:, :], XH, XL,
                                  (lambda kk: pe.wait_ge(x_ready, ND * s + kk + 1)) if first and k == 0 else None)
                        if first and k == 0:
                            site_stat(s)
                body(0)
                with pe.Fori(1, NF // 2) as i:
                    body(i)
                v0 = u0 + GU

                def down(k, j, order, start, stop, tiles):
                    pe.wait_ge(lo_ready, v0 + k + 1)
                    for n in order:
                        mm = split_product(j, P * n, AH[:, k, :], AL[:, k, :], bank[n][:, :], start, stop)
                        if tiles and n < ND - 1:
                            mm.then_inc(tile_ready, 1)
                    mm.then_inc(unit_done, 1)

                pe.wait_ge(al_ready, T0 + NF - 2)
                pe.wait_ge(root_done, s + 1)
                pe.wait_ge(lo_ready, v0 + 1)
                for n in (4, 5, 6, 7, 0, 1, 2, 3):
                    if n == 0:
                        pe.wait_ge(g_scaled, T0 + NF)
                        pe.wait_ge(u_scaled, T0 + NF)
                    mm = split_product(v0 % RING, P * n, AH[:, 0, :], AL[:, 0, :], bank[n][:, :], True, False)
                mm.then_inc(unit_done, 1)
                down(1, (v0 + 1) % RING, range(ND), False, False, False)
                with pe.Fori(0, (NF - 6) // 4) as i:
                    for k in range(2, 6):
                        pe.wait_ge(lo_ready, i * 4 + (v0 + k + 1))
                        for n in range(ND):
                            mm = split_product((v0 + k) % RING, P * n, AH[:, i * 4 + k, :], AL[:, i * 4 + k, :], bank[n][:, :], False, False)
                        mm.then_inc(unit_done, 1)
                pe.wait_ge(al_ready, T0 + NF)
                for k in range(NF - 4, NF):
                    down(k, (v0 + k) % RING, range(ND), False, k == NF - 1, k == NF - 1)

            def post_stat(p, n):
                pe.wait_ge(fsq_done, ND * p + n + 1)
                if n == 0 and p != 1:
                    pe.wait_ge(fg_done, ND * p + 1)
                nc.tensor.matmul(bank[7 if p == 1 else 0][:, :], ONES, SQ[:, n % 2, :], start=n == 0, stop=n == ND - 1).then_inc(fstat_done, 1)

            def turn_v(src, a, count):
                if a >= 2:
                    pe.wait_ge(v_ready, count - 1)
                for t in range(TT):
                    mm = nc.tensor.transpose(bank[4 + a % 2][:, P * t:P * t + P], src[:, P * t:P * t + P], IDENT)
                mm.then_inc(v_turned, 1)

            def attention_pe(A):
                n = len(A.steps)
                for it in range(n + 3):
                    if it < n:
                        w = att_width(A, it)
                        for c in range(A.maps):
                            m = A.m0 + it * A.maps + c
                            k = it * A.maps + c
                            if k >= 2:
                                pe.wait_ge(exp_done if A.name.startswith("mem") else sb_done, m - 1)
                            nc.tensor.matmul(bank[k % 2][:, 0:w], att_q(A, it, c), att_k(A, it, c), start=True, stop=True).then_inc(qk_done, 1)
                    s = it - 2
                    if 0 <= s < n:
                        w = att_width(A, s)
                        pe.wait_ge(p_done, A.s0 + s + 1)
                        if s >= 2:
                            pe.wait_ge(pt_ready, A.s0 + s - 1)
                        for j in range(w // P):
                            mm = nc.tensor.transpose(bank[2 + s % 2][:, P * j:P * j + P], att_sb(A, s, 0)[:, P * j:P * j + P], IDENT)
                        mm.then_inc(p_turned, 1)
                    s = it - 3
                    if 0 <= s < n:
                        h, i = A.steps[s]
                        g = s // A.per_group
                        if s % A.per_group == 0 and g >= 2:
                            pe.wait_ge(oh_done if A.name == "diff" else ol_done, (A.g0 - DIFF_H if A.name == "mem1" else A.g0) + g - 1)
                        w = att_width(A, s)
                        pe.wait_ge(pt_ready, A.s0 + s + 1)
                        for j in range(w // P):
                            mm = nc.tensor.matmul(bank[4 + g % 2][att_group_rows(A, s), P * i:P * i + P], att_v(A, s, j),
                                                  att_pt(A, s)[:, P * j:P * j + P], start=j == 0, stop=j == w // P - 1)
                        mm.then_inc(pv_done, 1)

            def gn_pe(name):
                n, size, groups, width, t0, k = gns[name]
                if k:
                    pe.wait_ge(gn_root, k)
                for i in range(n):
                    pe.wait_ge(gn_sq, t0 + i + 1)
                    win = SEL64_AT + 10 - 2 * i if size == 64 else SEL128_AT + 5 - i
                    nc.tensor.matmul(bank[7][0:groups, 0:width], CONST[:, win:win + groups], SQ[:, i % 2, 0:width],
                                     start=i == 0, stop=i == n - 1).then_inc(gn_stat, 1)
                pe.wait_ge(gn_rec, k + 1)
                sp_ = SP64 if size == 64 else SP128
                for i in range(n):
                    if i >= 2:
                        pe.wait_ge(gn_out, t0 + i - 1)
                    nc.tensor.matmul(bank[5 + i % 2][:, 0:width], sp_[0:groups, i, :], ACC[0:groups, 0:width],
                                     start=True, stop=True).then_inc(gn_spread, 1)

            pe.wait_ge(const_in, 32)
            pe.wait_ge(x_in, 16)
            for n in range(ND):
                for t in range(TT):
                    mm = nc.tensor.transpose(bank[n][:, P * t:P * t + P], XTOK[:, t, P * n:P * n + P], IDENT)
                mm.then_inc(xT_done, 1)
            ffn_pe(0, 0, F1_GU)
            for n in range(ND):
                post_stat(0, n)

            def mx_body(i):
                first = isinstance(i, int)
                for k in range(4):
                    if not first:
                        pe.wait_ge(ev, i * 4 + (k - 3))
                    tile_unit(i * 4 + (MX_IN + k), (MX_IN + k) % RING, bank[k][:, :], XH, XL,
                              (lambda kk: pe.wait_ge(x_ready, ND + kk + 1)) if first and k == 0 else None)
                    if first and k == 0:
                        site_stat(1)
            mx_body(0)
            with pe.Fori(1, 5) as i:
                mx_body(i)
            for a in range(4):
                pe.wait_ge(ev, 16 + a + 1)
                turn_v(U[:, 16 + a, :], a, a)
            with pe.Fori(5, 9) as i:
                mx_body(i)
            pe.wait_ge(tap_done, 3 * TAPS)
            pe.wait_ge(ptap_done, TAPS)
            for t in range(CH):
                mm = nc.tensor.matmul(bank[7][:, :], ONES, CO[:, t, :], start=t == 0, stop=t == CH - 1)
            mm.then_inc(ln_sum, 1)
            for t in range(CH):
                pe.wait_ge(ln_sq, t + 1)
                nc.tensor.matmul(bank[6][:, :], ONES, SQ[:, t % 2, :], start=t == 0, stop=t == CH - 1).then_inc(ln_var, 1)

            def half_unit(u, j, k0, wait):
                pe.wait_ge(lo_ready, u + 1)
                for n in range(2):
                    for k in range(4):
                        if wait:
                            wait(k)
                        mm = split_product(u % RING, 256 * k + P * n, XH[:, k0 + k, :], XL[:, k0 + k, :], bank[(2 * j + n) % 4][:, :],
                                           k == 0, k == 3)
                mm.then_inc(unit_done, 1)

            pe.wait_ge(ev, N_IN1)
            for j in range(4):
                if j >= 2:
                    pe.wait_ge(yb_done, 2 * (j - 1))
                half_unit(MX_CO + j, j, 0, (lambda k: pe.wait_ge(ln_lo, k + 1)) if j == 0 else None)
            pe.wait_ge(yb_done, ND)
            pe.wait_ge(v_ready, 4)
            attention_pe(atts["b1"])
            pe.wait_ge(ol_done, 4)
            for j in range(4):
                if j >= 2:
                    pe.wait_ge(ya_done, 2 * (j - 1))
                half_unit(MX_AO + j, j, 4, None)
            pe.wait_ge(ya_done, ND)
            for n in range(ND):
                if n >= 4:
                    pe.wait_ge(fg_done, ND + n - 3)
                tile_unit(MX_OUT + n, (MX_OUT + n) % RING, bank[n % 4][:, :], XH, XL,
                          (lambda kk: pe.wait_ge(mx_ready, kk + 1)) if n == 0 else None)
                if n:
                    post_stat(1, n - 1)
            post_stat(1, ND - 1)
            ffn_pe(1, 2, F2_GU)
            for n in range(ND):
                post_stat(2, n)

            for layer in range(2):
                u0 = LAYER0 + layer * LAYER_UNITS
                s = 3 + 2 * layer
                pe.wait_ge(mem_norm, NMT * (layer + 1))
                if layer == 0:
                    pe.wait_ge(fg_done, ND * 3)
                else:
                    pe.wait_ge(h_new, ND * (s + 1))
                for k in range(ND):
                    if k >= 2:
                        pe.wait_ge(meml_done, ND * layer + k - 1)
                    for t in range(NMT):
                        mm = nc.tensor.transpose(bank[4 + k % 2][:, P * t:P * t + P], MTOK[:, t, P * k:P * k + P], IDENT)
                    mm.then_inc(mem_turned, 1)
                pe.wait_ge(meml_done, ND * (layer + 1))
                for m in range(4):
                    u = u0 + m
                    tile_unit(u, u % RING, bank[(1, 2, 3, 6)[m]][:, 0:MEM], MH, ML)
                for b in range(NMT):
                    pe.wait_ge(mem_ev, 4 * layer + NMT + b + 1)
                    for t in range(NMT):
                        mm = nc.tensor.transpose(bank[4 + b][:, P * t:P * t + P], MVT[:, b, P * t:P * t + P], IDENT)
                    mm.then_inc(mv_turned, 1)
                e0 = N_IN1 + N_IN2 * layer

                def in_body(i):
                    first = isinstance(i, int)
                    for k in range(4):
                        if not first:
                            pe.wait_ge(ev, i * 4 + (e0 + k - 3))
                        tile_unit(i * 4 + (u0 + 4 + k), (u0 + 4 + k) % RING, bank[k][:, :], XH, XL,
                                  (lambda kk: pe.wait_ge(x_ready, ND * s + kk + 1)) if first and k == 0 else None)
                        if first and k == 0:
                            site_stat(s)
                in_body(0)
                with pe.Fori(1, N_IN2 // 4) as i:
                    in_body(i)
                pe.wait_ge(ev, e0 + N_IN2)
                pe.wait_ge(mv_ready, NMT * (layer + 1))
                for a in range(6):
                    turn_v(U[:, (6 if layer == 0 else 12) + a, :], a, 4 + 6 * layer + a)
                pe.wait_ge(v_ready, 4 + 6 * (layer + 1))
                pe.wait_ge(tab_in, 48 * (layer + 1))
                if layer == 0:
                    gn_pe("qc0")
                    gn_pe("mk0")
                    pe.wait_ge(gn_out, gns["mk0"][4] + 2)
                    plan = [(h, j) for h in range(RET_H) for j in range(TT)]
                    for it in range(len(plan) + 2):
                        if it < len(plan):
                            h, j = plan[it]
                            w = S - P * j
                            rows = slice(64 * (h % 2), 64 * (h % 2) + 64)
                            if it >= 2:
                                pe.wait_ge(ret_decayed, it - 1)
                            nc.tensor.matmul(bank[it % 2][:, 0:w], U[rows, 3 + h // 2, P * j:P * j + P], U[rows, h // 2, P * j:S],
                                             start=True, stop=True).then_inc(ret_qk, 1)
                        k = it - 2
                        if k >= 0:
                            h, j = plan[k]
                            w = S - P * j
                            if j == 0 and h >= 2:
                                pe.wait_ge(ret_ev, h - 1)
                            pe.wait_ge(ret_decayed, k + 1)
                            mm = nc.tensor.matmul(bank[4 + h % 2][:, P * j:S], V2[:, j, P * h:P * h + P], SB2[:, k % 3, 0:w],
                                                  start=j == 0, stop=j == TT - 1)
                            mm.then_inc(ret_pv, 1)
                    pe.wait_ge(ret_ev, RET_H)
                    gn_pe("o0")
                    pe.wait_ge(gn_out, gns["o0"][4] + 6)
                    attention_pe(atts["mem0"])
                else:
                    pe.wait_ge(lam_prod, 2)
                    nc.tensor.matmul(bank[6][:, 0:2], ONES[0:64, :], LAM[0:64, 0:2], start=True, stop=True).then_inc(lam_sum, 1)
                    pe.wait_ge(lam_exp, 1)
                    gn_pe("q1")
                    gn_pe("k1")
                    gn_pe("qc1")
                    gn_pe("mk1")
                    pe.wait_ge(gn_out, gns["mk1"][4] + 2)
                    attention_pe(atts["diff"])
                    pe.wait_ge(oh_done, atts["diff"].g0 + DIFF_H)
                    gn_pe("o1")
                    pe.wait_ge(gn_out, gns["o1"][4] + 6)
                    attention_pe(atts["mem1"])
                w0 = u0 + 4 + N_IN2
                pe.wait_ge(mx_ready, ND + 6 * (layer + 1))
                pe.wait_ge(ol_done, 4 + 2 * (layer + 1))
                for n in range(ND):
                    tile_unit(w0 + n, (w0 + n) % RING, bank[n][:, :], YH, YL)
                ffn_pe(2 + layer, s + 1, w0 + ND)
            for n in range(ND):
                pe.wait_ge(h_new, ND * 7 + n + 1)
                for t in range(TT):
                    mm = nc.tensor.transpose(bank[n][:, P * t:P * t + P], H[:, n, P * t:P * t + P], IDENT)
                mm.then_inc(y_turned, 1)


FENCE_AT = 16512


def pack_columns(inputs):
    def tiles(a):
        return np.asarray(a, np.float32).reshape(-1, P).T

    def halves(a):
        a = np.asarray(a, np.float32).reshape(64, 1)
        return np.concatenate([a, a], 0)

    parts = {
        "f1_pre": tiles(inputs["ffn1_norm_pre"]), "f1_post": tiles(inputs["ffn1_norm_post"]),
        "mx_pre": tiles(inputs["mix_norm_pre"]), "gate_bias": tiles(inputs["gate_bias"]),
        "glu_bias": tiles(inputs["conv_glu_bias"]), "dw_b": tiles(inputs["conv_dw_b"]),
        "ln_g": tiles(inputs["conv_ln_g"]), "ln_b": tiles(inputs["conv_ln_b"]),
        "mx_post": tiles(inputs["mix_norm_post"]), "f2_pre": tiles(inputs["ffn2_norm_pre"]),
        "f2_post": tiles(inputs["ffn2_norm_post"]),
        "dw_w": np.asarray(inputs["conv_dw_w"], np.float32).reshape(TAPS, CH, P).transpose(2, 1, 0).reshape(P, CH * TAPS),
        "attn0": tiles(inputs["attn_norm_w_2"][0]), "attn1": tiles(inputs["attn_norm_w_2"][1]),
        "mem": tiles(inputs["mem_norm_w_2"]),
        "mq0": halves(inputs["mem_q_norm_w_2"][0]), "mq1": halves(inputs["mem_q_norm_w_2"][1]),
        "mk0": halves(inputs["mem_k_norm_w_2"][0]), "mk1": halves(inputs["mem_k_norm_w_2"][1]),
        "ret_gn": tiles(inputs["ret_gn_w_2"]), "dq": halves(inputs["diff_q_norm_w_2"]),
        "dk": halves(inputs["diff_k_norm_w_2"]), "subln": tiles(inputs["diff_subln_w_2"]),
        "ffn0": tiles(inputs["ffn_norm_w_2"][0]), "ffn1": tiles(inputs["ffn_norm_w_2"][1]),
        "lq1": halves(inputs["diff_lambda_q1_2"]), "lk1": halves(inputs["diff_lambda_k1_2"]),
        "lq2": halves(inputs["diff_lambda_q2_2"]), "lk2": halves(inputs["diff_lambda_k2_2"]),
    }
    return np.ascontiguousarray(np.concatenate([parts[name] for name in COLS], 1))


def relative_rows(table):
    p, u = np.arange(P)[:, None], np.arange(256)[None, :]
    return np.ascontiguousarray(np.asarray(table)[0][:, np.minimum(p - u + 256, 256)].transpose(1, 0, 2))


def kernel(**inputs):
    import concourse.bacc as bacc
    from concourse.bass_utils import run_bass_kernel_spmd

    arrays = {"cols": pack_columns(inputs), "rel": relative_rows(inputs["rel_table"]), **shape_constants()}
    for name in ("x", "mem_2", "w_mem_kv_2", "w_in_2", "w_out_2", "w_gate_up_2", "w_down_2"):
        arrays[name] = np.ascontiguousarray(inputs[name])
    for name in ("ffn1_w_gate", "ffn1_w_up", "ffn1_w_down", "w_in", "w_attn_out", "conv_w_out", "w_out",
                 "ffn2_w_gate", "ffn2_w_up", "ffn2_w_down"):
        arrays[name] = np.ascontiguousarray(inputs[name])[0]
    nc = bacc.Bacc("TRN2", target_bir_lowering=False, num_devices=1)
    aps = {name: nc.dram_tensor(f"in_{name}", a.shape, F32, kind="ExternalInput").ap() for name, a in arrays.items()}
    out = nc.dram_tensor("out_y", (1, S, D), F32, kind="ExternalOutput").ap()
    build(nc, aps, out)
    r = run_bass_kernel_spmd(nc, [{f"in_{name}": a for name, a in arrays.items()}], core_ids=[0])
    return r.results[0]["out_y"]
```

```python
from contextlib import ExitStack
import math

import numpy as np
import concourse.bass as bass
from concourse import mybir

F32 = mybir.dt.float32
F32R = mybir.dt.float32r
ALU = mybir.AluOpType
ACT = mybir.ActivationFunctionType
AX_X = mybir.AxisListType.X

P = 128
S = 512
D = 1024
ND = D // P
TT = S // P
FF = 2816
NF = FF // P
EPS = 1e-6
MEM = 256
NMT = MEM // P
NEG = -1e30

HEADS, HD = 8, 64
CH = 512 // P
TAPS = 31
PAD = TAPS - 1
RET_H, DIFF_H, MEM_H = 6, 6, 4
MAIN = 768
NM = MAIN // P
W_IN2 = 3 * MAIN + 256
N_IN2 = W_IN2 // P
N_IN1 = 4608 // P
LAMBDA_INIT = 0.8 - 0.6 * math.exp(-0.3)

RING = 4
AHEAD = 3

GU = 2 * NF
F1_GU = 0
F1_DN = F1_GU + GU
MX_IN = F1_DN + NF
MX_CO = MX_IN + N_IN1
MX_AO = MX_CO + 4
MX_OUT = MX_AO + 4
F2_GU = MX_OUT + ND
F2_DN = F2_GU + GU
LAYER0 = F2_DN + NF
LAYER_UNITS = 4 + N_IN2 + ND + GU + NF
UNITS = LAYER0 + 2 * LAYER_UNITS

COLS = {}


def _columns():
    at = 0
    for name, n in (
        ("f1_pre", ND), ("f1_post", ND), ("mx_pre", ND), ("gate_bias", 2 * ND), ("glu_bias", 2 * CH),
        ("dw_b", CH), ("ln_g", CH), ("ln_b", CH), ("mx_post", ND), ("f2_pre", ND), ("f2_post", ND),
        ("dw_w", CH * TAPS), ("attn0", ND), ("attn1", ND), ("mem", ND), ("mq0", 1), ("mq1", 1),
        ("mk0", 1), ("mk1", 1), ("ret_gn", RET_H), ("dq", 1), ("dk", 1), ("subln", 1),
        ("ffn0", ND), ("ffn1", ND), ("lq1", 1), ("lk1", 1), ("lq2", 1), ("lk2", 1),
    ):
        COLS[name] = (at, n)
        at += n
    return at


NCOLS = _columns()

SEL64_AT = 2 * P
NCONST = 2 * P + 2


def shape_constants():
    p = np.arange(P)
    const = np.zeros((P, NCONST), np.float32)
    const[p, p] = 1.0
    const[:, P:2 * P] = 1.0
    const[:64, SEL64_AT] = 1.0
    const[64:, SEL64_AT + 1] = 1.0
    spread = np.zeros((12, 6, P), np.float32)
    for i in range(6):
        spread[2 * i, i, :64] = 1.0
        spread[2 * i + 1, i, 64:] = 1.0
    log_gamma = np.log(np.float32(1.0) - np.float32(2.0) ** (np.float32(-5.0) - np.arange(RET_H, dtype=np.float32)))
    u = np.arange(S)
    dist = np.abs(u[None, :] - p[:, None]).astype(np.float32)
    seen = (u[None, :] // 64) >= (p[:, None] // 64)
    decay = np.where(seen[None], np.exp(log_gamma[:, None, None] * dist[None]), 0.0).astype(np.float32)
    decay *= np.float32(0.125)
    slopes = (2.0 ** (-8.0 * np.arange(1, DIFF_H + 1, dtype=np.float32) / DIFF_H)).astype(np.float32)
    rel = u - 384
    dist = np.abs(p[:, None] - rel[None, :]).astype(np.float32)
    seen = np.floor_divide(rel[None, :], 64) <= (p[:, None] // 64)
    alibi = np.where(seen[None], -slopes[:, None, None] * dist[None], np.float32(NEG)).astype(np.float32)
    return {
        "const": const,
        "spread": spread.reshape(12, 6 * P),
        "decay": np.ascontiguousarray(decay.transpose(1, 0, 2)),
        "alibi": np.ascontiguousarray(alibi.transpose(1, 0, 2)),
    }


class Attention:

    def __init__(self, name, steps, maps, per_group, first_step, first_group):
        self.name, self.steps, self.maps, self.per_group = name, steps, maps, per_group
        self.s0, self.g0 = first_step, first_group
        self.m0 = None


ORDER2 = [[18, 19, 0, 1, 2, 3, 4, 5] + list(range(6, 18)), list(range(6, 12)) + [18, 19] + list(range(6)) + list(range(12, 18))]
ORDER1 = list(range(8)) + list(range(12, 20)) + list(range(8, 12)) + list(range(20, 36))

def beside_mixer():
    plan = [[] for _ in range(N_IN1)]
    for a in range(4):
        plan[13 + a].append(("turn", a))
    for it in range(HEADS * TT + 3):
        plan[17 + it // 2].append(("b1", it))
    for t in range(CH):
        plan[31].append(("ln_sum", t))
        plan[32].append(("ln_var", t))
        plan[34].append(("ln_silu", t))
        plan[35].append(("ln_hi", t))
    plan[32].append(("ln_root", 0))
    plan[33].append(("ln_norm", 0))
    return plan


def beside_layer0():
    plan = [[] for _ in range(N_IN2)]
    plan[2] = [("sq", "mk0", 0), ("sq", "mk0", 1), ("root", "mk0")]
    plan[3] = [("rows", "mk0"), ("out", "mk0", 0), ("out", "mk0", 1)]
    plan[4] = [("sq", "qc0", 0), ("sq", "qc0", 1), ("root", "qc0")]
    for it in range(MEM_H * TT + 3):
        plan[5 + it // 4].append(("mem0", it))
    for a in range(6):
        plan[9 + a].append(("turn", a))
    for it in range(RET_H * TT + 2):
        plan[10 + it // 4].append(("ret", it))
    for h in range(RET_H):
        plan[12 + h].append(("sq", "o0", h))
    plan[17].append(("root", "o0"))
    plan[18].append(("rows", "o0"))
    for h in range(RET_H):
        plan[18].append(("out", "o0", h))
        if h < 4:
            plan[18].append(("silu", h))
            plan[19].append(("gated", h))
    plan[19].append(("silu", 4))
    return plan


def beside_layer1():
    plan = [[] for _ in range(N_IN2)]
    plan[2] = [("sq", "mk1", 0), ("sq", "mk1", 1), ("root", "mk1")]
    plan[3] = [("rows", "mk1"), ("out", "mk1", 0), ("out", "mk1", 1)]
    plan[4] = [("sq", "k1", 0), ("sq", "k1", 1), ("sq", "k1", 2)]
    plan[5] = [("sq", "k1", 3), ("sq", "k1", 4)]
    plan[6] = [("sq", "k1", 5), ("root", "k1")]
    plan[7] = [("rows", "k1")] + [("out", "k1", i) for i in range(6)]
    plan[8] = [("lam",), ("sq", "qc1", 0), ("sq", "qc1", 1), ("root", "qc1")]
    for it in range(MEM_H * TT + 3):
        plan[9 + it // 4].append(("mem1", it))
    for i in range(6):
        plan[9 + i].append(("sq", "q1", i))
    plan[14].append(("root", "q1"))
    for h in range(5):
        plan[15 + h] += [("turn", h)] + [("diff", TT * h + i) for i in range(TT)]
    plan[19] = [("sq", "o1a", 0), ("sq", "o1a", 1), ("sq", "o1a", 2), ("turn", 4), ("diff", 16), ("root", "o1a"), ("diff", 17),
                ("rows", "o1a"), ("diff", 18), ("out", "o1a", 0), ("out", "o1a", 1), ("diff", 19), ("out", "o1a", 2)]
    return plan


TAIL0 = [("block", 0, k) for k in (6, 7)] + [("silu", 5), ("gated", 4)] + [("block", 0, k) for k in (0, 1, 2, 3)] + \
        [("gated", 5), ("low", 5), ("block", 1, 6), ("block", 1, 7), ("block", 0, 4), ("block", 1, 0), ("block", 1, 1), ("block", 0, 5)] + \
        [("block", 1, k) for k in (2, 3, 4, 5)] + [("block", n, k) for n in (2, 3) for k in (6, 7, 0, 1, 2, 3, 4, 5)]
TAIL1 = [("block", 0, 6), ("block", 0, 7), ("turn", 5), ("low", 2), ("diff", 20), ("block", 0, 0), ("block", 0, 1), ("diff", 21),
         ("block", 0, 2), ("block", 1, 6), ("diff", 22), ("block", 1, 7), ("block", 1, 0), ("sq", "o1b", 0), ("sq", "o1b", 1),
         ("diff", 23), ("block", 1, 1), ("block", 1, 2), ("diff", 24), ("block", 2, 6), ("root", "o1b"),
         ("block", 2, 7), ("block", 2, 0), ("diff", 25), ("rows", "o1b"), ("block", 2, 1), ("out", "o1b", 0), ("diff", 26),
         ("block", 2, 2), ("out", "o1b", 1), ("block", 3, 6), ("block", 3, 7), ("sq", "o1c", 0), ("low", 4), ("root", "o1c"),
         ("block", 3, 0), ("block", 3, 1), ("block", 3, 2), ("block", 0, 3), ("block", 1, 3), ("rows", "o1c"),
         ("block", 2, 3), ("block", 3, 3), ("out", "o1c", 0), ("low", 5), ("block", 0, 4), ("block", 1, 4), ("block", 2, 4), ("block", 3, 4),
         ("block", 0, 5), ("block", 1, 5), ("block", 2, 5), ("block", 3, 5)]


def unit_bank(k):
    return k if k < 4 else k % 2


def build(nc, d, out):
    with ExitStack() as ctx:
        ctx.enter_context(nc.sbuf_tensor("fence", [P, 53200], F32))
        FENCE = FENCE_AT
        taken = [FENCE]

        def place(name, shape, dt, at=None):
            size = 4 * int(np.prod(shape[1:]))
            if at is None:
                at = taken[0]
                taken[0] += (size + 31) // 32 * 32
            return nc.alloc_sbuf_tensor_at(name, shape, dt, offset=at)

        def sem(name):
            return ctx.enter_context(nc.semaphore(name))

        H = place("H", [P, ND, S], F32)
        XH = place("XH", [P, ND, S], F32R)
        XL = place("XL", [P, ND, S], F32R)
        RAW = place("RAW", [P, RING, D], F32)
        WHI = place("WHI", [P, RING, D], F32R)
        WLO = place("WLO", [P, RING, D], F32R)
        R = place("R", [P, S], F32)
        ACC = place("ACC", [P, S], F32)
        SQ = place("SQ", [P, 2, S], F32)
        tmp_at = taken[0]
        TMP = place("TMP", [P, 4, S], F32)
        MTOK = place("MTOK", [P, NMT, D], F32, tmp_at)
        COL = place("COL", [P, NCOLS], F32)
        CONST = place("CONST", [P, NCONST], F32)
        EPSC = place("EPSC", [P, 3], F32)
        PG = place("PG", [P, 3], F32)
        STAT = place("STAT", [P, 32], F32)
        LAM = place("LAM", [P, 8], F32)
        arena = taken[0]
        IDENT, ONES = CONST[:, 0:P], CONST[:, P:2 * P]

        KB = 2048
        AH = place("AH", [P, NF, S], F32R, arena)
        AL = place("AL", [P, NF, S], F32R, arena + NF * KB)
        FG = place("FG", [P, ND, S], F32, arena)
        XTOK = place("XTOK", [P, TT, D], F32, arena)
        U = place("U", [P, N_IN1, S], F32, arena)
        CO = place("CO", [P, CH, S], F32, arena)
        V1 = place("V1", [P, TT, 512], F32, arena + 4 * KB)
        SB1 = place("SB1", [P, 3, S], F32, arena + 16 * KB)
        OH1 = place("OH1", [P, CH, S], F32R, arena + 8 * KB)
        OL1 = place("OL1", [P, CH, S], F32R, arena + 12 * KB)
        CPAD = 544
        C = place("C", [P, CH, CPAD], F32, arena + 36 * KB)
        CNH = place("CNH", [P, CH, S], F32R, arena + 36 * KB)
        CNL = place("CNL", [P, CH, S], F32R, arena)
        PT1 = place("PT1", [P, 2, S], F32, arena + 36 * KB + CH * CPAD * 4)
        BIAS1 = place("BIAS1", [P, HEADS, 256], F32, arena + 38 * KB + CH * CPAD * 4)
        V2 = place("V2", [P, TT, MAIN], F32, arena + 20 * KB)
        TAB = place("TAB", [P, 6, S], F32, arena + 26 * KB)
        SB2 = place("SB2", [P, 6, S], F32, arena + 32 * KB)
        PT2 = place("PT2", [P, 2, S], F32, arena + 38 * KB)
        MKT = place("MKT", [P, NMT, MEM], F32, arena + 40 * KB)
        MV = place("MV", [P, NMT, MEM], F32, arena + 41 * KB)
        SPREAD = place("SPREAD", [P, 6, P], F32, arena + 42 * KB)
        YLM = place("YLM", [P, 2, S], F32R, arena + 42 * KB + 3072)
        GR = place("GR", [P, 48], F32, arena + 44 * KB + 3072)
        RQC = place("RQC", [P, 16], F32, arena + 44 * KB + 3072 + 192)
        RQD = place("RQD", [P, 48], F32, arena + 44 * KB + 3072 + 256)
        MVT = place("MVT", [P, NMT, MEM], F32, arena + 38 * KB)
        MH = place("MH", [P, ND, MEM], F32R, arena + 20 * KB)
        ML = place("ML", [P, ND, MEM], F32R, arena + 24 * KB)
        YH = place("YH", [P, 6, S], F32R, arena)
        YL0 = place("YL0", [P, 6, S], F32R, arena + 20 * KB)
        YL1 = place("YL1", [P, 6, S], F32R, arena + 6 * KB)
        YHM = place("YHM", [P, 2, S], F32R, arena + 18 * KB)
        O2 = place("O2", [P, 6, S], F32, arena + 12 * KB)
        O2R = place("O2R", [P, 6, S], F32, arena + 6 * KB)

        bank = [ctx.enter_context(nc.psum_tensor(f"bank{i}", [P, S], F32)) for i in range(8)]

        const_in = sem("const_in")
        eps_set = sem("eps_set")
        x_in = sem("x_in")
        raw_in = [sem(f"raw_in{i}") for i in range(RING)]
        hi_ready, lo_ready, unit_done = sem("hi_ready"), sem("lo_ready"), sem("unit_done")
        tile_ready = sem("tile_ready")
        xT_done = sem("xT_done")
        h_new, xh_ready, x_ready = sem("h_new"), sem("xh_ready"), sem("x_ready")
        sq_ready, acc_done = sem("sq_ready"), sem("acc_done")
        stat_done, root_done, rstd_done = sem("stat_done"), sem("root_done"), sem("rstd_done")
        g_scaled, silu_done, u_scaled = sem("g_scaled"), sem("silu_done"), sem("u_scaled")
        a_done, ah_ready, al_ready = sem("a_done"), sem("ah_ready"), sem("al_ready")
        fsq_done, fg_done, fstat_done = sem("fsq_done"), sem("fg_done"), sem("fstat_done")
        froot_done, frstd_done, f_scaled = sem("froot_done"), sem("frstd_done"), sem("f_scaled")
        ev = sem("ev")
        glu_sig, c_done, gate_done = sem("glu_sig"), sem("c_done"), sem("gate_done")
        pad_zero = sem("pad_zero")
        tap_done, ptap_mul, ptap_done = sem("tap_done"), sem("ptap_mul"), sem("ptap_done")
        ln_sum, ln_cent, ln_sq, ln_var = sem("ln_sum"), sem("ln_cent"), sem("ln_sq"), sem("ln_var")
        ln_root, ln_rstd, ln_norm = sem("ln_root"), sem("ln_rstd"), sem("ln_norm")
        ln_silu, ln_hi, ln_lo = sem("ln_silu"), sem("ln_hi"), sem("ln_lo")
        yb_done, ya_done, m_done = sem("yb_done"), sem("ya_done"), sem("m_done")
        mh_done, mx_ready = sem("mh_done"), sem("mx_ready")
        v_turned, v_ready = sem("v_turned"), sem("v_ready")
        bias_in, bias_masked = sem("bias_in"), sem("bias_masked")
        qk_done, sb_done, nmax_done = sem("qk_done"), sem("sb_done"), sem("nmax_done")
        exp_done, rinv_done, p_done = sem("exp_done"), sem("rinv_done"), sem("p_done")
        p_turned, pt_ready, pv_done = sem("p_turned"), sem("pt_ready"), sem("pv_done")
        oh_done, ol_done = sem("oh_done"), sem("ol_done")
        mem_in, mem_ss, mem_root = sem("mem_in"), sem("mem_ss"), sem("mem_root")
        mem_rec, mem_norm, mem_turned = sem("mem_rec"), sem("mem_norm"), sem("mem_turned")
        memh_done, meml_done, mem_ev = sem("memh_done"), sem("meml_done"), sem("mem_ev")
        mv_turned, mv_ready = sem("mv_turned"), sem("mv_ready")
        gn_sq, gn_stat, gn_root = sem("gn_sq"), sem("gn_stat"), sem("gn_root")
        gn_rec, gn_spread, gn_out = sem("gn_rec"), sem("gn_spread"), sem("gn_out")
        gn_rows, gn_row_out, gains_set = sem("gn_rows"), sem("gn_row_out"), sem("gains_set")
        tab_in, spread_in = sem("tab_in"), sem("spread_in")
        sg_done, ret_qk, ret_decayed, ret_pv, ret_ev = sem("sg_done"), sem("ret_qk"), sem("ret_decayed"), sem("ret_pv"), sem("ret_ev")
        og_gated = sem("og_gated")
        lam_prod, lam_sum, lam_exp, lam_set = sem("lam_prod"), sem("lam_sum"), sem("lam_exp"), sem("lam_set")
        y_turned, y_ready, y_out = sem("y_turned"), sem("y_ready"), sem("y_out")

        def col(name, i=0, rows=slice(None)):
            at, n = COLS[name]
            return COL[rows, at + i:at + i + 1]

        def view(ap):
            return ap.bitcast(F32)

        SITES = ["f1_pre", "mx_pre", "f2_pre", "attn0", "ffn0", "attn1", "ffn1"]
        b1_steps = [(h, i) for h in range(HEADS) for i in range(TT)]
        mem_steps = [(h, i) for h in range(MEM_H) for i in range(TT)]
        diff_steps = [(h, i) for h in range(DIFF_H) for i in range(TT)]
        atts, s0, g0, m0 = {}, 0, 0, 0
        for name, steps, maps, per in (("b1", b1_steps, 1, 8), ("mem0", mem_steps, 1, 8),
                                       ("mem1", mem_steps, 1, 8), ("diff", diff_steps, 2, 4)):
            A = Attention(name, steps, maps, per, s0, g0)
            A.m0 = m0
            atts[name] = A
            s0, g0, m0 = s0 + len(steps), g0 + len(steps) // per, m0 + maps * len(steps)

        def att_width(A, s):
            h, i = A.steps[s]
            return MEM if A.name.startswith("mem") else P * (i + 1)

        def att_q(A, s, c):
            h, i = A.steps[s]
            tok = slice(P * i, P * i + P)
            if A.name == "b1":
                return U[64 * (h % 2):64 * (h % 2) + 64, 8 + h // 2, tok]
            if A.name == "diff":
                return U[64 * c:64 * c + 64, h, tok]
            return U[64 * (h % 2):64 * (h % 2) + 64, 18 + h // 2, tok]

        def att_k(A, s, c):
            h, i = A.steps[s]
            w = att_width(A, s)
            if A.name == "b1":
                return U[64 * (h % 2):64 * (h % 2) + 64, 12 + h // 2, 0:w]
            if A.name == "diff":
                return U[64 * c:64 * c + 64, 6 + h, 0:w]
            return MKT[64 * (h % 2):64 * (h % 2) + 64, h // 2, 0:w]

        def att_v(A, s, j):
            h, i = A.steps[s]
            if A.name == "b1":
                return V1[:, j, 64 * h:64 * h + 64]
            if A.name == "diff":
                return V2[:, j, P * h:P * h + P]
            return MV[:, j, 64 * h:64 * h + 64]

        def att_sb(A, s, c):
            return (SB1[:, s % 3, :] if A.name == "b1" else SB2[:, (s % 3) * A.maps + c, :])

        def att_pt(A, s):
            return PT1[:, s % 2, :] if A.name == "b1" else PT2[:, s % 2, :]

        def att_group_rows(A, s):
            h, i = A.steps[s]
            return slice(0, P) if A.name == "diff" else slice(64 * (h % 2), 64 * (h % 2) + 64)

        def stat_cols(A, s, c):
            k = (s % 3) * A.maps + c
            return STAT[:, k:k + 1], STAT[:, 8 + k:9 + k], STAT[:, 16 + k:17 + k]

        def att_scale(A, s, c):
            h, i = A.steps[s]
            if A.name == "b1":
                return 0.125
            if A.name == "diff":
                return RQD[:, 12 * i + 2 * h + c:12 * i + 2 * h + c + 1]
            return RQC[:, 4 * i + h:4 * i + h + 1]

        gns, t0, q0 = {}, 0, 0
        for k, (name, n, size, width) in enumerate((
                ("mk0", 2, 64, MEM), ("qc0", 2, 64, S), ("o0", 6, 128, S), ("mk1", 2, 64, MEM), ("k1", 6, 64, S),
                ("qc1", 2, 64, S), ("q1", 6, 64, S), ("o1a", 3, 128, S), ("o1b", 2, 128, S), ("o1c", 1, 128, S))):
            gns[name] = (n, size, width, t0, k, q0)
            t0 += n
            if name not in ("qc0", "qc1", "q1"):
                q0 += n

        def gn_tile(name, i):
            return {"qc0": lambda: U[:, 18 + i, :], "qc1": lambda: U[:, 18 + i, :],
                    "mk0": lambda: MKT[:, i, :], "mk1": lambda: MKT[:, i, :],
                    "o0": lambda: O2R[:, i, :], "o1a": lambda: O2[:, i, :], "o1b": lambda: O2[:, 3 + i, :],
                    "o1c": lambda: O2[:, 5, :], "q1": lambda: U[:, i, :], "k1": lambda: U[:, 6 + i, :]}[name]()

        def gn_gain(name, i):
            return {"mk0": lambda: PG[:, 0:1], "mk1": lambda: PG[:, 1:2], "o0": lambda: col("ret_gn", i),
                    "k1": lambda: PG[:, 2:3]}.get(name, lambda: LAM[:, 5:6])()

        def gn_table(name):
            n, size, width, t0, k, q0 = gns[name]
            to = RQC if name in ("qc0", "qc1") else RQD if name == "q1" else GR
            return to[:, 0:2 * n * (width // P)]

        def gn_source(eng, name, i):
            if name[:2] == "mk":
                eng.wait_ge(mem_ev, 4 * int(name[2]) + i + 1)
            elif name[0] in "qk":
                layer = int(name[-1])
                tile = {"q": 18 if name[1] == "c" else 0, "k": 6}[name[0]] + i
                eng.wait_ge(ev, N_IN1 + N_IN2 * layer + ORDER2[layer].index(tile) + 1)
            elif name == "o0":
                eng.wait_ge(ret_ev, i + 1)
            else:
                eng.wait_ge(oh_done, atts["diff"].g0 + {"a": 0, "b": 3, "c": 5}[name[2]] + i + 1)

        def y_hi(layer, k):
            return YH[:, k, :] if k < 6 else YHM[:, k - 6, :]

        def y_lo(layer, k):
            return YLM[:, k - 6, :] if k >= 6 else YL0[:, k, :] if layer == 0 else YL1[:, k, :]

        V_TILES = [(16, 12, 0), (6, 8, 4), (12, 14, 10)]
        E0 = [0, N_IN1, N_IN1 + N_IN2]

        def v_place(phase, a):
            return (V1 if phase == 0 else V2)[:, :, P * a:P * a + P]

        ROWED = ["mk0", "o0", "mk1", "k1", "o1a", "o1b", "o1c"]
        PLAN1, PLAN2, TAIL = beside_mixer(), [beside_layer0(), beside_layer1()], [TAIL0, TAIL1]

        block = ctx.enter_context(nc.Block())

        @block.sync
        def _(sp):
            sp.dma_start(COL[:, :], d["cols"]).then_inc(const_in, 16)
            sp.dma_start(CONST[:, :], d["const"]).then_inc(const_in, 16)
            sp.dma_start(XTOK[:, :, :], d["x"][0].rearrange("(t p) n -> p t n", p=P)).then_inc(x_in, 16)

            def load(u, j, src):
                if not isinstance(u, int) or u >= RING:
                    sp.wait_ge(lo_ready, u - RING + 1)
                slot = RAW[:, j, :]
                if len(src.shape) == 3:
                    slot = slot.rearrange("p (t n) -> p t n", n=src.shape[2])
                sp.dma_start(slot, src).then_inc(raw_in[j], 16)

            def tile_src(w, n):
                return w.rearrange("(t p) n -> p t n", p=P)[:, :, bass.ts(n, P)]

            def tiles(w, n0, count, u0):
                done = 0
                if u0 < RING:
                    for k in range(4):
                        load(u0 + k, (u0 + k) % RING, tile_src(w, n0 + k))
                    done = 4
                if count - done >= 4:
                    with sp.Fori(done // 4, count // 4) as i:
                        for k in range(4):
                            load(u0 + i * 4 + k, (u0 + k) % RING, tile_src(w, n0 + i * 4 + k))
                for k in range(count // 4 * 4, count):
                    load(u0 + k, (u0 + k) % RING, tile_src(w, n0 + k))

            def ffn(wg, wu, up0, wd, u0):
                def body(i, first):
                    for k in range(4):
                        w, off = (wg, 0) if k % 2 == 0 else (wu, up0)
                        load(u0 + i * 4 + k, (u0 + k) % RING, tile_src(w, off + i * 2 + k // 2))
                lo = 0
                if u0 == 0:
                    body(0, True)
                    lo = 1
                with sp.Fori(lo, NF // 2) as i:
                    body(i, False)
                v0 = u0 + GU
                rows = wd.rearrange("(t p) n -> t p n", p=P)
                with sp.Fori(0, NF // 4) as i:
                    for k in range(4):
                        load(v0 + i * 4 + k, (v0 + k) % RING, rows[i * 4 + k])
                for k in range(NF // 4 * 4, NF):
                    load(v0 + k, (v0 + k) % RING, rows[k])

            def half_rows(w, u0):
                for k in range(4):
                    load(u0 + k, (u0 + k) % RING, w.rearrange("(t p) n -> p t n", p=P)[:, :, 256 * k:256 * k + 256])

            def second_tables(layer, u0, k):
                if k == 0:
                    sp.wait_ge(unit_done, u0)
                    sp.dma_start(SPREAD[0:12, :, :], d["spread"].rearrange("g (i p) -> g i p", p=P)).then_inc(spread_in, 16)
                if k == 8:
                    sp.wait_ge(unit_done, u0 + 4)
                    sp.dma_start(TAB[:, :, :], d["decay" if layer == 0 else "alibi"]).then_inc(tab_in, 16)

            ffn(d["ffn1_w_gate"], d["ffn1_w_up"], 0, d["ffn1_w_down"], F1_GU)
            tiles(d["w_in"], 12, 8, MX_IN)
            sp.wait_ge(unit_done, MX_IN)
            sp.dma_start(BIAS1[:, :, :], d["rel"]).then_inc(bias_in, 16)
            tiles(d["w_in"], 4, 8, MX_IN + 8)
            tiles(d["w_in"], 0, 4, MX_IN + 16)
            tiles(d["w_in"], 20, 16, MX_IN + 20)
            half_rows(d["conv_w_out"], MX_CO)
            half_rows(d["w_attn_out"], MX_AO)
            tiles(d["w_out"], 0, ND, MX_OUT)
            ffn(d["ffn2_w_gate"], d["ffn2_w_up"], 0, d["ffn2_w_down"], F2_GU)
            for layer in range(2):
                u0 = LAYER0 + layer * LAYER_UNITS
                tiles(d["w_mem_kv_2"][layer], 0, 4, u0)
                for k in range(N_IN2):
                    load(u0 + 4 + k, (u0 + 4 + k) % RING, tile_src(d["w_in_2"][layer], ORDER2[layer][k]))
                    second_tables(layer, u0, k)
                tiles(d["w_out_2"][layer], 0, ND, u0 + 4 + N_IN2)
                ffn(d["w_gate_up_2"][layer], d["w_gate_up_2"][layer], NF, d["w_down_2"][layer], u0 + 4 + N_IN2 + ND)
            for n in range(0, ND, 2):
                sp.wait_ge(y_ready, n + 2)
                sp.dma_start(out[0].rearrange("(t p) n -> p t n", p=P)[:, :, n * P:(n + 2) * P],
                             XTOK[:, :, n * P:(n + 2) * P]).then_inc(y_out, 16)
            sp.wait_ge(y_out, 16 * (ND // 2))

        @block.gpsimd
        def _(pool):
            nc.gpsimd.memset(EPSC[:, 0:1], EPS).then_inc(eps_set, 1)
            nc.gpsimd.memset(EPSC[:, 1:2], 4 * EPS).then_inc(eps_set, 1)
            nc.gpsimd.memset(EPSC[:, 2:3], 64 * EPS).then_inc(eps_set, 1)

            def site_sums(s):
                for n in range(1, ND):
                    pool.wait_ge(sq_ready, ND * s + n + 1)
                    if n >= 2:
                        pool.wait_ge(acc_done, (ND - 1) * s + n - 1)
                    nc.gpsimd.tensor_tensor(ACC[:, :], ACC[:, :], SQ[:, n % 2, :], ALU.add).then_inc(acc_done, 1)

            site_sums(0)
            pool.wait_ge(unit_done, MX_IN)
            nc.gpsimd.memset(C[:, :, 0:PAD], 0.0).then_inc(pad_zero, 1)
            site_sums(1)
            pool.wait_ge(c_done, CH)
            pool.wait_ge(pad_zero, 1)
            pool.wait_ge(stat_done, 2)
            t = CH - 1
            for tap in range(TAPS):
                w = col("dw_w", t * TAPS + tap)
                if tap == 0:
                    nc.gpsimd.tensor_scalar(CO[:, t, :], C[:, t, 0:S], w, col("dw_b", t), ALU.mult, ALU.add).then_inc(ptap_done, 1)
                    continue
                if tap >= 3:
                    pool.wait_ge(ptap_done, tap - 1)
                nc.gpsimd.tensor_scalar(SQ[:, tap % 2, :], C[:, t, tap:tap + S], w, 0.0, ALU.mult, ALU.add).then_inc(ptap_mul, 1)
                pool.wait_ge(ptap_mul, tap)
                pool.wait_ge(ptap_done, tap)
                nc.gpsimd.tensor_tensor(CO[:, t, :], CO[:, t, :], SQ[:, tap % 2, :], ALU.add).then_inc(ptap_done, 1)
            for s in range(2, 7):
                site_sums(s)

        @block.scalar
        def _(act):
            def hi(u, j=None):
                if isinstance(u, int):
                    if u >= UNITS:
                        return
                    j = u % RING
                    act.wait_ge(raw_in[j], 16 * (u // RING + 1))
                    if u >= RING:
                        act.wait_ge(unit_done, u - RING + 1)
                nc.scalar.activation(WHI[:, j, :], RAW[:, j, :], ACT.Copy).then_inc(hi_ready, 1)

            def hi_loop(u0, i, k):
                j = (u0 + k) % RING
                act.wait_ge(raw_in[j], (i * 16) + 16 * ((u0 + k) // RING + 1))
                act.wait_ge(unit_done, i * 4 + (u0 + k - RING + 1))
                hi(None, j)

            def hi_any(u0, i, k):
                if isinstance(i, int):
                    hi(u0 + 4 * i + k)
                else:
                    hi_loop(u0, i, k)

            def site_act(s, n):
                act.wait_ge(h_new, ND * s + n + 1)
                nc.scalar.mul(XH[:, n, :], H[:, n, :], col(SITES[s], n)).then_inc(xh_ready, 1)
                if n >= 3:
                    act.wait_ge(acc_done, (ND - 1) * s + n - 2)
                nc.scalar.activation(ACC[:, :] if n == 0 else SQ[:, n % 2, :], H[:, n, :], ACT.Square).then_inc(sq_ready, 1)

            def site_root(s):
                act.wait_ge(stat_done, s + 1)
                nc.scalar.activation(R[:, :], bank[7][:, :], ACT.Sqrt, scale=1.0 / D, bias=EPSC[:, 0:1]).then_inc(root_done, 1)

            def ffn_act(f, s, u0, after_gu=None, in_down=None):
                T0 = NF * f

                def body(i):
                    for t in range(2):
                        hi_any(u0 + AHEAD, i, 2 * t)
                        if t == 0 and isinstance(i, int) and i == 0:
                            site_root(s)
                        act.wait_ge(g_scaled, i * 2 + (T0 + t + 1))
                        nc.scalar.activation(TMP[:, t, :], TMP[:, t, :], ACT.Silu).then_inc(silu_done, 1)
                        hi_any(u0 + AHEAD, i, 2 * t + 1)
                        act.wait_ge(a_done, i * 2 + (T0 + t + 1))
                        nc.scalar.activation(AH[:, i * 2 + t, :], TMP[:, 2 + t, :], ACT.Copy).then_inc(ah_ready, 1)
                body(0)
                with act.Fori(1, NF // 2) as i:
                    body(i)
                if after_gu:
                    after_gu()
                v0 = u0 + GU
                with act.Fori(0, 4) as i:
                    for k in range(4):
                        hi_loop(v0 + AHEAD, i, k)
                if in_down:
                    in_down()
                for k in range(16, NF):
                    hi(v0 + k + AHEAD)

            def post_square(p, n, wait):
                wait(act, n)
                if n >= 2:
                    act.wait_ge(fstat_done, ND * p + n - 1)
                nc.scalar.activation(SQ[:, n % 2, :], bank[n if p != 1 else n % 4][:, :], ACT.Square).then_inc(fsq_done, 1)

            def post_root(p):
                four = 1 if p == 1 else 4
                act.wait_ge(fstat_done, ND * (p + 1))
                nc.scalar.activation(R[:, :], bank[7 if p == 1 else 0][:, :], ACT.Sqrt, scale=four / D,
                                     bias=EPSC[:, four // 4:four // 4 + 1]).then_inc(froot_done, 1)

            def down_wait(e, t8):
                def wait(eng, n):
                    if n < ND - 1:
                        eng.wait_ge(tile_ready, (ND - 1) * t8 + n + 1)
                    else:
                        eng.wait_ge(unit_done, e)
                return wait

            def attention_act(A, it):
                n = len(A.steps)
                if it < n:
                    w = att_width(A, it)
                    for c in range(A.maps):
                        nmax, total, _ = stat_cols(A, it, c)
                        act.wait_ge(nmax_done, A.m0 + it * A.maps + c + 1)
                        src = att_sb(A, it, c)[:, 0:w]
                        if A.name.startswith("mem"):
                            if it >= 3:
                                act.wait_ge(p_turned, A.s0 + it - 2)
                            nc.scalar.activation(src, bank[2 + it % 2][:, 0:w], ACT.Exp, scale=att_scale(A, it, c), bias=nmax,
                                                 accum_out=total).then_inc(exp_done, 1)
                        else:
                            nc.scalar.activation(src, src, ACT.Exp, bias=nmax, accum_out=total).then_inc(exp_done, 1)
                s = it - 2
                if 0 <= s < n:
                    w = att_width(A, s)
                    act.wait_ge(p_turned, A.s0 + s + 1)
                    if s >= 2:
                        act.wait_ge(pv_done, A.s0 + s - 1)
                    nc.scalar.activation(att_pt(A, s)[:, 0:w], bank[4 + s % 2][:, 0:w], ACT.Copy).then_inc(pt_ready, 1)
                s = it - 3
                if s >= 0 and s % A.per_group == A.per_group - 1:
                    g = s // A.per_group
                    act.wait_ge(pv_done, A.s0 + s + 1)
                    dst = O2[:, g, :] if A.name == "diff" else OH1[:, g, :] if A.name == "b1" else YHM[:, g, :]
                    nc.scalar.activation(dst, bank[6][:, :], ACT.Copy).then_inc(oh_done, 1)

            def stage(phase, what):
                kind = what[0]
                if kind in atts:
                    attention_act(atts[kind], what[1])
                elif kind == "turn":
                    a = what[1]
                    tile, unit, before = V_TILES[phase]
                    if phase == 0 and a == 0:
                        act.wait_ge(c_done, CH)
                    act.wait_ge(v_turned, before + a + 1)
                    nc.scalar.activation(v_place(phase, a), bank[unit_bank(unit + a)][:, :].rearrange("p (t f) -> p t f", f=P),
                                         ACT.Copy).then_inc(v_ready, 1)
                elif kind == "sq":
                    name, i = what[1:]
                    n, size, width, t0, k, q0 = gns[name]
                    gn_source(act, name, i)
                    if t0 + i >= 2:
                        act.wait_ge(gn_stat, t0 + i - 1)
                    nc.scalar.activation(SQ[:, (t0 + i) % 2, 0:width], gn_tile(name, i), ACT.Square).then_inc(gn_sq, 1)
                elif kind == "root":
                    name = what[1]
                    n, size, width, t0, k, q0 = gns[name]
                    act.wait_ge(gn_stat, t0 + n)
                    scale, eps = (1.0, 2) if name[0] == "q" else (1.0 / size, 0)
                    table = gn_table(name)
                    nc.scalar.activation(table, bank[7][:, 0:table.shape[1]], ACT.Sqrt, scale=scale, bias=EPSC[:, eps:eps + 1]).then_inc(gn_root, 1)
                elif kind == "rows":
                    n, size, width, t0, k, q0 = gns[what[1]]
                    act.wait_ge(gn_rows, ROWED.index(what[1]) + 1)
                    if q0:
                        act.wait_ge(gn_spread, q0)
                    nc.scalar.activation(ACC[0:2 * n, 0:width], bank[7][0:2 * n, 0:width], ACT.Copy).then_inc(gn_row_out, 1)
                elif kind == "out" and what[1][:2] == "o1":
                    h = {"a": 0, "b": 3, "c": 5}[what[1][2]] + what[2]
                    act.wait_ge(gn_out, gns[what[1]][5] + what[2] + 1)
                    nc.scalar.activation(y_hi(1, h), O2[:, h, :], ACT.Copy).then_inc(mh_done, 1)
                elif kind == "lam":
                    act.wait_ge(lam_sum, 1)
                    nc.scalar.activation(LAM[:, 2:4], bank[7][:, 0:2], ACT.Exp).then_inc(lam_exp, 1)
                elif kind == "silu":
                    h = what[1]
                    act.wait_ge(ev, E0[1] + 14 + h + 1)
                    nc.scalar.activation(U[:, 12 + h, :], U[:, 12 + h, :], ACT.Silu).then_inc(sg_done, 1)
                elif kind == "gated":
                    act.wait_ge(og_gated, what[1] + 1)
                    nc.scalar.activation(y_hi(0, what[1]), O2R[:, what[1], :], ACT.Copy).then_inc(mh_done, 1)
                elif kind == "ret":
                    k = what[1] - 2
                    if k >= 0 and k % TT == TT - 1:
                        h = k // TT
                        act.wait_ge(ret_pv, TT * (h + 1))
                        nc.scalar.activation(O2R[:, h, :], bank[4 + h % 2][:, :], ACT.Copy).then_inc(ret_ev, 1)
                elif kind == "ln_var":
                    t = what[1]
                    act.wait_ge(ln_cent, t + 1)
                    if t >= 2:
                        act.wait_ge(ln_var, t - 1)
                    nc.scalar.activation(SQ[:, t % 2, :], CO[:, t, :], ACT.Square).then_inc(ln_sq, 1)
                elif kind == "ln_root":
                    act.wait_ge(ln_var, CH)
                    nc.scalar.activation(ACC[:, :], bank[7][:, :], ACT.Sqrt, scale=1.0 / 512, bias=EPSC[:, 0:1]).then_inc(ln_root, 1)
                elif kind == "ln_silu":
                    t = what[1]
                    act.wait_ge(ln_norm, t + 1)
                    nc.scalar.activation(CO[:, t, :], CO[:, t, :], ACT.Silu, scale=col("ln_g", t), bias=col("ln_b", t)).then_inc(ln_silu, 1)
                elif kind == "ln_hi":
                    t = what[1]
                    act.wait_ge(ln_silu, t + 1)
                    nc.scalar.activation(CNH[:, t, :], CO[:, t, :], ACT.Copy).then_inc(ln_hi, 1)

            for u in range(AHEAD):
                hi(u)
            act.wait_ge(const_in, 32)
            act.wait_ge(eps_set, 3)
            for n in range(ND):
                site_act(0, n)
            ffn_act(0, 0, F1_GU)
            wait = down_wait(MX_IN, 0)
            for n in range(ND):
                post_square(0, n, wait)
            post_root(0)
            for n in range(ND):
                site_act(1, n)

            for k in range(N_IN1):
                hi(MX_IN + k + AHEAD)
                if k == 0:
                    site_root(1)
                if k == 8:
                    for a in range(CH):
                        act.wait_ge(ev, 5 + a)
                        nc.scalar.activation(U[:, 4 + a, :], U[:, 4 + a, :], ACT.Sigmoid, bias=col("glu_bias", CH + a)).then_inc(glu_sig, 1)
                for what in PLAN1[k]:
                    stage(0, what)

            def gates(n0):
                for n in range(n0, n0 + ND):
                    act.wait_ge(ev, 20 + n + 1)
                    nc.scalar.activation(U[:, 20 + n, :], U[:, 20 + n, :], ACT.Sigmoid, bias=col("gate_bias", n)).then_inc(gate_done, 1)

            hi(MX_CO + AHEAD)
            gates(ND)
            hi(MX_CO + 1 + AHEAD)
            gates(0)
            hi(MX_CO + 2 + AHEAD)
            hi(MX_CO + 3 + AHEAD)
            for j in range(4):
                hi(MX_AO + j + AHEAD)
                for n in (2 * j, 2 * j + 1):
                    act.wait_ge(m_done, n + 1)
                    nc.scalar.activation(XH[:, n, :], U[:, 20 + n, :], ACT.Copy).then_inc(mh_done, 1)
            for n in range(ND):
                hi(MX_OUT + n + AHEAD)
                post_square(1, n, lambda eng, n: eng.wait_ge(unit_done, MX_OUT + n + 1))
            post_root(1)
            for n in range(ND):
                site_act(2, n)

            def mem_load(layer):
                act.wait_ge(al_ready, NF * (2 + layer))
                act.dma_start(MTOK[:, :, :], d["mem_2"][0].rearrange("(t p) n -> p t n", p=P)).then_inc(mem_in, 16)

            def mem_sums(layer):
                act.wait_ge(mem_in, 16 * (layer + 1))
                for t in range(NMT):
                    if t:
                        act.wait_ge(mem_ss, NMT * layer + t)
                    nc.scalar.activation(SQ[:, :, :].rearrange("p a n -> p (a n)"), MTOK[:, t, :], ACT.Square,
                                         accum_out=LAM[:, 6 + t:7 + t]).then_inc(mem_ss, 1)
                act.wait_ge(mem_ss, NMT * (layer + 1))
                nc.scalar.activation(LAM[:, 6:8], LAM[:, 6:8], ACT.Sqrt, scale=1.0 / D, bias=EPSC[:, 0:1]).then_inc(mem_root, 1)

            ffn_act(1, 2, F2_GU, lambda: mem_load(0), lambda: mem_sums(0))

            for layer in range(2):
                u0 = LAYER0 + layer * LAYER_UNITS
                if layer == 0:
                    wait = down_wait(LAYER0, 1)
                    for n in range(ND):
                        post_square(2, n, wait)
                for k in range(ND):
                    act.wait_ge(mem_turned, ND * layer + k + 1)
                    nc.scalar.mul(MH[:, k, :], bank[4 + k % 2][:, 0:MEM], col("mem", k)).then_inc(memh_done, 1)
                if layer == 0:
                    post_root(2)
                s = 3 + 2 * layer
                for n in range(ND):
                    site_act(s, n)
                for m in range(4):
                    hi(u0 + m + AHEAD)
                for b in range(NMT):
                    act.wait_ge(mv_turned, NMT * layer + b + 1)
                    nc.scalar.activation(MV[:, :, P * b:P * b + P], bank[4 + b][:, 0:MEM].rearrange("p (t f) -> p t f", f=P),
                                         ACT.Copy).then_inc(mv_ready, 1)

                for k in range(N_IN2):
                    hi(u0 + 4 + k + AHEAD)
                    if k == 0:
                        site_root(s)
                    for what in PLAN2[layer][k]:
                        stage(1 + layer, what)
                w0 = u0 + 4 + N_IN2
                hi(w0 + AHEAD)
                for what in TAIL[layer]:
                    stage(1 + layer, what)
                for n in range(ND):
                    if n:
                        hi(w0 + n + AHEAD)
                    site_act(s + 1, n)
                if layer == 0:
                    ffn_act(2, s + 1, u0 + 4 + N_IN2 + ND, lambda: mem_load(1), lambda: mem_sums(1))
                else:
                    ffn_act(3, s + 1, u0 + 4 + N_IN2 + ND)
            for n in range(ND):
                act.wait_ge(y_turned, n + 1)
                nc.scalar.activation(XTOK[:, :, P * n:P * n + P], bank[n][:, :].rearrange("p (t f) -> p t f", f=P),
                                     ACT.Copy).then_inc(y_ready, 1)

        @block.vector
        def _(dve):
            def lo(u, j=None):
                if isinstance(u, int):
                    if u >= UNITS:
                        return
                    j = u % RING
                    dve.wait_ge(hi_ready, u + 1)
                nc.vector.tensor_tensor(WLO[:, j, :], RAW[:, j, :], view(WHI[:, j, :]), ALU.subtract).then_inc(lo_ready, 1)

            def lo_any(u0, i, k):
                if isinstance(i, int):
                    lo(u0 + 4 * i + k)
                else:
                    dve.wait_ge(hi_ready, i * 4 + (u0 + k + 1))
                    lo(None, (u0 + k) % RING)

            def site_dve(s, n):
                dve.wait_ge(xh_ready, ND * s + n + 1)
                nc.vector.scalar_tensor_tensor(out=XL[:, n, :], in0=H[:, n, :], scalar=col(SITES[s], n), in1=view(XH[:, n, :]),
                                               op0=ALU.mult, op1=ALU.subtract).then_inc(x_ready, 1)

            def site_rstd(s):
                dve.wait_ge(root_done, s + 1)
                nc.vector.reciprocal(R[:, :], R[:, :]).then_inc(rstd_done, 1)
                dve.wait_ge(rstd_done, s + 1)

            def ffn_dve(f, s, u0, in_down=None):
                T0 = NF * f

                def al(T, t):
                    dve.wait_ge(ah_ready, T + (T0 + 1))
                    nc.vector.tensor_tensor(AL[:, T, :], TMP[:, 2 + t, :], view(AH[:, T, :]), ALU.subtract).then_inc(al_ready, 1)

                def body(i):
                    first = isinstance(i, int)
                    for t in range(2):
                        lo_any(u0 + AHEAD, i, 2 * t)
                        dve.wait_ge(unit_done, i * 4 + (u0 + 2 * t + 1))
                        if first and t == 0:
                            site_rstd(s)
                        if not first:
                            dve.wait_ge(a_done, i * 2 + (T0 + t - 1))
                        nc.vector.tensor_tensor(TMP[:, t, :], bank[2 * t][:, :], R[:, :], ALU.mult).then_inc(g_scaled, 1)
                        if not first or t:
                            al(i * 2 + t - 1, 1 - t)
                        lo_any(u0 + AHEAD, i, 2 * t + 1)
                        dve.wait_ge(unit_done, i * 4 + (u0 + 2 * t + 2))
                        if not first:
                            dve.wait_ge(al_ready, i * 2 + (T0 + t - 1))
                        nc.vector.tensor_tensor(TMP[:, 2 + t, :], bank[2 * t + 1][:, :], R[:, :], ALU.mult).then_inc(u_scaled, 1)
                        dve.wait_ge(u_scaled, i * 2 + (T0 + t + 1))
                        dve.wait_ge(silu_done, i * 2 + (T0 + t + 1))
                        nc.vector.tensor_tensor(TMP[:, 2 + t, :], TMP[:, 2 + t, :], TMP[:, t, :], ALU.mult).then_inc(a_done, 1)
                body(0)
                with dve.Fori(1, NF // 2) as i:
                    body(i)
                al(NF - 1, 1)
                v0 = u0 + GU
                with dve.Fori(0, 4) as i:
                    for k in range(4):
                        lo_any(v0 + AHEAD, i, k)
                if in_down:
                    in_down()
                for k in range(16, NF):
                    lo(v0 + k + AHEAD)

            def post_gain(p, n, name):
                dve.wait_ge(fsq_done, ND * p + n + 1)
                nc.vector.tensor_scalar(FG[:, n, :], bank[n if p != 1 else n % 4][:, :], col(name, n), None, ALU.mult).then_inc(fg_done, 1)

            def post_update(p, s):
                dve.wait_ge(froot_done, p + 1)
                nc.vector.reciprocal(R[:, :], R[:, :]).then_inc(frstd_done, 1)
                dve.wait_ge(frstd_done, p + 1)
                dve.wait_ge(fg_done, ND * (p + 1))
                for n in range(ND):
                    nc.vector.tensor_tensor(FG[:, n, :], FG[:, n, :], R[:, :], ALU.mult).then_inc(f_scaled, 1)
                    dve.wait_ge(f_scaled, ND * p + n + 1)
                    nc.vector.tensor_tensor(H[:, n, :], H[:, n, :], FG[:, n, :], ALU.add).then_inc(h_new, 1)
                    if n:
                        site_dve(s, n - 1)
                site_dve(s, ND - 1)

            def down_ready(e, t8):
                def ready(n):
                    if n < ND - 1:
                        dve.wait_ge(tile_ready, (ND - 1) * t8 + n + 1)
                    else:
                        dve.wait_ge(unit_done, e)
                return ready

            def attention_dve(A, it):
                n = len(A.steps)
                is_mem = A.name.startswith("mem")
                if it == 0:
                    if A.name != "b1":
                        dve.wait_ge(gn_rec, gns["q1" if A.name == "diff" else "qc" + A.name[3]][4] + 1)
                        dve.wait_ge(p_turned, A.s0)
                    else:
                        dve.wait_ge(v_turned, 4)
                        dve.wait_ge(bias_masked, 1)
                    if A.name == "diff":
                        dve.wait_ge(tab_in, 32)
                if it < n:
                    h, i = A.steps[it]
                    w = att_width(A, it)
                    for c in range(A.maps):
                        m = A.m0 + it * A.maps + c
                        nmax, total, rinv = stat_cols(A, it, c)
                        src = bank[2 + (it * A.maps + c) % 2][:, 0:w]
                        scale = att_scale(A, it, c)
                        dve.wait_ge(qk_done, m + 1)
                        if is_mem:
                            if it >= 3:
                                dve.wait_ge(exp_done, m - 2)
                            nc.vector.tensor_reduce(nmax, src, AX_X, ALU.max, negate=True).then_inc(sb_done, 1)
                            dve.wait_ge(sb_done, m + 1)
                            nc.vector.tensor_scalar(nmax, nmax, scale, None, ALU.mult).then_inc(nmax_done, 1)
                            continue
                        sb = att_sb(A, it, c)
                        if it >= 3:
                            dve.wait_ge(p_turned, A.s0 + it - 2)
                        if A.name == "b1":
                            near = min(w, 256)
                            if w > near:
                                nc.vector.tensor_scalar(sb[:, 0:w - near], src[:, 0:w - near], scale, BIAS1[:, h, 0:1],
                                                        ALU.mult, ALU.add)
                            nc.vector.scalar_tensor_tensor(out=sb[:, w - near:w], in0=src[:, w - near:w], scalar=scale,
                                                           in1=BIAS1[:, h, 256 - near:256], op0=ALU.mult, op1=ALU.add).then_inc(sb_done, 1)
                        else:
                            nc.vector.scalar_tensor_tensor(out=sb[:, 0:w], in0=src, scalar=scale, in1=TAB[:, h, S - w:S],
                                                           op0=ALU.mult, op1=ALU.add).then_inc(sb_done, 1)
                        dve.wait_ge(sb_done, m + 1)
                        nc.vector.tensor_reduce(nmax, sb[:, 0:w], AX_X, ALU.max, negate=True).then_inc(nmax_done, 1)
                s = it - 1
                if 0 <= s < n:
                    w = att_width(A, s)
                    m = A.m0 + s * A.maps
                    for c in range(A.maps):
                        _, total, rinv = stat_cols(A, s, c)
                        dve.wait_ge(exp_done, m + c + 1)
                        nc.vector.reciprocal(rinv, total).then_inc(rinv_done, 1)
                    dve.wait_ge(rinv_done, m + A.maps)
                    p0 = att_sb(A, s, 0)[:, 0:w]
                    _, _, r0 = stat_cols(A, s, 0)
                    if A.maps == 1:
                        nc.vector.tensor_scalar(p0, p0, r0, None, ALU.mult).then_inc(p_done, 1)
                    else:
                        _, _, r1 = stat_cols(A, s, 1)
                        nc.vector.tensor_scalar(r1, r1, LAM[:, 4:5], None, ALU.mult).then_inc(lam_prod, 1)
                        nc.vector.tensor_scalar(p0, p0, r0, None, ALU.mult).then_inc(lam_prod, 1)
                        dve.wait_ge(lam_prod, 2 + 2 * (s + 1))
                        nc.vector.scalar_tensor_tensor(out=p0, in0=att_sb(A, s, 1)[:, 0:w], scalar=r1, in1=p0,
                                                       op0=ALU.mult, op1=ALU.add).then_inc(p_done, 1)
                s = it - 3
                if s >= 0 and s % A.per_group == A.per_group - 1 and A.name != "diff":
                    g = s // A.per_group
                    high, low = (OH1[:, g, :], OL1[:, g, :]) if A.name == "b1" else (YHM[:, g, :], YLM[:, g, :])
                    dve.wait_ge(oh_done, A.g0 + g + 1)
                    nc.vector.tensor_tensor(low, bank[6][:, :], view(high), ALU.subtract).then_inc(ol_done, 1)

            def y_low(layer, h):
                dve.wait_ge(mh_done, ND + 6 * layer + h + 1)
                nc.vector.tensor_tensor(y_lo(layer, h), (O2 if layer else O2R)[:, h, :], view(y_hi(layer, h)), ALU.subtract).then_inc(mx_ready, 1)

            def stage(phase, what):
                kind = what[0]
                if kind in atts:
                    attention_dve(atts[kind], what[1])
                elif kind == "root":
                    k = gns[what[1]][4]
                    table = gn_table(what[1])
                    dve.wait_ge(gn_root, k + 1)
                    nc.vector.reciprocal(table, table).then_inc(gn_rec, 1)
                elif kind == "out":
                    name, i = what[1:]
                    q0 = gns[name][5]
                    width = gns[name][2]
                    dve.wait_ge(gn_spread, q0 + i + 1)
                    tile = gn_tile(name, i)
                    nc.vector.scalar_tensor_tensor(out=tile, in0=tile, scalar=gn_gain(name, i), in1=bank[7][:, 0:width],
                                                   op0=ALU.mult, op1=ALU.mult).then_inc(gn_out, 1)
                    if name[:2] == "o1" and i:
                        y_low(1, {"a": 0, "b": 3}[name[2]] + i - 1)
                elif kind == "low":
                    y_low(phase - 1, what[1])
                elif kind == "lam":
                    dve.wait_ge(lam_exp, 1)
                    nc.vector.tensor_tensor(LAM[:, 4:5], LAM[:, 3:4], LAM[:, 2:3], ALU.subtract).then_inc(lam_set, 1)
                    dve.wait_ge(lam_set, 1)
                    nc.vector.tensor_scalar(LAM[:, 4:5], LAM[:, 4:5], -LAMBDA_INIT, None, ALU.add).then_inc(lam_set, 1)
                    nc.vector.tensor_scalar(LAM[:, 5:6], col("subln"), 1.0 - LAMBDA_INIT, None, ALU.mult).then_inc(lam_set, 1)
                    dve.wait_ge(lam_set, 3)
                elif kind == "gated":
                    h = what[1]
                    dve.wait_ge(gn_out, gns["o0"][5] + h + 1)
                    dve.wait_ge(sg_done, h + 1)
                    nc.vector.tensor_tensor(O2R[:, h, :], O2R[:, h, :], U[:, 12 + h, :], ALU.mult).then_inc(og_gated, 1)
                    if h:
                        y_low(0, h - 1)
                elif kind == "ret" and what[1] < RET_H * TT:
                    k = what[1]
                    h, j = k // TT, k % TT
                    w = S - P * j
                    if k == 0:
                        dve.wait_ge(tab_in, 16)
                        dve.wait_ge(p_turned, atts["mem0"].s0 + 16)
                    dve.wait_ge(ret_qk, k + 1)
                    if k >= 3:
                        dve.wait_ge(ret_pv, k - 2)
                    nc.vector.tensor_tensor(SB2[:, k % 3, 0:w], bank[2 + k % 2][:, 0:w], TAB[:, h, 0:w], ALU.mult).then_inc(ret_decayed, 1)
                elif kind == "ln_sum" and what[1] == CH - 1:
                    dve.wait_ge(ln_sum, 1)
                    for t in range(CH):
                        nc.vector.scalar_tensor_tensor(out=CO[:, t, :], in0=bank[7][:, :], scalar=-1.0 / 512, in1=CO[:, t, :],
                                                       op0=ALU.mult, op1=ALU.add).then_inc(ln_cent, 1)
                elif kind == "ln_root":
                    dve.wait_ge(ln_root, 1)
                    nc.vector.reciprocal(ACC[:, :], ACC[:, :]).then_inc(ln_rstd, 1)
                elif kind == "ln_norm":
                    dve.wait_ge(ln_rstd, 1)
                    for t in range(CH):
                        nc.vector.tensor_tensor(CO[:, t, :], CO[:, t, :], ACC[:, :], ALU.mult).then_inc(ln_norm, 1)
                elif kind == "ln_hi":
                    t = what[1]
                    dve.wait_ge(ln_hi, t + 1)
                    nc.vector.tensor_tensor(CNL[:, t, :], CO[:, t, :], view(CNH[:, t, :]), ALU.subtract).then_inc(ln_lo, 1)

            for u in range(AHEAD):
                lo(u)
            dve.wait_ge(const_in, 32)
            nc.vector.tensor_tensor(PG[:, 0:1], col("mq0"), col("mk0"), ALU.mult).then_inc(gains_set, 1)
            nc.vector.tensor_tensor(PG[:, 1:2], col("mq1"), col("mk1"), ALU.mult).then_inc(gains_set, 1)
            nc.vector.tensor_tensor(PG[:, 2:3], col("dq"), col("dk"), ALU.mult).then_inc(gains_set, 1)
            dve.wait_ge(gains_set, 3)
            nc.vector.tensor_tensor(LAM[0:64, 0:1], col("lq1", 0, slice(0, 64)), col("lk1", 0, slice(0, 64)), ALU.mult).then_inc(lam_prod, 1)
            nc.vector.tensor_tensor(LAM[0:64, 1:2], col("lq2", 0, slice(0, 64)), col("lk2", 0, slice(0, 64)), ALU.mult).then_inc(lam_prod, 1)
            for n in range(ND):
                dve.wait_ge(xT_done, n + 1)
                nc.vector.tensor_copy(H[:, n, :], bank[n][:, :]).then_inc(h_new, 1)
                if n:
                    site_dve(0, n - 1)
            site_dve(0, ND - 1)
            ffn_dve(0, 0, F1_GU)
            for n in range(ND):
                post_gain(0, n, "f1_post")
            post_update(0, 1)

            def taps(a, b):
                for j in range(a, b):
                    tap, t = j // 3, j % 3
                    w = col("dw_w", t * TAPS + tap)
                    if tap == 0:
                        nc.vector.tensor_scalar(CO[:, t, :], C[:, t, 0:S], w, col("dw_b", t), ALU.mult, ALU.add).then_inc(tap_done, 1)
                        continue
                    dve.wait_ge(tap_done, j - 2)
                    nc.vector.scalar_tensor_tensor(out=CO[:, t, :], in0=C[:, t, tap:tap + S], scalar=w, in1=CO[:, t, :],
                                                   op0=ALU.mult, op1=ALU.add).then_inc(tap_done, 1)

            tap_at = 0
            for k in range(N_IN1):
                lo(MX_IN + k + AHEAD)
                if k == 8:
                    for a in range(CH):
                        dve.wait_ge(glu_sig, a + 1)
                        nc.vector.scalar_tensor_tensor(out=C[:, a, PAD:PAD + S], in0=U[:, a, :], scalar=col("glu_bias", a), in1=U[:, 4 + a, :],
                                                       op0=ALU.add, op1=ALU.mult).then_inc(c_done, 1)
                    dve.wait_ge(pad_zero, 1)
                    dve.wait_ge(c_done, CH)
                if k == 14:
                    dve.wait_ge(bias_in, 16)
                    nc.vector.memset(BIAS1[0:64, :, 192:256], NEG).then_inc(bias_masked, 1)
                for what in PLAN1[k]:
                    stage(0, what)
                if k > 8:
                    n = min(5 if k < 17 else 4, 3 * TAPS - tap_at)
                    taps(tap_at, tap_at + n)
                    tap_at += n
                dve.wait_ge(unit_done, MX_IN + k + 1)
                if k == 0:
                    site_rstd(1)
                nc.vector.tensor_tensor(U[:, ORDER1[k], :], bank[unit_bank(k)][:, :], R[:, :], ALU.mult).then_inc(ev, 1)
            assert tap_at == 3 * TAPS
            for j in range(4):
                lo(MX_CO + j + AHEAD)
                dve.wait_ge(unit_done, MX_CO + j + 1)
                for n in (2 * j, 2 * j + 1):
                    dve.wait_ge(gate_done, n + 1)
                    nc.vector.tensor_tensor(U[:, 28 + n, :], bank[n % 4][:, :], U[:, 28 + n, :], ALU.mult).then_inc(yb_done, 1)

            def m_lo(n):
                dve.wait_ge(mh_done, n + 1)
                nc.vector.tensor_tensor(XL[:, n, :], U[:, 20 + n, :], view(XH[:, n, :]), ALU.subtract).then_inc(mx_ready, 1)

            for j in range(4):
                lo(MX_AO + j + AHEAD)
                dve.wait_ge(unit_done, MX_AO + j + 1)
                for n in (2 * j, 2 * j + 1):
                    dve.wait_ge(gate_done, ND + n + 1)
                    nc.vector.tensor_tensor(U[:, 20 + n, :], bank[n % 4][:, :], U[:, 20 + n, :], ALU.mult).then_inc(ya_done, 1)
                    dve.wait_ge(ya_done, n + 1)
                    dve.wait_ge(yb_done, n + 1)
                    nc.vector.tensor_tensor(U[:, 20 + n, :], U[:, 20 + n, :], U[:, 28 + n, :], ALU.add).then_inc(m_done, 1)
                    if n:
                        m_lo(n - 1)
            m_lo(ND - 1)
            for n in range(ND):
                lo(MX_OUT + n + AHEAD)
                post_gain(1, n, "mx_post")
            post_update(1, 2)

            def mem_scale(layer):
                dve.wait_ge(mem_root, layer + 1)
                nc.vector.reciprocal(LAM[:, 6:8], LAM[:, 6:8]).then_inc(mem_rec, 1)
                dve.wait_ge(mem_rec, layer + 1)
                for t in range(NMT):
                    nc.vector.tensor_scalar(MTOK[:, t, :], MTOK[:, t, :], LAM[:, 6 + t:7 + t], None, ALU.mult).then_inc(mem_norm, 1)

            ffn_dve(1, 2, F2_GU, lambda: mem_scale(0))

            for layer in range(2):
                u0 = LAYER0 + layer * LAYER_UNITS
                s = 3 + 2 * layer
                if layer == 0:
                    for n in range(ND):
                        post_gain(2, n, "f2_post")
                else:
                    ready = down_ready(u0, 2)
                    for n in range(ND):
                        ready(n)
                        nc.vector.tensor_tensor(H[:, n, :], H[:, n, :], bank[n][:, :], ALU.add).then_inc(h_new, 1)
                for k in range(ND):
                    dve.wait_ge(memh_done, ND * layer + k + 1)
                    nc.vector.scalar_tensor_tensor(out=ML[:, k, :], in0=bank[4 + k % 2][:, 0:MEM], scalar=col("mem", k), in1=view(MH[:, k, :]),
                                                   op0=ALU.mult, op1=ALU.subtract).then_inc(meml_done, 1)
                if layer == 0:
                    post_update(2, 3)
                else:
                    for n in range(ND):
                        site_dve(s, n)
                for m in range(4):
                    lo(u0 + m + AHEAD)
                    dve.wait_ge(unit_done, u0 + m + 1)
                    dst = MKT[:, m, :] if m < NMT else MVT[:, m - NMT, :]
                    nc.vector.tensor_copy(dst, bank[(1, 2, 3, 6)[m]][:, 0:MEM]).then_inc(mem_ev, 1)

                for k in range(N_IN2):
                    lo(u0 + 4 + k + AHEAD)
                    for what in PLAN2[layer][k]:
                        stage(1 + layer, what)
                    dve.wait_ge(unit_done, u0 + 4 + k + 1)
                    if k == 0:
                        site_rstd(s)
                    nc.vector.tensor_tensor(U[:, ORDER2[layer][k], :], bank[unit_bank(k)][:, :], R[:, :], ALU.mult).then_inc(ev, 1)
                w0 = u0 + 4 + N_IN2
                lo(w0 + AHEAD)
                for what in TAIL[layer]:
                    stage(1 + layer, what)
                for n in range(ND):
                    if n:
                        lo(w0 + n + AHEAD)
                    dve.wait_ge(unit_done, w0 + n + 1)
                    nc.vector.tensor_tensor(H[:, n, :], H[:, n, :], bank[n][:, :], ALU.add).then_inc(h_new, 1)
                    if n:
                        site_dve(s + 1, n - 1)
                site_dve(s + 1, ND - 1)
                ffn_dve(2 + layer, s + 1, w0 + ND, (lambda: mem_scale(1)) if layer == 0 else None)
            ready = down_ready(UNITS, 3)
            for n in range(ND):
                ready(n)
                nc.vector.tensor_tensor(H[:, n, :], H[:, n, :], bank[n][:, :], ALU.add).then_inc(h_new, 1)

        @block.tensor
        def _(pe):
            def split_product(j, at, rhs_hi, rhs_lo, dst, start, stop):
                w = slice(at, at + P)
                nc.tensor.matmul(dst, WHI[:, j, w], rhs_hi, start=start, stop=False)
                nc.tensor.matmul(dst, WHI[:, j, w], rhs_lo, start=False, stop=False)
                return nc.tensor.matmul(dst, WLO[:, j, w], rhs_hi, start=False, stop=stop)

            def tile_unit(u, j, dst, xh, xl, before=None, plan=(), phase=0):
                pe.wait_ge(lo_ready, u + 1)
                for k in range(ND):
                    if before:
                        before(k)
                    mm = split_product(j, P * k, xh[:, k, :], xl[:, k, :], dst, k == 0, k == ND - 1)
                    if k == ND - 1:
                        mm.then_inc(unit_done, 1)
                    for n, what in enumerate(plan):
                        if max(1, (n + 1) * ND // (len(plan) + 1)) == k:
                            stage(phase, what)

            def site_stat(s):
                pe.wait_ge(acc_done, (ND - 1) * (s + 1))
                nc.tensor.matmul(bank[7][:, :], ONES, ACC[:, :], start=True, stop=True).then_inc(stat_done, 1)

            def ffn_pe(f, s, u0):
                T0 = NF * f

                def body(i):
                    first = isinstance(i, int)
                    for k in range(4):
                        if not first:
                            pe.wait_ge(g_scaled if k % 2 == 0 else u_scaled, i * 2 + (T0 + k // 2 - 1))
                        tile_unit(i * 4 + (u0 + k), (u0 + k) % RING, bank[k][:, :], XH, XL,
                                  (lambda kk: pe.wait_ge(x_ready, ND * s + kk + 1)) if first and k == 0 else None)
                        if first and k == 0:
                            site_stat(s)
                body(0)
                with pe.Fori(1, NF // 2) as i:
                    body(i)
                v0 = u0 + GU

                def down(k, j, order, start, stop, tiles):
                    pe.wait_ge(lo_ready, v0 + k + 1)
                    for n in order:
                        mm = split_product(j, P * n, AH[:, k, :], AL[:, k, :], bank[n][:, :], start, stop)
                        if tiles and n < ND - 1:
                            mm.then_inc(tile_ready, 1)
                    mm.then_inc(unit_done, 1)

                pe.wait_ge(al_ready, T0 + NF - 2)
                pe.wait_ge(root_done, s + 1)
                pe.wait_ge(lo_ready, v0 + 1)
                for n in (4, 5, 6, 7, 0, 1, 2, 3):
                    if n == 0:
                        pe.wait_ge(g_scaled, T0 + NF)
                        pe.wait_ge(u_scaled, T0 + NF)
                    mm = split_product(v0 % RING, P * n, AH[:, 0, :], AL[:, 0, :], bank[n][:, :], True, False)
                mm.then_inc(unit_done, 1)
                down(1, (v0 + 1) % RING, range(ND), False, False, False)
                with pe.Fori(0, (NF - 6) // 4) as i:
                    for k in range(2, 6):
                        pe.wait_ge(lo_ready, i * 4 + (v0 + k + 1))
                        for n in range(ND):
                            mm = split_product((v0 + k) % RING, P * n, AH[:, i * 4 + k, :], AL[:, i * 4 + k, :], bank[n][:, :], False, False)
                        mm.then_inc(unit_done, 1)
                pe.wait_ge(al_ready, T0 + NF)
                for k in range(NF - 4, NF):
                    down(k, (v0 + k) % RING, range(ND), False, k == NF - 1, k == NF - 1)

            def post_stat(p, n):
                pe.wait_ge(fsq_done, ND * p + n + 1)
                if n == 0 and p != 1:
                    pe.wait_ge(fg_done, ND * p + 1)
                nc.tensor.matmul(bank[7 if p == 1 else 0][:, :], ONES, SQ[:, n % 2, :], start=n == 0, stop=n == ND - 1).then_inc(fstat_done, 1)

            def attention_pe(A, it):
                n = len(A.steps)
                if it == 0 and A.name != "b1":
                    name = "k1" if A.name == "diff" else "mk" + A.name[3]
                    pe.wait_ge(gn_out, gns[name][5] + gns[name][0])
                if it < n:
                    h, i = A.steps[it]
                    w = att_width(A, it)
                    if i == 0:
                        pe.wait_ge(ev, {"b1": 16 + h // 2, "mem0": E0[1] + 3, "mem1": E0[2] + 7, "diff": E0[2] + 8 + h}[A.name] + 1)
                    for c in range(A.maps):
                        m = A.m0 + it * A.maps + c
                        k = it * A.maps + c
                        if k >= 2:
                            pe.wait_ge(exp_done if A.name.startswith("mem") else sb_done, m - 1)
                        elif m >= 2:
                            pe.wait_ge(exp_done, A.m0)
                        nc.tensor.matmul(bank[2 + k % 2][:, 0:w], att_q(A, it, c), att_k(A, it, c), start=True, stop=True).then_inc(qk_done, 1)
                s = it - 2
                if 0 <= s < n:
                    w = att_width(A, s)
                    pe.wait_ge(p_done, A.s0 + s + 1)
                    if A.s0 + s >= 2:
                        pe.wait_ge(pt_ready, A.s0 + s - 1)
                    for j in range(w // P):
                        mm = nc.tensor.transpose(bank[4 + s % 2][:, P * j:P * j + P], att_sb(A, s, 0)[:, P * j:P * j + P], IDENT)
                    mm.then_inc(p_turned, 1)
                s = it - 3
                if 0 <= s < n:
                    h, i = A.steps[s]
                    g = s // A.per_group
                    if s % A.per_group == 0 and A.g0 + g > 0:
                        pe.wait_ge(oh_done if A.name == "diff" and g else ol_done, A.g0 + g)
                    if i == 0 and not A.name.startswith("mem"):
                        pe.wait_ge(v_ready, 4 if A.name == "b1" else V_TILES[2][2] + h + 1)
                    if s == 0 and A.name.startswith("mem"):
                        pe.wait_ge(mv_ready, NMT * (int(A.name[3]) + 1))
                    w = att_width(A, s)
                    pe.wait_ge(pt_ready, A.s0 + s + 1)
                    for j in range(w // P):
                        mm = nc.tensor.matmul(bank[6][att_group_rows(A, s), P * i:P * i + P], att_v(A, s, j),
                                              att_pt(A, s)[:, P * j:P * j + P], start=j == 0, stop=j == w // P - 1)
                    mm.then_inc(pv_done, 1)

            def stage(phase, what):
                kind = what[0]
                if kind in atts:
                    attention_pe(atts[kind], what[1])
                elif kind == "turn":
                    a = what[1]
                    tile, unit, before = V_TILES[phase]
                    pe.wait_ge(ev, E0[phase] + unit + a + 1)
                    for t in range(TT):
                        mm = nc.tensor.transpose(bank[unit_bank(unit + a)][:, P * t:P * t + P], U[:, tile + a, P * t:P * t + P], IDENT)
                    mm.then_inc(v_turned, 1)
                elif kind == "sq":
                    name, i = what[1:]
                    n, size, width, t0, k, q0 = gns[name]
                    if i == 0:
                        pe.wait_ge(root_done, 4 if phase == 1 else 6)
                        if k:
                            pe.wait_ge(gn_root, k)
                            pe.wait_ge(gn_out, q0)
                        if name == "qc1":
                            pe.wait_ge(lam_exp, 1)
                    pe.wait_ge(gn_sq, t0 + i + 1)
                    ones = CONST[:, SEL64_AT:SEL64_AT + 2] if size == 64 else ONES[:, 0:2]
                    for t in range(width // P):
                        at = t * 2 * n + 2 * i
                        mm = nc.tensor.matmul(bank[7][:, at:at + 2], SQ[:, (t0 + i) % 2, P * t:P * t + P], ones, start=True, stop=True)
                    mm.then_inc(gn_stat, 1)
                elif kind == "rows":
                    n, size, width, t0, k, q0 = gns[what[1]]
                    pe.wait_ge(gn_rec, k + 1)
                    for t in range(width // P):
                        mm = nc.tensor.transpose(bank[7][0:2 * n, P * t:P * t + P], GR[:, t * 2 * n:(t + 1) * 2 * n], IDENT)
                    mm.then_inc(gn_rows, 1)
                elif kind == "out":
                    name, i = what[1:]
                    n, size, width, t0, k, q0 = gns[name]
                    if i == 0:
                        pe.wait_ge(spread_in, 16 * phase)
                        pe.wait_ge(gn_row_out, ROWED.index(name) + 1)
                    else:
                        pe.wait_ge(gn_out, q0 + i)
                    nc.tensor.matmul(bank[7][:, 0:width], SPREAD[0:2 * n, i, :], ACC[0:2 * n, 0:width], start=True, stop=True).then_inc(gn_spread, 1)
                elif kind == "lam":
                    pe.wait_ge(lam_prod, 2)
                    pe.wait_ge(gn_out, gns["k1"][5] + 6)
                    nc.tensor.matmul(bank[7][:, 0:2], ONES[0:64, :], LAM[0:64, 0:2], start=True, stop=True).then_inc(lam_sum, 1)
                elif kind == "ret":
                    it = what[1]
                    if it < RET_H * TT:
                        h, j = it // TT, it % TT
                        w = S - P * j
                        rows = slice(64 * (h % 2), 64 * (h % 2) + 64)
                        if it == 0:
                            pe.wait_ge(ev, E0[1] + 8)
                            pe.wait_ge(exp_done, atts["mem1"].m0)
                        if it >= 2:
                            pe.wait_ge(ret_decayed, it - 1)
                        nc.tensor.matmul(bank[2 + it % 2][:, 0:w], U[rows, 3 + h // 2, P * j:P * j + P], U[rows, h // 2, P * j:S],
                                         start=True, stop=True).then_inc(ret_qk, 1)
                    k = it - 2
                    if k >= 0:
                        h, j = k // TT, k % TT
                        w = S - P * j
                        if j == 0:
                            pe.wait_ge(v_ready, V_TILES[1][2] + h + 1)
                            if h >= 2:
                                pe.wait_ge(ret_ev, h - 1)
                            else:
                                pe.wait_ge(pt_ready, atts["mem1"].s0)
                        pe.wait_ge(ret_decayed, k + 1)
                        nc.tensor.matmul(bank[4 + h % 2][:, P * j:S], V2[:, j, P * h:P * h + P], SB2[:, k % 3, 0:w],
                                         start=j == 0, stop=j == TT - 1).then_inc(ret_pv, 1)
                elif kind == "ln_sum":
                    t = what[1]
                    if t == 0:
                        pe.wait_ge(tap_done, 3 * TAPS)
                        pe.wait_ge(ptap_done, TAPS)
                    mm = nc.tensor.matmul(bank[7][:, :], ONES, CO[:, t, :], start=t == 0, stop=t == CH - 1)
                    if t == CH - 1:
                        mm.then_inc(ln_sum, 1)
                elif kind == "ln_var":
                    t = what[1]
                    if t == 0:
                        pe.wait_ge(ln_cent, CH)
                    pe.wait_ge(ln_sq, t + 1)
                    nc.tensor.matmul(bank[7][:, :], ONES, SQ[:, t % 2, :], start=t == 0, stop=t == CH - 1).then_inc(ln_var, 1)
                elif kind == "block":
                    n, k = what[1:]
                    layer = phase - 1
                    w0 = LAYER0 + layer * LAYER_UNITS + 4 + N_IN2
                    if k == 6:
                        pe.wait_ge(lo_ready, w0 + n + 1)
                        pe.wait_ge(ev, E0[phase] + N_IN2)
                        pe.wait_ge(v_ready, V_TILES[phase][2] + (5 if n == 0 and layer else 6))
                        if n >= 2 and layer:
                            pe.wait_ge(sb_done, atts["diff"].m0 + 2 * DIFF_H * TT)
                        elif n >= 2:
                            pe.wait_ge(ret_decayed, RET_H * TT)
                        if n == 0:
                            pe.wait_ge(ol_done, 4 + 2 * (layer + 1))
                    elif k < 6:
                        pe.wait_ge(mx_ready, ND + 6 * layer + k + 1)
                    mm = split_product((w0 + n) % RING, P * k, y_hi(layer, k), y_lo(layer, k), bank[n][:, :], k == 6, k == 5)
                    if k == 5:
                        mm.then_inc(unit_done, 1)

            pe.wait_ge(const_in, 32)
            pe.wait_ge(x_in, 16)
            for n in range(ND):
                for t in range(TT):
                    mm = nc.tensor.transpose(bank[n][:, P * t:P * t + P], XTOK[:, t, P * n:P * n + P], IDENT)
                mm.then_inc(xT_done, 1)
            ffn_pe(0, 0, F1_GU)
            for n in range(ND):
                post_stat(0, n)

            def projection(phase, s, u_in, plan, v_unit, n_v):
                for k in range(len(plan)):
                    if k >= 4:
                        pe.wait_ge(ev, E0[phase] + (k - 1 if k >= 6 else k - 3))
                    if v_unit <= k - 2 < v_unit + n_v:
                        pe.wait_ge(v_ready, V_TILES[phase][2] + k - 2 - v_unit + 1)
                    tile_unit(u_in + k, (u_in + k) % RING, bank[unit_bank(k)][:, :], XH, XL,
                              (lambda kk: pe.wait_ge(x_ready, ND * s + kk + 1)) if k == 0 else None, plan[k], phase)
                    if k == 0:
                        site_stat(s)

            projection(0, 1, MX_IN, PLAN1, 12, 4)

            def half_unit(u, j, xh, xl, wait):
                pe.wait_ge(lo_ready, u + 1)
                for n in range(2):
                    for k in range(4):
                        if wait:
                            wait(k)
                        mm = split_product(u % RING, 256 * k + P * n, xh[:, k, :], xl[:, k, :], bank[(2 * j + n) % 4][:, :],
                                           k == 0, k == 3)
                mm.then_inc(unit_done, 1)

            pe.wait_ge(ev, N_IN1)
            for j in range(4):
                if j >= 2:
                    pe.wait_ge(yb_done, 2 * (j - 1))
                half_unit(MX_CO + j, j, CNH, CNL, (lambda k: pe.wait_ge(ln_lo, k + 1)) if j == 0 else None)
            pe.wait_ge(ol_done, 4)
            for j in range(4):
                if j < 2:
                    pe.wait_ge(yb_done, 4 + 2 * (j + 1))
                else:
                    pe.wait_ge(ya_done, 2 * (j - 1))
                half_unit(MX_AO + j, j, OH1, OL1, None)
            pe.wait_ge(ya_done, ND)
            for n in range(ND):
                if n >= 4:
                    pe.wait_ge(fg_done, ND + n - 3)
                tile_unit(MX_OUT + n, (MX_OUT + n) % RING, bank[n % 4][:, :], XH, XL,
                          (lambda kk: pe.wait_ge(mx_ready, kk + 1)) if n == 0 else None)
                if n:
                    post_stat(1, n - 1)
            post_stat(1, ND - 1)
            ffn_pe(1, 2, F2_GU)
            for n in range(ND):
                post_stat(2, n)

            for layer in range(2):
                u0 = LAYER0 + layer * LAYER_UNITS
                s = 3 + 2 * layer
                pe.wait_ge(mem_norm, NMT * (layer + 1))
                if layer == 0:
                    pe.wait_ge(fg_done, ND * 3)
                else:
                    pe.wait_ge(h_new, ND * (s + 1))
                for k in range(ND):
                    if k >= 2:
                        pe.wait_ge(meml_done, ND * layer + k - 1)
                    for t in range(NMT):
                        mm = nc.tensor.transpose(bank[4 + k % 2][:, P * t:P * t + P], MTOK[:, t, P * k:P * k + P], IDENT)
                    mm.then_inc(mem_turned, 1)
                pe.wait_ge(meml_done, ND * (layer + 1))
                for m in range(4):
                    u = u0 + m
                    tile_unit(u, u % RING, bank[(1, 2, 3, 6)[m]][:, 0:MEM], MH, ML)
                for b in range(NMT):
                    pe.wait_ge(mem_ev, 4 * layer + NMT + b + 1)
                    for t in range(NMT):
                        mm = nc.tensor.transpose(bank[4 + b][:, P * t:P * t + P], MVT[:, b, P * t:P * t + P], IDENT)
                    mm.then_inc(mv_turned, 1)
                projection(1 + layer, s, u0 + 4, PLAN2[layer], V_TILES[1 + layer][1], 6)
                for what in TAIL[layer]:
                    stage(1 + layer, what)
                w0 = u0 + 4 + N_IN2
                if layer:
                    pe.wait_ge(oh_done, atts["diff"].g0 + DIFF_H)
                    pe.wait_ge(gn_out, gns["o1c"][5] + 1)
                for n in range(4, ND):
                    pe.wait_ge(lo_ready, w0 + n + 1)
                    for k in range(ND):
                        mm = split_product((w0 + n) % RING, P * k, y_hi(layer, k), y_lo(layer, k), bank[n][:, :], k == 0, k == ND - 1)
                    mm.then_inc(unit_done, 1)
                ffn_pe(2 + layer, s + 1, w0 + ND)
            for n in range(ND):
                pe.wait_ge(h_new, ND * 7 + n + 1)
                for t in range(TT):
                    mm = nc.tensor.transpose(bank[n][:, P * t:P * t + P], H[:, n, P * t:P * t + P], IDENT)
                mm.then_inc(y_turned, 1)


FENCE_AT = 16512


def pack_columns(inputs):
    def tiles(a):
        return np.asarray(a, np.float32).reshape(-1, P).T

    def halves(a):
        a = np.asarray(a, np.float32).reshape(64, 1)
        return np.concatenate([a, a], 0)

    parts = {
        "f1_pre": tiles(inputs["ffn1_norm_pre"]), "f1_post": tiles(inputs["ffn1_norm_post"]),
        "mx_pre": tiles(inputs["mix_norm_pre"]), "gate_bias": tiles(inputs["gate_bias"]),
        "glu_bias": tiles(inputs["conv_glu_bias"]), "dw_b": tiles(inputs["conv_dw_b"]),
        "ln_g": tiles(inputs["conv_ln_g"]), "ln_b": tiles(inputs["conv_ln_b"]),
        "mx_post": tiles(inputs["mix_norm_post"]), "f2_pre": tiles(inputs["ffn2_norm_pre"]),
        "f2_post": tiles(inputs["ffn2_norm_post"]),
        "dw_w": np.asarray(inputs["conv_dw_w"], np.float32).reshape(TAPS, CH, P).transpose(2, 1, 0).reshape(P, CH * TAPS),
        "attn0": tiles(inputs["attn_norm_w_2"][0]), "attn1": tiles(inputs["attn_norm_w_2"][1]),
        "mem": tiles(inputs["mem_norm_w_2"]),
        "mq0": halves(inputs["mem_q_norm_w_2"][0]), "mq1": halves(inputs["mem_q_norm_w_2"][1]),
        "mk0": halves(inputs["mem_k_norm_w_2"][0]), "mk1": halves(inputs["mem_k_norm_w_2"][1]),
        "ret_gn": tiles(inputs["ret_gn_w_2"]), "dq": halves(inputs["diff_q_norm_w_2"]),
        "dk": halves(inputs["diff_k_norm_w_2"]), "subln": tiles(inputs["diff_subln_w_2"]),
        "ffn0": tiles(inputs["ffn_norm_w_2"][0]), "ffn1": tiles(inputs["ffn_norm_w_2"][1]),
        "lq1": halves(inputs["diff_lambda_q1_2"]), "lk1": halves(inputs["diff_lambda_k1_2"]),
        "lq2": halves(inputs["diff_lambda_q2_2"]), "lk2": halves(inputs["diff_lambda_k2_2"]),
    }
    return np.ascontiguousarray(np.concatenate([parts[name] for name in COLS], 1))


def relative_rows(table):
    p, u = np.arange(P)[:, None], np.arange(256)[None, :]
    return np.ascontiguousarray(np.asarray(table)[0][:, np.minimum(p - u + 256, 256)].transpose(1, 0, 2))


def kernel(**inputs):
    import concourse.bacc as bacc
    from concourse.bass_utils import run_bass_kernel_spmd

    arrays = {"cols": pack_columns(inputs), "rel": relative_rows(inputs["rel_table"]), **shape_constants()}
    for name in ("x", "mem_2", "w_mem_kv_2", "w_in_2", "w_out_2", "w_gate_up_2", "w_down_2"):
        arrays[name] = np.ascontiguousarray(inputs[name])
    for name in ("ffn1_w_gate", "ffn1_w_up", "ffn1_w_down", "w_in", "w_attn_out", "conv_w_out", "w_out",
                 "ffn2_w_gate", "ffn2_w_up", "ffn2_w_down"):
        arrays[name] = np.ascontiguousarray(inputs[name])[0]
    nc = bacc.Bacc("TRN2", target_bir_lowering=False, num_devices=1)
    aps = {name: nc.dram_tensor(f"in_{name}", a.shape, F32, kind="ExternalInput").ap() for name, a in arrays.items()}
    out = nc.dram_tensor("out_y", (1, S, D), F32, kind="ExternalOutput").ap()
    build(nc, aps, out)
    r = run_bass_kernel_spmd(nc, [{f"in_{name}": a for name, a in arrays.items()}], core_ids=[0])
    return r.results[0]["out_y"]
```

```python
from contextlib import ExitStack
import math

import numpy as np
import concourse.bass as bass
from concourse import mybir

F32 = mybir.dt.float32
F32R = mybir.dt.float32r
ALU = mybir.AluOpType
ACT = mybir.ActivationFunctionType
AX_X = mybir.AxisListType.X

P = 128
S = 512
D = 1024
ND = D // P
TT = S // P
FF = 2816
NF = FF // P
EPS = 1e-6
MEM = 256
NMT = MEM // P
NEG = -1e30

HEADS, HD = 8, 64
CH = 512 // P
TAPS = 31
PAD = TAPS - 1
RET_H, DIFF_H, MEM_H = 6, 6, 4
MAIN = 768
NM = MAIN // P
W_IN2 = 3 * MAIN + 256
N_IN2 = W_IN2 // P
N_IN1 = 4608 // P
LAMBDA_INIT = 0.8 - 0.6 * math.exp(-0.3)

RING = 4
AHEAD = 3
LAG = 4

GU = 2 * NF
F1_GU = 0
F1_DN = F1_GU + GU
MX_IN = F1_DN + NF
MX_CO = MX_IN + N_IN1
MX_AO = MX_CO + 4
MX_OUT = MX_AO + 4
F2_GU = MX_OUT + ND
F2_DN = F2_GU + GU
LAYER0 = F2_DN + NF
LAYER_UNITS = 4 + N_IN2 + ND + GU + NF
UNITS = LAYER0 + 2 * LAYER_UNITS

COLS = {}


def _columns():
    at = 0
    for name, n in (
        ("f1_pre", ND), ("f1_post", ND), ("mx_pre", ND), ("gate_bias", 2 * ND), ("glu_bias", 2 * CH),
        ("dw_b", CH), ("ln_g", CH), ("ln_b", CH), ("mx_post", ND), ("f2_pre", ND), ("f2_post", ND),
        ("dw_w", CH * TAPS), ("attn0", ND), ("attn1", ND), ("mem", ND), ("mq0", 1), ("mq1", 1),
        ("mk0", 1), ("mk1", 1), ("ret_gn", RET_H), ("dq", 1), ("dk", 1), ("subln", 1),
        ("ffn0", ND), ("ffn1", ND), ("lq1", 1), ("lk1", 1), ("lq2", 1), ("lk2", 1),
    ):
        COLS[name] = (at, n)
        at += n
    return at


NCOLS = _columns()

SEL64_AT = 2 * P
NCONST = 2 * P + 2


def shape_constants():
    p = np.arange(P)
    const = np.zeros((P, NCONST), np.float32)
    const[p, p] = 1.0
    const[:, P:2 * P] = 1.0
    const[:64, SEL64_AT] = 1.0
    const[64:, SEL64_AT + 1] = 1.0
    spread = np.zeros((12, 6, P), np.float32)
    for i in range(6):
        spread[2 * i, i, :64] = 1.0
        spread[2 * i + 1, i, 64:] = 1.0
    log_gamma = np.log(np.float32(1.0) - np.float32(2.0) ** (np.float32(-5.0) - np.arange(RET_H, dtype=np.float32)))
    u = np.arange(S)
    dist = np.abs(u[None, :] - p[:, None]).astype(np.float32)
    seen = (u[None, :] // 64) >= (p[:, None] // 64)
    decay = np.where(seen[None], np.exp(log_gamma[:, None, None] * dist[None]), 0.0).astype(np.float32)
    decay *= np.float32(0.125)
    slopes = (2.0 ** (-8.0 * np.arange(1, DIFF_H + 1, dtype=np.float32) / DIFF_H)).astype(np.float32)
    rel = u - 384
    dist = np.abs(p[:, None] - rel[None, :]).astype(np.float32)
    seen = np.floor_divide(rel[None, :], 64) <= (p[:, None] // 64)
    alibi = np.float32(8.0) * np.where(seen[None], -slopes[:, None, None] * dist[None], np.float32(NEG)).astype(np.float32)
    return {
        "const": const,
        "spread": spread.reshape(12, 6 * P),
        "decay": np.ascontiguousarray(decay.transpose(1, 0, 2)),
        "alibi": np.ascontiguousarray(alibi.transpose(1, 0, 2)),
    }


class Attention:

    def __init__(self, name, steps, maps, per_group, first_step, first_group):
        self.name, self.steps, self.maps, self.per_group = name, steps, maps, per_group
        self.s0, self.g0 = first_step, first_group
        self.m0 = None


ORDER2 = [[18, 19, 0, 1, 2, 3, 4, 5] + list(range(6, 18)), list(range(6, 12)) + [18, 19] + list(range(6)) + list(range(12, 18))]
ORDER1 = list(range(8)) + list(range(12, 20)) + list(range(8, 12)) + list(range(20, 36))

def beside_mixer():
    plan = [[] for _ in range(N_IN1)]
    for a in range(4):
        plan[13 + a].append(("turn", a))
    for it in range(HEADS * TT + LAG):
        plan[17 + it // 2].append(("b1", it))
    for t in range(CH):
        plan[31].append(("ln_sum", t))
        plan[32].append(("ln_var", t))
        plan[34].append(("ln_silu", t))
        plan[35].append(("ln_hi", t))
    plan[32].append(("ln_root", 0))
    plan[33].append(("ln_norm", 0))
    return plan


def beside_layer0():
    plan = [[] for _ in range(N_IN2)]
    plan[3] = [("mv", 0), ("mv", 1), ("sq", "mk0", 0), ("sq", "mk0", 1), ("stat", "mk0", 0), ("stat", "mk0", 1), ("root", "mk0")]
    plan[4] = [("rows", "mk0"), ("out", "mk0", 0), ("out", "mk0", 1)]
    plan[5] = [("sq", "qc0", 0), ("sq", "qc0", 1), ("stat", "qc0", 0), ("stat", "qc0", 1), ("root", "qc0")]
    for it in range(MEM_H * TT + LAG):
        plan[6 + it // 5].append(("mem0", it))
    for h, k in enumerate((12, 12, 13, 14, 15, 16)):
        plan[k].append(("sq", "o0", h))
    for a in range(6):
        plan[9 + a].append(("turn", a))
    for it in range(RET_H * TT + 2):
        plan[10 + it // 5].append(("ret", it))
    for h, k in enumerate((12, 12, 13, 14, 15, 16)):
        plan[k].append(("stat", "o0", h))
    plan[16].append(("root", "o0"))
    plan[17].append(("rows", "o0"))
    plan[17] += [("out", "o0", h) for h in range(3)] + [("silu", h) for h in range(3)]
    plan[18] = [("silu", 3), ("out", "o0", 3), ("gated", 0), ("out", "o0", 4), ("gated", 1), ("out", "o0", 5)]
    plan[19] = [("silu", 4), ("gated", 2), ("gated", 3), ("gated", 4)]
    return plan


def beside_layer1():
    plan = [[] for _ in range(N_IN2)]
    plan[3] = [("mv", 0), ("mv", 1), ("sq", "mk1", 0), ("sq", "mk1", 1), ("stat", "mk1", 0), ("stat", "mk1", 1), ("root", "mk1")]
    plan[4] = [("rows", "mk1"), ("out", "mk1", 0), ("out", "mk1", 1)]
    plan[5] = [("sq", "k1", 0), ("sq", "k1", 1), ("stat", "k1", 0), ("sq", "k1", 2), ("stat", "k1", 1), ("sq", "k1", 3),
               ("stat", "k1", 2), ("stat", "k1", 3)]
    plan[6] = [("sq", "k1", 4), ("sq", "k1", 5), ("stat", "k1", 4), ("stat", "k1", 5), ("root", "k1")]
    plan[7] = [("rows", "k1")] + [("out", "k1", i) for i in range(6)]
    plan[8] = [("lam",), ("sq", "qc1", 0), ("sq", "qc1", 1), ("stat", "qc1", 0), ("stat", "qc1", 1), ("root", "qc1")]
    for i in range(6):
        plan[9 + i].append(("sq", "q1", i))
    for it in range(MEM_H * TT + LAG):
        plan[9 + it // 4].append(("mem1", it))
    for i in range(6):
        plan[9 + i].append(("stat", "q1", i))
    plan[14] = [("sq", "q1", 5), ("stat", "q1", 5), ("root", "q1"), ("rows", "q1"), ("out", "q1", 0), ("out", "q1", 1)]
    for h in range(5):
        steps = [("diff", TT * h + i) for i in range(TT)]
        plan[15 + h] = steps[:2] + [("turn", h)] + steps[2:]
        if h < 4:
            plan[15 + h].insert(1, ("out", "q1", 2 + h))
    plan[19] = [("sq", "o1a", 0), ("sq", "o1a", 1), ("diff", 16), ("stat", "o1a", 0), ("stat", "o1a", 1), ("diff", 17),
                ("root", "o1a"), ("turn", 4), ("diff", 18), ("rows", "o1a"), ("diff", 19)]
    return plan


TAIL0 = [("silu", 5)] + [("block", 0, k) for k in (6, 7, 0, 1, 2, 3)] + \
        [("gated", 5), ("low", 5), ("block", 1, 6), ("block", 1, 7), ("block", 0, 4), ("block", 1, 0), ("block", 1, 1), ("block", 0, 5)] + \
        [("block", 1, k) for k in (2, 3, 4, 5)] + [("block", n, k) for n in (2, 3) for k in (6, 7, 0, 1, 2, 3, 4, 5)]
TAIL1 = [("block", 0, 6), ("out", "o1a", 0), ("block", 0, 7), ("out", "o1a", 1), ("diff", 20), ("turn", 5), ("low", 1), ("sq", "o1b", 0), ("block", 0, 0), ("diff", 21),
         ("block", 0, 1), ("stat", "o1b", 0), ("block", 1, 6), ("diff", 22), ("block", 1, 7), ("block", 1, 0), ("sq", "o1b", 1), ("diff", 23),
         ("block", 1, 1), ("stat", "o1b", 1), ("root", "o1b"), ("block", 2, 6), ("diff", 24), ("rows", "o1b"), ("block", 2, 7),
         ("block", 2, 0), ("out", "o1b", 0), ("diff", 25), ("block", 2, 1), ("out", "o1b", 1), ("sq", "o1c", 0), ("diff", 26),
         ("low", 3), ("block", 3, 6), ("block", 3, 7), ("diff", 27), ("block", 3, 0), ("sq", "o1c", 1), ("stat", "o1c", 0), ("block", 3, 1),
         ("block", 0, 2), ("block", 1, 2), ("stat", "o1c", 1), ("root", "o1c"),
         ("block", 2, 2), ("block", 3, 2), ("block", 0, 3), ("rows", "o1c"), ("block", 1, 3), ("block", 2, 3), ("out", "o1c", 0),
         ("block", 3, 3), ("out", "o1c", 1), ("low", 5), ("block", 0, 4), ("block", 1, 4), ("block", 0, 5),
         ("block", 2, 4), ("block", 1, 5), ("block", 3, 4), ("block", 2, 5), ("block", 3, 5)]


def unit_bank(k):
    return (1, 2, 3, 0)[k] if k < 4 else 1 - k % 2


def out_bank(n):
    return (1, 0)[n] if n < 2 else n


MEM_BANK = ((5, 3, 4, 6), (4, 5, 6, 3))


def turn_bank(layer, k):
    return 1 + k % 4 if layer == 0 else k % 4


MIX_BANK = (4, 5, 6, 0, 1, 2, 3, 4)
SPREAD_SLOT = [3, 2, 2]


def build(nc, d, out):
    with ExitStack() as ctx:
        ctx.enter_context(nc.sbuf_tensor("fence", [P, 53200], F32))
        FENCE = FENCE_AT
        taken = [FENCE]

        def place(name, shape, dt, at=None):
            size = 4 * int(np.prod(shape[1:]))
            if at is None:
                at = taken[0]
                taken[0] += (size + 31) // 32 * 32
            return nc.alloc_sbuf_tensor_at(name, shape, dt, offset=at)

        def sem(name):
            return ctx.enter_context(nc.semaphore(name))

        H = place("H", [P, ND, S], F32)
        XH = place("XH", [P, ND, S], F32R)
        XL = place("XL", [P, ND, S], F32R)
        RAW = place("RAW", [P, RING, D], F32)
        WHI = place("WHI", [P, RING, D], F32R)
        WLO = place("WLO", [P, RING, D], F32R)
        R = place("R", [P, S], F32)
        ACC = place("ACC", [P, S], F32)
        SQ = place("SQ", [P, 2, S], F32)
        tmp_at = taken[0]
        TMP = place("TMP", [P, 4, S], F32)
        MTOK = place("MTOK", [P, NMT, D], F32, tmp_at)
        ROWS = place("ROWS", [12, 2, S], F32R, tmp_at)
        COL = place("COL", [P, NCOLS], F32)
        CONST = place("CONST", [P, NCONST], F32)
        EPSC = place("EPSC", [P, 3], F32)
        RT = place("RT", [P, TT], F32)
        PG = place("PG", [P, 2], F32)
        STAT = place("STAT", [P, 32], F32)
        LAM = place("LAM", [P, 8], F32)
        arena = taken[0]
        IDENT, ONES = CONST[:, 0:P], CONST[:, P:2 * P]

        KB = 2048
        AH = place("AH", [P, NF, S], F32R, arena)
        AL = place("AL", [P, NF, S], F32R, arena + NF * KB)
        FG = place("FG", [P, ND, S], F32, arena)
        XTOK = place("XTOK", [P, TT, D], F32, arena)
        U = place("U", [P, N_IN1, S], F32, arena)
        CO = place("CO", [P, CH, S], F32, arena)
        V1 = place("V1", [P, TT, 512], F32, arena + 4 * KB)
        SB1 = place("SB1", [P, 4, S], F32, arena + 16 * KB)
        OH1 = place("OH1", [P, CH, S], F32R, arena + 8 * KB)
        OL1 = place("OL1", [P, CH, S], F32R, arena + 12 * KB)
        CPAD = 544
        C = place("C", [P, CH, CPAD], F32, arena + 36 * KB)
        CNH = place("CNH", [P, CH, S], F32R, arena + 36 * KB)
        CNL = place("CNL", [P, CH, S], F32R, arena)
        PT1 = place("PT1", [P, 2, S], F32, arena + 36 * KB + CH * CPAD * 4)
        BIAS1 = place("BIAS1", [P, HEADS, 256], F32, arena + 38 * KB + CH * CPAD * 4)
        V2 = place("V2", [P, TT, MAIN], F32, arena + 20 * KB)
        TAB = place("TAB", [P, 6, S], F32, arena + 26 * KB)
        SB2 = place("SB2", [P, 6, S], F32, arena + 32 * KB)
        PT2 = place("PT2", [P, 2, S], F32, arena + 38 * KB)
        MKT = place("MKT", [P, NMT, MEM], F32, arena + 40 * KB)
        MV = place("MV", [P, NMT, MEM], F32, arena + 41 * KB)
        SPREAD = place("SPREAD", [P, 6, P], F32, arena + 42 * KB)
        SPREAD_R = place("SPREAD_R", [P, 6, P], F32R, arena + 42 * KB)
        YLM = place("YLM", [P, 2, S], F32R, arena + 42 * KB + 3072)
        GR = place("GR", [P, 48], F32, arena + 44 * KB + 3072)
        RQC = place("RQC", [P, 16], F32, arena + 44 * KB + 3072 + 192)
        MVT = place("MVT", [P, NMT, MEM], F32, arena + 38 * KB)
        MH = place("MH", [P, ND, MEM], F32R, arena + 20 * KB)
        ML = place("ML", [P, ND, MEM], F32R, arena + 24 * KB)
        YH = place("YH", [P, 6, S], F32R, arena)
        YL0 = place("YL0", [P, 6, S], F32R, arena + 20 * KB)
        YL1 = place("YL1", [P, 6, S], F32R, arena + 6 * KB)
        YHM = place("YHM", [P, 2, S], F32R, arena + 18 * KB)
        O2 = place("O2", [P, 6, S], F32, arena + 12 * KB)
        O2R = place("O2R", [P, 6, S], F32, arena + 6 * KB)

        bank = [ctx.enter_context(nc.psum_tensor(f"bank{i}", [P, S], F32)) for i in range(8)]

        const_in, col_in = sem("const_in"), sem("col_in")
        eps_set = sem("eps_set")
        x_in = [sem(f"x_in{i}") for i in range(4)]
        raw_in = [sem(f"raw_in{i}") for i in range(RING)]
        hi_ready, lo_ready, unit_done = sem("hi_ready"), sem("lo_ready"), sem("unit_done")
        tile_ready = sem("tile_ready")
        xT_done = sem("xT_done")
        h_new, xh_ready, x_ready = sem("h_new"), sem("xh_ready"), sem("x_ready")
        sq_ready, acc_done = sem("sq_ready"), sem("acc_done")
        stat_done, root_done, rstd_done = sem("stat_done"), sem("root_done"), sem("rstd_done")
        inv_done, diag_done, spread_done = sem("inv_done"), sem("diag_done"), sem("spread_done")
        g_scaled, silu_done, u_scaled = sem("g_scaled"), sem("silu_done"), sem("u_scaled")
        a_done, ah_ready, al_ready = sem("a_done"), sem("ah_ready"), sem("al_ready")
        fsum_done, fga_done = sem("fsum_done"), sem("fga_done")
        fsq_done, fg_done, fstat_done = sem("fsq_done"), sem("fg_done"), sem("fstat_done")
        froot_done, f_scaled = sem("froot_done"), sem("f_scaled")
        ev = sem("ev")
        glu_sig, c_done, gate_done = sem("glu_sig"), sem("c_done"), sem("gate_done")
        pad_zero = sem("pad_zero")
        tap_done, ptap_mul, ptap_done = sem("tap_done"), sem("ptap_mul"), sem("ptap_done")
        ln_sum, ln_cent, ln_sq, ln_var = sem("ln_sum"), sem("ln_cent"), sem("ln_sq"), sem("ln_var")
        ln_root, ln_rstd, ln_norm = sem("ln_root"), sem("ln_rstd"), sem("ln_norm")
        ln_silu, ln_hi, ln_lo = sem("ln_silu"), sem("ln_hi"), sem("ln_lo")
        yb_done, ya_done, m_done = sem("yb_done"), sem("ya_done"), sem("m_done")
        mh_done, mx_ready = sem("mh_done"), sem("mx_ready")
        v_turned, v_ready = sem("v_turned"), sem("v_ready")
        bias_in, bias_masked = sem("bias_in"), sem("bias_masked")
        qk_done, sb_done, nmax_done = sem("qk_done"), sem("sb_done"), sem("nmax_done")
        exp_done, rinv_done, p_done = sem("exp_done"), sem("rinv_done"), sem("p_done")
        p_turned, pt_ready, pv_done = sem("p_turned"), sem("pt_ready"), sem("pv_done")
        oh_done, ol_done = sem("oh_done"), sem("ol_done")
        mem_in, mem_ss, mem_root = sem("mem_in"), sem("mem_ss"), sem("mem_root")
        mem_rec, mem_norm, mem_turned = sem("mem_rec"), sem("mem_norm"), sem("mem_turned")
        memh_done, meml_done, mem_ev = sem("memh_done"), sem("meml_done"), sem("mem_ev")
        mv_turned, mv_ready = sem("mv_turned"), sem("mv_ready")
        gn_sq, gn_stat, gn_root = sem("gn_sq"), sem("gn_stat"), sem("gn_root")
        gn_rec, gn_spread, gn_out = sem("gn_rec"), sem("gn_spread"), sem("gn_out")
        gn_rows, gn_row_out, gains_set = sem("gn_rows"), sem("gn_row_out"), sem("gains_set")
        gn_row_hi, spread_set = sem("gn_row_hi"), sem("spread_set")
        tab_in, spread_in = sem("tab_in"), sem("spread_in")
        sg_done, ret_qk, ret_decayed, ret_pv, ret_ev = sem("sg_done"), sem("ret_qk"), sem("ret_decayed"), sem("ret_pv"), sem("ret_ev")
        og_gated = sem("og_gated")
        lam_prod, lam_sum, lam_exp, lam_set = sem("lam_prod"), sem("lam_sum"), sem("lam_exp"), sem("lam_set")
        y_turned, y_ready, y_out = sem("y_turned"), sem("y_ready"), sem("y_out")

        def col(name, i=0, rows=slice(None)):
            at, n = COLS[name]
            return COL[rows, at + i:at + i + 1]

        def view(ap):
            return ap.bitcast(F32)

        SITES = ["f1_pre", "mx_pre", "f2_pre", "attn0", "ffn0", "attn1", "ffn1"]
        b1_steps = [(h, i) for h in range(HEADS) for i in range(TT)]
        mem_steps = [(h, i) for h in range(MEM_H) for i in range(TT)]
        diff_steps = [(h, i) for h in range(DIFF_H) for i in range(TT)]
        atts, s0, g0, m0 = {}, 0, 0, 0
        for name, steps, maps, per in (("b1", b1_steps, 1, 8), ("mem0", mem_steps, 1, 8),
                                       ("mem1", mem_steps, 1, 8), ("diff", diff_steps, 2, 4)):
            A = Attention(name, steps, maps, per, s0, g0)
            A.m0 = m0
            atts[name] = A
            s0, g0, m0 = s0 + len(steps), g0 + len(steps) // per, m0 + maps * len(steps)

        def att_width(A, s):
            h, i = A.steps[s]
            return MEM if A.name.startswith("mem") else P * (i + 1)

        def att_q(A, s, c):
            h, i = A.steps[s]
            tok = slice(P * i, P * i + P)
            if A.name == "b1":
                return U[64 * (h % 2):64 * (h % 2) + 64, 8 + h // 2, tok]
            if A.name == "diff":
                return U[64 * c:64 * c + 64, h, tok]
            return U[64 * (h % 2):64 * (h % 2) + 64, 18 + h // 2, tok]

        def att_k(A, s, c):
            h, i = A.steps[s]
            w = att_width(A, s)
            if A.name == "b1":
                return U[64 * (h % 2):64 * (h % 2) + 64, 12 + h // 2, 0:w]
            if A.name == "diff":
                return U[64 * c:64 * c + 64, 6 + h, 0:w]
            return MKT[64 * (h % 2):64 * (h % 2) + 64, h // 2, 0:w]

        def att_v(A, s, j):
            h, i = A.steps[s]
            if A.name == "b1":
                return V1[:, j, 64 * h:64 * h + 64]
            if A.name == "diff":
                return V2[:, j, P * h:P * h + P]
            return MV[:, j, 64 * h:64 * h + 64]

        def att_sb(A, s, c):
            return (SB1[:, s % 4, :] if A.name == "b1" else SB2[:, 4 + s % 2 if c else s % 4, :])

        def att_pt(A, s):
            return PT1[:, s % 2, :] if A.name == "b1" else PT2[:, s % 2, :]

        def att_group_rows(A, s):
            h, i = A.steps[s]
            return slice(0, P) if A.name == "diff" else slice(64 * (h % 2), 64 * (h % 2) + 64)

        def stat_cols(A, s, c):
            k = (s % 4) * A.maps + c
            return STAT[:, k:k + 1], STAT[:, 8 + k:9 + k], STAT[:, 16 + k:17 + k]

        def att_scale(A, s, c):
            h, i = A.steps[s]
            if A.name in ("b1", "diff"):
                return 0.125
            return RQC[:, 4 * i + h:4 * i + h + 1]

        gns, t0, q0 = {}, 0, 0
        for k, (name, n, size, width) in enumerate((
                ("mk0", 2, 64, MEM), ("qc0", 2, 64, S), ("o0", 6, 128, S), ("mk1", 2, 64, MEM), ("k1", 6, 64, S),
                ("qc1", 2, 64, S), ("q1", 6, 64, S), ("o1a", 2, 128, S), ("o1b", 2, 128, S), ("o1c", 2, 128, S))):
            gns[name] = (n, size, width, t0, k, q0)
            t0 += n
            if name not in ("qc0", "qc1"):
                q0 += n

        def gn_tile(name, i):
            return {"qc0": lambda: U[:, 18 + i, :], "qc1": lambda: U[:, 18 + i, :],
                    "mk0": lambda: MKT[:, i, :], "mk1": lambda: MKT[:, i, :],
                    "o0": lambda: O2R[:, i, :], "o1a": lambda: O2[:, i, :], "o1b": lambda: O2[:, 2 + i, :],
                    "o1c": lambda: O2[:, 4 + i, :], "q1": lambda: U[:, i, :], "k1": lambda: U[:, 6 + i, :]}[name]()

        def gn_gain(name, i):
            return {"mk0": lambda: PG[:, 0:1], "mk1": lambda: PG[:, 1:2], "o0": lambda: col("ret_gn", i),
                    "q1": lambda: col("dq"), "k1": lambda: col("dk")}.get(name, lambda: LAM[:, 5:6])()

        def gn_table(name):
            n, size, width, t0, k, q0 = gns[name]
            to = RQC if name in ("qc0", "qc1") else GR
            return to[:, 0:2 * n * (width // P)]

        def gn_source(eng, name, i):
            if name[:2] == "mk":
                eng.wait_ge(mem_ev, 4 * int(name[2]) + i + 1)
            elif name[0] in "qk":
                layer = int(name[-1])
                tile = {"q": 18 if name[1] == "c" else 0, "k": 6}[name[0]] + i
                eng.wait_ge(ev, N_IN1 + N_IN2 * layer + ORDER2[layer].index(tile) + 1)
            elif name == "o0":
                eng.wait_ge(ret_ev, i + 1)
            else:
                eng.wait_ge(oh_done, atts["diff"].g0 + {"a": 0, "b": 2, "c": 4}[name[2]] + i + 1)

        def y_hi(layer, k):
            return YH[:, k, :] if k < 6 else YHM[:, k - 6, :]

        def y_lo(layer, k):
            return YLM[:, k - 6, :] if k >= 6 else YL0[:, k, :] if layer == 0 else YL1[:, k, :]

        V_TILES = [(16, 12, 0), (6, 8, 4), (12, 14, 10)]
        NORMS = ["s0", "p0", "s1", "p1", "s2", "p2", "s3", "s4", "s5", "s6"]
        FG_EARLY, FG0 = (6, 8, 6), (0, 6, 14)
        LO_POOL = [MX_IN + k for k in range(22, 36)] + [LAYER0 + LAYER_UNITS + 4 + k for k in range(14, 24)]
        E0 = [0, N_IN1, N_IN1 + N_IN2]

        def v_place(phase, a):
            return (V1 if phase == 0 else V2)[:, :, P * a:P * a + P]

        ROWED = ["mk0", "o0", "mk1", "k1", "q1", "o1a", "o1b", "o1c"]
        PLAN1, PLAN2, TAIL = beside_mixer(), [beside_layer0(), beside_layer1()], [TAIL0, TAIL1]

        block = ctx.enter_context(nc.Block())

        @block.sync
        def _(sp):
            def x_quarter(i):
                part = slice(2 * P * i, 2 * P * (i + 1))
                sp.dma_start(XTOK[:, :, part], d["x"][0].rearrange("(t p) n -> p t n", p=P)[:, :, part]).then_inc(x_in[i], 16)

            sp.dma_start(CONST[:, :], d["const"]).then_inc(const_in, 16)
            x_quarter(0)

            def load(u, j, src):
                if not isinstance(u, int) or u >= RING:
                    sp.wait_ge(lo_ready, u - RING + 1)
                slot = RAW[:, j, :]
                if len(src.shape) == 3:
                    slot = slot.rearrange("p (t n) -> p t n", n=src.shape[2])
                sp.dma_start(slot, src).then_inc(raw_in[j], 16)

            def tile_src(w, n):
                return w.rearrange("(t p) n -> p t n", p=P)[:, :, bass.ts(n, P)]

            def tiles(w, n0, count, u0):
                done = 0
                if u0 < RING:
                    for k in range(4):
                        load(u0 + k, (u0 + k) % RING, tile_src(w, n0 + k))
                    done = 4
                if count - done >= 4:
                    with sp.Fori(done // 4, count // 4) as i:
                        for k in range(4):
                            load(u0 + i * 4 + k, (u0 + k) % RING, tile_src(w, n0 + i * 4 + k))
                for k in range(count // 4 * 4, count):
                    load(u0 + k, (u0 + k) % RING, tile_src(w, n0 + k))

            def ffn(wg, wu, up0, wd, u0):
                def body(i, first):
                    for k in range(4):
                        if u0 == 0 and first and k == 2:
                            sp.dma_start(COL[:, :], d["cols"]).then_inc(col_in, 16)
                            for q in (1, 2, 3):
                                x_quarter(q)
                        w, off = (wg, 0) if k % 2 == 0 else (wu, up0)
                        load(u0 + i * 4 + k, (u0 + k) % RING, tile_src(w, off + i * 2 + k // 2))
                lo = 0
                if u0 == 0:
                    body(0, True)
                    lo = 1
                with sp.Fori(lo, NF // 2) as i:
                    body(i, False)
                v0 = u0 + GU
                rows = wd.rearrange("(t p) n -> t p n", p=P)
                with sp.Fori(0, NF // 4) as i:
                    for k in range(4):
                        load(v0 + i * 4 + k, (v0 + k) % RING, rows[i * 4 + k])
                for k in range(NF // 4 * 4, NF):
                    load(v0 + k, (v0 + k) % RING, rows[k])

            def half_rows(w, u0):
                for k in range(4):
                    load(u0 + k, (u0 + k) % RING, w.rearrange("(t p) n -> p t n", p=P)[:, :, 256 * k:256 * k + 256])

            def second_tables(layer, u0, k):
                if k == 0:
                    sp.wait_ge(unit_done, u0)
                    sp.dma_start(SPREAD[0:12, :, :], d["spread"].rearrange("g (i p) -> g i p", p=P)).then_inc(spread_in, 16)
                if k == 8:
                    sp.wait_ge(unit_done, u0 + 4)
                    sp.dma_start(TAB[:, :, :], d["decay" if layer == 0 else "alibi"]).then_inc(tab_in, 16)

            ffn(d["ffn1_w_gate"], d["ffn1_w_up"], 0, d["ffn1_w_down"], F1_GU)
            tiles(d["w_in"], 12, 8, MX_IN)
            sp.wait_ge(unit_done, MX_IN)
            sp.dma_start(BIAS1[:, :, :], d["rel"]).then_inc(bias_in, 16)
            tiles(d["w_in"], 4, 8, MX_IN + 8)
            tiles(d["w_in"], 0, 4, MX_IN + 16)
            tiles(d["w_in"], 20, 16, MX_IN + 20)
            half_rows(d["conv_w_out"], MX_CO)
            half_rows(d["w_attn_out"], MX_AO)
            tiles(d["w_out"], 0, ND, MX_OUT)
            ffn(d["ffn2_w_gate"], d["ffn2_w_up"], 0, d["ffn2_w_down"], F2_GU)
            for layer in range(2):
                u0 = LAYER0 + layer * LAYER_UNITS
                tiles(d["w_mem_kv_2"][layer], 0, 4, u0)
                for k in range(N_IN2):
                    load(u0 + 4 + k, (u0 + 4 + k) % RING, tile_src(d["w_in_2"][layer], ORDER2[layer][k]))
                    second_tables(layer, u0, k)
                tiles(d["w_out_2"][layer], 0, ND, u0 + 4 + N_IN2)
                ffn(d["w_gate_up_2"][layer], d["w_gate_up_2"][layer], NF, d["w_down_2"][layer], u0 + 4 + N_IN2 + ND)
            for n in range(0, ND, 2):
                sp.wait_ge(y_ready, n + 2)
                sp.dma_start(out[0].rearrange("(t p) n -> p t n", p=P)[:, :, n * P:(n + 2) * P],
                             XTOK[:, :, n * P:(n + 2) * P]).then_inc(y_out, 16)
            sp.wait_ge(y_out, 16 * (ND // 2))

        @block.gpsimd
        def _(pool):
            nc.gpsimd.memset(EPSC[:, 0:1], EPS).then_inc(eps_set, 1)
            nc.gpsimd.memset(EPSC[:, 1:2], 4 * EPS).then_inc(eps_set, 1)
            nc.gpsimd.memset(EPSC[:, 2:3], 64 * EPS).then_inc(eps_set, 1)

            def site_sums(s):
                for n in range(1, ND):
                    pool.wait_ge(sq_ready, ND * s + n + 1)
                    if n >= 2:
                        pool.wait_ge(acc_done, (ND - 1) * s + n - 1)
                    nc.gpsimd.tensor_tensor(ACC[:, :], ACC[:, :], SQ[:, n % 2, :], ALU.add).then_inc(acc_done, 1)

            def odd_updates(p, s):
                for n in range(1, ND, 2):
                    pool.wait_ge(f_scaled, ND * p + n + 1)
                    pool.wait_ge(h_new, ND * s + n)
                    nc.gpsimd.tensor_tensor(H[:, n, :], H[:, n, :], FG[:, n, :], ALU.add).then_inc(h_new, 1)

            def lo(u):
                pool.wait_ge(hi_ready, u + 1)
                pool.wait_ge(lo_ready, u)
                nc.gpsimd.tensor_tensor(WLO[:, u % RING, :], RAW[:, u % RING, :], view(WHI[:, u % RING, :]), ALU.subtract).then_inc(lo_ready, 1)

            site_sums(0)
            pool.wait_ge(unit_done, MX_IN)
            nc.gpsimd.memset(C[:, :, 0:PAD], 0.0).then_inc(pad_zero, 1)
            odd_updates(0, 1)
            pool.wait_ge(c_done, CH)
            pool.wait_ge(pad_zero, 1)
            pool.wait_ge(stat_done, 2)
            t = CH - 1
            for tap in range(TAPS):
                w = col("dw_w", t * TAPS + tap)
                if tap == 0:
                    nc.gpsimd.tensor_scalar(CO[:, t, :], C[:, t, 0:S], w, col("dw_b", t), ALU.mult, ALU.add).then_inc(ptap_done, 1)
                    continue
                if tap >= 3:
                    pool.wait_ge(ptap_done, tap - 1)
                nc.gpsimd.tensor_scalar(SQ[:, tap % 2, :], C[:, t, tap:tap + S], w, 0.0, ALU.mult, ALU.add).then_inc(ptap_mul, 1)
                pool.wait_ge(ptap_mul, tap)
                pool.wait_ge(ptap_done, tap)
                nc.gpsimd.tensor_tensor(CO[:, t, :], CO[:, t, :], SQ[:, tap % 2, :], ALU.add).then_inc(ptap_done, 1)
            for u in LO_POOL[:14]:
                lo(u)
            odd_updates(1, 2)
            odd_updates(2, 3)
            site_sums(4)
            site_sums(5)
            for u in LO_POOL[14:]:
                lo(u)
            site_sums(6)

        @block.scalar
        def _(act):
            def hi(u, j=None):
                if isinstance(u, int):
                    if u >= UNITS:
                        return
                    j = u % RING
                    act.wait_ge(raw_in[j], 16 * (u // RING + 1))
                    if u >= RING:
                        act.wait_ge(unit_done, u - RING + 1)
                nc.scalar.activation(WHI[:, j, :], RAW[:, j, :], ACT.Copy).then_inc(hi_ready, 1)

            def hi_loop(u0, i, k):
                j = (u0 + k) % RING
                act.wait_ge(raw_in[j], (i * 16) + 16 * ((u0 + k) // RING + 1))
                act.wait_ge(unit_done, i * 4 + (u0 + k - RING + 1))
                hi(None, j)

            def hi_any(u0, i, k):
                if isinstance(i, int):
                    hi(u0 + 4 * i + k)
                else:
                    hi_loop(u0, i, k)

            def site_split(s, n):
                act.wait_ge(h_new, ND * s + n + 1)
                nc.scalar.mul(XH[:, n, :], H[:, n, :], col(SITES[s], n)).then_inc(xh_ready, 1)

            def site_square(s, n):
                if n >= 3:
                    act.wait_ge(acc_done, (ND - 1) * s + n - 2)
                nc.scalar.activation(ACC[:, :] if n == 0 else SQ[:, n % 2, :], H[:, n, :], ACT.Square).then_inc(sq_ready, 1)

            def site_act(s, n):
                site_split(s, n)
                site_square(s, n)

            def site_root(s):
                act.wait_ge(stat_done, s + 1)
                nc.scalar.activation(RT[:, :], bank[7][:, 0:TT], ACT.Sqrt, scale=1.0 / D, bias=EPSC[:, 0:1]).then_inc(root_done, 1)

            def site_rstd(s):
                act.wait_ge(spread_done, NORMS.index(f"s{s}") + 1)
                nc.scalar.activation(R[:, :], bank[7][:, :], ACT.Copy).then_inc(rstd_done, 1)

            def ffn_act(f, s, u0, after_gu=None, in_down=None, last=NF):
                T0 = NF * f

                def body(i):
                    first = isinstance(i, int)
                    if first:
                        for k in range(3):
                            hi(u0 + AHEAD + k)
                        site_root(s)
                        site_rstd(s)
                    for t in range(2):
                        if not first:
                            hi_any(u0 + AHEAD, i, 2 * t)
                        act.wait_ge(g_scaled, i * 2 + (T0 + t + 1))
                        nc.scalar.activation(TMP[:, t, :], TMP[:, t, :], ACT.Silu).then_inc(silu_done, 1)
                        if not first or t:
                            hi_any(u0 + AHEAD, i, 2 * t + 1)
                        act.wait_ge(a_done, i * 2 + (T0 + t + 1))
                        nc.scalar.activation(AH[:, i * 2 + t, :], TMP[:, 2 + t, :], ACT.Copy).then_inc(ah_ready, 1)
                body(0)
                with act.Fori(1, NF // 2) as i:
                    body(i)
                if after_gu:
                    after_gu()
                v0 = u0 + GU
                with act.Fori(0, 4) as i:
                    for k in range(4):
                        hi_loop(v0 + AHEAD, i, k)
                if in_down:
                    in_down()
                if last < NF:
                    nc.scalar.preload_act_table(ACT.Sqrt)
                for k in range(16, last):
                    hi(v0 + k + AHEAD)

            def post_square(p, n, wait):
                wait(act, n)
                if n >= 3:
                    act.wait_ge(fsum_done, (ND - 1) * p + n - 2)
                nc.scalar.activation(ACC[:, :] if n == 0 else SQ[:, n % 2, :], bank[MIX_BANK[n] if p == 1 else n][:, :], ACT.Square).then_inc(fsq_done, 1)

            def post_root(p):
                four = 1 if p == 1 else 4
                act.wait_ge(fstat_done, p + 1)
                nc.scalar.activation(RT[:, :], bank[7 if p == 1 else 0][:, 0:TT], ACT.Sqrt, scale=four / D,
                                     bias=EPSC[:, four // 4:four // 4 + 1]).then_inc(froot_done, 1)
                for n in range(FG_EARLY[p], ND):
                    nc.scalar.mul(FG[:, n, :], bank[n][:, :], col("f1_post" if p == 0 else "f2_post", n)).then_inc(fga_done, 1)

            def down_wait(e, t8):
                def wait(eng, n):
                    if n < ND - 1:
                        eng.wait_ge(tile_ready, (ND - 1) * t8 + n + 1)
                    else:
                        eng.wait_ge(unit_done, e)
                return wait

            def attention_act(A, it):
                n = len(A.steps)
                if it < n:
                    w = att_width(A, it)
                    for c in range(A.maps):
                        nmax, total, _ = stat_cols(A, it, c)
                        act.wait_ge(nmax_done, A.m0 + it * A.maps + c + 1)
                        src = att_sb(A, it, c)[:, 0:w]
                        if A.name.startswith("mem"):
                            if it >= 4:
                                act.wait_ge(p_turned, A.s0 + it - 3)
                            nc.scalar.activation(src, bank[2 + it % 2][:, 0:w], ACT.Exp, scale=att_scale(A, it, c), bias=nmax,
                                                 accum_out=total).then_inc(exp_done, 1)
                        else:
                            nc.scalar.activation(src, src, ACT.Exp, scale=0.125 if A.name == "diff" else 1.0, bias=nmax,
                                                 accum_out=total).then_inc(exp_done, 1)
                s = it - 3
                if 0 <= s < n:
                    w = att_width(A, s)
                    act.wait_ge(p_turned, A.s0 + s + 1)
                    if s >= 2:
                        act.wait_ge(pv_done, A.s0 + s - 1)
                    nc.scalar.activation(att_pt(A, s)[:, 0:w], bank[4 + s % 2][:, 0:w], ACT.Copy).then_inc(pt_ready, 1)
                s = it - LAG
                if s >= 0 and s % A.per_group == A.per_group - 1:
                    g = s // A.per_group
                    act.wait_ge(pv_done, A.s0 + s + 1)
                    dst = O2[:, g, :] if A.name == "diff" else OH1[:, g, :] if A.name == "b1" else YHM[:, g, :]
                    nc.scalar.activation(dst, bank[6][:, :], ACT.Copy).then_inc(oh_done, 1)

            def stage(phase, what):
                kind = what[0]
                if kind in atts:
                    attention_act(atts[kind], what[1])
                elif kind == "turn":
                    a = what[1]
                    tile, unit, before = V_TILES[phase]
                    if phase == 0 and a == 0:
                        act.wait_ge(c_done, CH)
                    act.wait_ge(v_turned, before + a + 1)
                    nc.scalar.activation(v_place(phase, a), bank[unit_bank(unit + a)][:, :].rearrange("p (t f) -> p t f", f=P),
                                         ACT.Copy).then_inc(v_ready, 1)
                elif kind == "sq":
                    name, i = what[1:]
                    n, size, width, t0, k, q0 = gns[name]
                    gn_source(act, name, i)
                    if t0 + i >= 2:
                        act.wait_ge(gn_stat, t0 + i - 1)
                    nc.scalar.activation(SQ[:, (t0 + i) % 2, 0:width], gn_tile(name, i), ACT.Square).then_inc(gn_sq, 1)
                elif kind == "root":
                    name = what[1]
                    n, size, width, t0, k, q0 = gns[name]
                    act.wait_ge(gn_stat, t0 + n)
                    scale, eps = (1.0, 2) if name[:2] == "qc" else (1.0 / size, 0)
                    table = gn_table(name)
                    nc.scalar.activation(table, bank[7][:, 0:table.shape[1]], ACT.Sqrt, scale=scale, bias=EPSC[:, eps:eps + 1]).then_inc(gn_root, 1)
                elif kind == "rows":
                    n, size, width, t0, k, q0 = gns[what[1]]
                    act.wait_ge(gn_rows, ROWED.index(what[1]) + 1)
                    if q0:
                        act.wait_ge(gn_spread, q0)
                    if what[1][:2] == "mk":
                        act.wait_ge(spread_in, 16 * phase)
                        nc.scalar.activation(SPREAD_R[0:12, :, :], SPREAD[0:12, :, :], ACT.Copy).then_inc(spread_set, 1)
                    nc.scalar.activation(ROWS[0:2 * n, 0, 0:width], bank[7][0:2 * n, 0:width], ACT.Copy).then_inc(gn_row_hi, 1)
                elif kind == "out" and what[1][:2] == "o1":
                    h = {"a": 0, "b": 2, "c": 4}[what[1][2]] + what[2]
                    act.wait_ge(gn_out, gns[what[1]][5] + what[2] + 1)
                    nc.scalar.activation(y_hi(1, h), O2[:, h, :], ACT.Copy).then_inc(mh_done, 1)
                elif kind == "mv":
                    b = what[1]
                    act.wait_ge(mv_turned, NMT * (phase - 1) + b + 1)
                    nc.scalar.activation(MV[:, :, P * b:P * b + P], bank[4 + b][:, 0:MEM].rearrange("p (t f) -> p t f", f=P),
                                         ACT.Copy).then_inc(mv_ready, 1)
                elif kind == "lam":
                    act.wait_ge(lam_sum, 1)
                    nc.scalar.activation(LAM[:, 2:4], bank[7][:, 0:2], ACT.Exp).then_inc(lam_exp, 1)
                elif kind == "silu":
                    h = what[1]
                    act.wait_ge(ev, E0[1] + 14 + h + 1)
                    nc.scalar.activation(U[:, 12 + h, :], U[:, 12 + h, :], ACT.Silu).then_inc(sg_done, 1)
                elif kind == "gated":
                    act.wait_ge(og_gated, what[1] + 1)
                    nc.scalar.activation(y_hi(0, what[1]), O2R[:, what[1], :], ACT.Copy).then_inc(mh_done, 1)
                elif kind == "ret":
                    k = what[1] - 2
                    if k >= 0 and k % TT == TT - 1:
                        h = k // TT
                        act.wait_ge(ret_pv, TT * (h + 1))
                        nc.scalar.activation(O2R[:, h, :], bank[4 + h % 2][:, :], ACT.Copy).then_inc(ret_ev, 1)
                elif kind == "ln_var":
                    t = what[1]
                    act.wait_ge(ln_cent, t + 1)
                    if t >= 2:
                        act.wait_ge(ln_var, t - 1)
                    nc.scalar.activation(SQ[:, t % 2, :], CO[:, t, :], ACT.Square).then_inc(ln_sq, 1)
                elif kind == "ln_root":
                    act.wait_ge(ln_var, CH)
                    nc.scalar.activation(ACC[:, :], bank[7][:, :], ACT.Sqrt, scale=1.0 / 512, bias=EPSC[:, 0:1]).then_inc(ln_root, 1)
                elif kind == "ln_silu":
                    t = what[1]
                    act.wait_ge(ln_norm, t + 1)
                    nc.scalar.activation(CO[:, t, :], CO[:, t, :], ACT.Silu, scale=col("ln_g", t), bias=col("ln_b", t)).then_inc(ln_silu, 1)
                elif kind == "ln_hi":
                    t = what[1]
                    act.wait_ge(ln_silu, t + 1)
                    nc.scalar.activation(CNH[:, t, :], CO[:, t, :], ACT.Copy).then_inc(ln_hi, 1)

            hi(0)
            hi(1)
            act.wait_ge(col_in, 16)
            act.wait_ge(eps_set, 3)
            for n in range(ND):
                site_act(0, n)
                if n == 5:
                    hi(2)
            ffn_act(0, 0, F1_GU, last=NF - 1)
            wait = down_wait(MX_IN, 0)
            for n in range(ND):
                post_square(0, n, wait)
            post_root(0)
            hi(MX_IN + AHEAD - 1)
            hi(MX_IN + AHEAD)
            for n in range(ND):
                site_split(1, n)
            for n in range(ND):
                site_square(1, n)

            for k in range(N_IN1):
                if k:
                    hi(MX_IN + k + AHEAD)
                if k == SPREAD_SLOT[0]:
                    site_rstd(1)
                if k == SPREAD_SLOT[0] - 1:
                    site_root(1)
                if k == 8:
                    for a in range(CH):
                        act.wait_ge(ev, 5 + a)
                        nc.scalar.activation(U[:, 4 + a, :], U[:, 4 + a, :], ACT.Sigmoid, bias=col("glu_bias", CH + a)).then_inc(glu_sig, 1)
                for what in PLAN1[k]:
                    stage(0, what)

            def gates(n0):
                for n in range(n0, n0 + ND):
                    act.wait_ge(ev, 20 + n + 1)
                    nc.scalar.activation(U[:, 20 + n, :], U[:, 20 + n, :], ACT.Sigmoid, bias=col("gate_bias", n)).then_inc(gate_done, 1)

            hi(MX_CO + AHEAD)
            gates(ND)
            hi(MX_CO + 1 + AHEAD)
            gates(0)
            hi(MX_CO + 2 + AHEAD)
            hi(MX_CO + 3 + AHEAD)
            for j in range(4):
                hi(MX_AO + j + AHEAD)
                for n in (2 * j, 2 * j + 1):
                    act.wait_ge(m_done, n + 1)
                    nc.scalar.activation(XH[:, n, :], U[:, 20 + n, :], ACT.Copy).then_inc(mh_done, 1)
            for n in range(ND):
                hi(MX_OUT + n + AHEAD)
                post_square(1, n, lambda eng, n: eng.wait_ge(unit_done, MX_OUT + n + 1))
            post_root(1)
            for n in range(ND):
                site_split(2, n)
            for n in range(ND):
                site_square(2, n)

            def mem_load(layer):
                act.wait_ge(al_ready, NF * (2 + layer))
                act.dma_start(MTOK[:, :, :], d["mem_2"][0].rearrange("(t p) n -> p t n", p=P)).then_inc(mem_in, 16)

            def mem_sums(layer):
                act.wait_ge(mem_in, 16 * (layer + 1))
                for t in range(NMT):
                    if t:
                        act.wait_ge(mem_ss, NMT * layer + t)
                    nc.scalar.activation(SQ[:, :, :].rearrange("p a n -> p (a n)"), MTOK[:, t, :], ACT.Square,
                                         accum_out=LAM[:, 6 + t:7 + t]).then_inc(mem_ss, 1)
                act.wait_ge(mem_ss, NMT * (layer + 1))
                nc.scalar.activation(LAM[:, 6:8], LAM[:, 6:8], ACT.Sqrt, scale=1.0 / D, bias=EPSC[:, 0:1]).then_inc(mem_root, 1)

            ffn_act(1, 2, F2_GU, lambda: mem_load(0), lambda: mem_sums(0), NF - 1)

            for layer in range(2):
                u0 = LAYER0 + layer * LAYER_UNITS
                if layer == 0:
                    wait = down_wait(LAYER0, 1)
                    for n in range(ND):
                        post_square(2, n, wait)
                if layer == 0:
                    post_root(2)
                    hi(u0 + AHEAD - 1)
                hi(u0 + AHEAD)
                for k in range(ND):
                    act.wait_ge(mem_turned, ND * layer + k + 1)
                    nc.scalar.mul(MH[:, k, :], bank[turn_bank(layer, k)][:, 0:MEM], col("mem", k)).then_inc(memh_done, 1)
                s = 3 + 2 * layer
                for n in range(ND):
                    site_split(s, n)
                    if layer:
                        site_square(s, n)
                    if n == 3:
                        hi(u0 + 1 + AHEAD)
                    if n == 5:
                        hi(u0 + 2 + AHEAD)
                if layer == 0:
                    for n in range(ND):
                        site_square(s, n)
                hi(u0 + 3 + AHEAD)
                for k in range(N_IN2):
                    hi(u0 + 4 + k + AHEAD)
                    if k == SPREAD_SLOT[1 + layer] - 1:
                        site_root(s)
                    if k == SPREAD_SLOT[1 + layer]:
                        site_rstd(s)
                    for what in PLAN2[layer][k]:
                        stage(1 + layer, what)
                w0 = u0 + 4 + N_IN2
                hi(w0 + AHEAD)
                for what in TAIL[layer]:
                    stage(1 + layer, what)
                for n in range(ND):
                    if n:
                        hi(w0 + n + AHEAD)
                    site_act(s + 1, n)
                if layer == 0:
                    ffn_act(2, s + 1, u0 + 4 + N_IN2 + ND, lambda: mem_load(1), lambda: mem_sums(1))
                else:
                    ffn_act(3, s + 1, u0 + 4 + N_IN2 + ND)
            for n in range(ND):
                act.wait_ge(y_turned, n + 1)
                nc.scalar.activation(XTOK[:, :, P * n:P * n + P], bank[n][:, :].rearrange("p (t f) -> p t f", f=P),
                                     ACT.Copy).then_inc(y_ready, 1)

        @block.vector
        def _(dve):
            def lo(u, j=None):
                if isinstance(u, int):
                    if u >= UNITS:
                        return
                    if u in LO_POOL:
                        return
                    j = u % RING
                    dve.wait_ge(hi_ready, u + 1)
                    if u - 1 in LO_POOL:
                        dve.wait_ge(lo_ready, u)
                nc.vector.tensor_tensor(WLO[:, j, :], RAW[:, j, :], view(WHI[:, j, :]), ALU.subtract).then_inc(lo_ready, 1)

            def lo_any(u0, i, k):
                if isinstance(i, int):
                    lo(u0 + 4 * i + k)
                else:
                    dve.wait_ge(hi_ready, i * 4 + (u0 + k + 1))
                    lo(None, (u0 + k) % RING)

            def site_dve(s, n):
                dve.wait_ge(xh_ready, ND * s + n + 1)
                nc.vector.scalar_tensor_tensor(out=XL[:, n, :], in0=H[:, n, :], scalar=col(SITES[s], n), in1=view(XH[:, n, :]),
                                               op0=ALU.mult, op1=ALU.subtract).then_inc(x_ready, 1)

            def inverse(norm, root, count):
                k = NORMS.index(norm)
                dve.wait_ge(root, count)
                nc.vector.reciprocal(RT[:, :], RT[:, :]).then_inc(inv_done, 1)
                dve.wait_ge(inv_done, k + 1)
                for t in range(TT):
                    nc.vector.tensor_scalar(ACC[:, P * t:P * t + P], IDENT, RT[:, t:t + 1], None, ALU.mult).then_inc(diag_done, 1)

            def site_inverse(s):
                inverse(f"s{s}", root_done, s + 1)

            def site_sums(s):
                for n in range(1, ND):
                    dve.wait_ge(sq_ready, ND * s + n + 1)
                    if n >= 2:
                        dve.wait_ge(acc_done, (ND - 1) * s + n - 1)
                    nc.vector.tensor_tensor(ACC[:, :], ACC[:, :], SQ[:, n % 2, :], ALU.add).then_inc(acc_done, 1)

            def ffn_dve(f, s, u0, in_down=None, last=NF):
                T0 = NF * f

                def al(T, t):
                    dve.wait_ge(ah_ready, T + (T0 + 1))
                    nc.vector.tensor_tensor(AL[:, T, :], TMP[:, 2 + t, :], view(AH[:, T, :]), ALU.subtract).then_inc(al_ready, 1)

                def body(i):
                    first = isinstance(i, int)
                    if first:
                        for k in range(3):
                            lo(u0 + AHEAD + k)
                        site_inverse(s)
                    for t in range(2):
                        if not first:
                            lo_any(u0 + AHEAD, i, 2 * t)
                        dve.wait_ge(unit_done, i * 4 + (u0 + 2 * t + 1))
                        if first and t == 0:
                            dve.wait_ge(rstd_done, s + 1)
                        if not first:
                            dve.wait_ge(a_done, i * 2 + (T0 + t - 1))
                        nc.vector.tensor_tensor(TMP[:, t, :], bank[2 * t][:, :], R[:, :], ALU.mult).then_inc(g_scaled, 1)
                        if not first or t:
                            al(i * 2 + t - 1, 1 - t)
                        if not first or t:
                            lo_any(u0 + AHEAD, i, 2 * t + 1)
                        dve.wait_ge(unit_done, i * 4 + (u0 + 2 * t + 2))
                        if not first:
                            dve.wait_ge(al_ready, i * 2 + (T0 + t - 1))
                        nc.vector.tensor_tensor(TMP[:, 2 + t, :], bank[2 * t + 1][:, :], R[:, :], ALU.mult).then_inc(u_scaled, 1)
                        dve.wait_ge(u_scaled, i * 2 + (T0 + t + 1))
                        dve.wait_ge(silu_done, i * 2 + (T0 + t + 1))
                        nc.vector.tensor_tensor(TMP[:, 2 + t, :], TMP[:, 2 + t, :], TMP[:, t, :], ALU.mult).then_inc(a_done, 1)
                body(0)
                with dve.Fori(1, NF // 2) as i:
                    body(i)
                al(NF - 1, 1)
                v0 = u0 + GU
                with dve.Fori(0, 4) as i:
                    for k in range(4):
                        lo_any(v0 + AHEAD, i, k)
                if in_down:
                    in_down()
                for k in range(16, last):
                    lo(v0 + k + AHEAD)

            def post_gain(p, n, name):
                dve.wait_ge(fsq_done, ND * p + n + 1)
                nc.vector.tensor_scalar(FG[:, n, :], bank[MIX_BANK[n] if p == 1 else n][:, :], col(name, n), None, ALU.mult).then_inc(fg_done, 1)

            def post_sum(p, n):
                dve.wait_ge(fsq_done, ND * p + n + 1)
                if n >= 2:
                    dve.wait_ge(fsum_done, (ND - 1) * p + n - 1)
                nc.vector.tensor_tensor(ACC[:, :], ACC[:, :], SQ[:, n % 2, :], ALU.add).then_inc(fsum_done, 1)

            def post_ffn(p, name):
                post_gain(p, 0, name)
                for n in range(1, ND):
                    post_sum(p, n)
                for n in (1, 2, 3):
                    post_gain(p, n, name)
                inverse(f"p{p}", froot_done, p + 1)
                post_gain(p, 4, name)
                post_gain(p, 5, name)

            def post_update(p, s, early=()):
                dve.wait_ge(fg_done, FG0[p] + FG_EARLY[p])
                dve.wait_ge(spread_done, NORMS.index(f"p{p}") + 1)
                rms = bank[7 if p == 1 else 0]
                early = list(early)

                def scale(n):
                    if n >= FG_EARLY[p]:
                        dve.wait_ge(fga_done, (p // 2) * 2 + n - 5)
                    nc.vector.tensor_tensor(FG[:, n, :], FG[:, n, :], rms[:, :], ALU.mult).then_inc(f_scaled, 1)

                scale(0)
                for n in range(0, ND, 2):
                    dve.wait_ge(f_scaled, ND * p + n + 1)
                    dve.wait_ge(h_new, ND * s + n)
                    nc.vector.tensor_tensor(H[:, n, :], H[:, n, :], FG[:, n, :], ALU.add).then_inc(h_new, 1)
                    if n:
                        site_dve(s, n - 1)
                    scale(n + 1)
                    if n + 2 < ND:
                        scale(n + 2)
                    site_dve(s, n)
                    if n >= 4 and early:
                        lo(early.pop(0))
                site_dve(s, ND - 1)
                site_sums(s)

            def down_ready(e, t8):
                def ready(n):
                    if n < ND - 1:
                        dve.wait_ge(tile_ready, (ND - 1) * t8 + n + 1)
                    else:
                        dve.wait_ge(unit_done, e)
                return ready

            def attention_dve(A, it):
                n = len(A.steps)
                is_mem = A.name.startswith("mem")
                if it == 0:
                    if A.name != "b1":
                        if is_mem:
                            dve.wait_ge(gn_rec, gns["qc" + A.name[3]][4] + 1)
                        dve.wait_ge(p_turned, A.s0)
                    else:
                        dve.wait_ge(v_turned, 4)
                        dve.wait_ge(bias_masked, 1)
                    if A.name == "diff":
                        dve.wait_ge(tab_in, 32)
                if it < n:
                    h, i = A.steps[it]
                    w = att_width(A, it)
                    for c in range(A.maps):
                        m = A.m0 + it * A.maps + c
                        nmax, total, rinv = stat_cols(A, it, c)
                        src = bank[2 + (it * A.maps + c) % 2][:, 0:w]
                        scale = att_scale(A, it, c)
                        dve.wait_ge(qk_done, m + 1)
                        if is_mem:
                            if it >= 4:
                                dve.wait_ge(exp_done, m - 3)
                            nc.vector.tensor_reduce(nmax, src, AX_X, ALU.max, negate=True).then_inc(sb_done, 1)
                            dve.wait_ge(sb_done, m + 1)
                            nc.vector.tensor_scalar(nmax, nmax, scale, None, ALU.mult).then_inc(nmax_done, 1)
                            continue
                        sb = att_sb(A, it, c)
                        if it >= 4:
                            dve.wait_ge(p_turned, A.s0 + it - 3)
                        if c and it >= 2:
                            dve.wait_ge(p_done, A.s0 + it - 1)
                        if A.name == "diff":
                            nc.vector.tensor_tensor_reduce(sb[:, 0:w], src, TAB[:, h, S - w:S], 1.0, -3e38, ALU.add, ALU.max, nmax).then_inc(sb_done, 1)
                            dve.wait_ge(sb_done, m + 1)
                            nc.vector.tensor_scalar(nmax, nmax, -0.125, None, ALU.mult).then_inc(nmax_done, 1)
                            continue
                        near = min(w, 256)
                        if w > near:
                            nc.vector.tensor_scalar(sb[:, 0:w - near], src[:, 0:w - near], scale, BIAS1[:, h, 0:1],
                                                    ALU.mult, ALU.add)
                        nc.vector.scalar_tensor_tensor(out=sb[:, w - near:w], in0=src[:, w - near:w], scalar=scale,
                                                       in1=BIAS1[:, h, 256 - near:256], op0=ALU.mult, op1=ALU.add).then_inc(sb_done, 1)
                        dve.wait_ge(sb_done, m + 1)
                        nc.vector.tensor_reduce(nmax, sb[:, 0:w], AX_X, ALU.max, negate=True).then_inc(nmax_done, 1)
                s = it - 1
                if 0 <= s < n:
                    w = att_width(A, s)
                    m = A.m0 + s * A.maps
                    for c in range(A.maps):
                        _, total, rinv = stat_cols(A, s, c)
                        dve.wait_ge(exp_done, m + c + 1)
                        nc.vector.reciprocal(rinv, total).then_inc(rinv_done, 1)
                    dve.wait_ge(rinv_done, m + A.maps)
                    p0 = att_sb(A, s, 0)[:, 0:w]
                    _, _, r0 = stat_cols(A, s, 0)
                    if A.maps == 1:
                        nc.vector.tensor_scalar(p0, p0, r0, None, ALU.mult).then_inc(p_done, 1)
                    else:
                        _, _, r1 = stat_cols(A, s, 1)
                        nc.vector.tensor_scalar(r1, r1, LAM[:, 4:5], None, ALU.mult).then_inc(lam_prod, 1)
                        nc.vector.tensor_scalar(p0, p0, r0, None, ALU.mult).then_inc(lam_prod, 1)
                        dve.wait_ge(lam_prod, 2 + 2 * (s + 1))
                        nc.vector.scalar_tensor_tensor(out=p0, in0=att_sb(A, s, 1)[:, 0:w], scalar=r1, in1=p0,
                                                       op0=ALU.mult, op1=ALU.add).then_inc(p_done, 1)
                s = it - LAG
                if s >= 0 and s % A.per_group == A.per_group - 1 and A.name != "diff":
                    g = s // A.per_group
                    high, low = (OH1[:, g, :], OL1[:, g, :]) if A.name == "b1" else (YHM[:, g, :], YLM[:, g, :])
                    dve.wait_ge(oh_done, A.g0 + g + 1)
                    nc.vector.tensor_tensor(low, bank[6][:, :], view(high), ALU.subtract).then_inc(ol_done, 1)

            def y_low(layer, h):
                dve.wait_ge(mh_done, ND + 6 * layer + h + 1)
                nc.vector.tensor_tensor(y_lo(layer, h), (O2 if layer else O2R)[:, h, :], view(y_hi(layer, h)), ALU.subtract).then_inc(mx_ready, 1)

            def stage(phase, what):
                kind = what[0]
                if kind in atts:
                    attention_dve(atts[kind], what[1])
                elif kind == "root":
                    k = gns[what[1]][4]
                    table = gn_table(what[1])
                    dve.wait_ge(gn_root, k + 1)
                    nc.vector.reciprocal(table, table).then_inc(gn_rec, 1)
                elif kind == "rows":
                    n, size, width, t0, k, q0 = gns[what[1]]
                    dve.wait_ge(gn_row_hi, ROWED.index(what[1]) + 1)
                    nc.vector.tensor_tensor(ROWS[0:2 * n, 1, 0:width], bank[7][0:2 * n, 0:width], view(ROWS[0:2 * n, 0, 0:width]),
                                            ALU.subtract).then_inc(gn_row_out, 1)
                elif kind == "out":
                    name, i = what[1:]
                    q0 = gns[name][5]
                    width = gns[name][2]
                    dve.wait_ge(gn_spread, q0 + i + 1)
                    tile = gn_tile(name, i)
                    nc.vector.scalar_tensor_tensor(out=tile, in0=tile, scalar=gn_gain(name, i), in1=bank[7][:, 0:width],
                                                   op0=ALU.mult, op1=ALU.mult).then_inc(gn_out, 1)
                    if name[:2] == "o1" and i:
                        y_low(1, {"a": 0, "b": 2, "c": 4}[name[2]] + i - 1)
                elif kind == "low":
                    y_low(phase - 1, what[1])
                elif kind == "lam":
                    dve.wait_ge(lam_exp, 1)
                    nc.vector.tensor_tensor(LAM[:, 4:5], LAM[:, 3:4], LAM[:, 2:3], ALU.subtract).then_inc(lam_set, 1)
                    dve.wait_ge(lam_set, 1)
                    nc.vector.tensor_scalar(LAM[:, 4:5], LAM[:, 4:5], -LAMBDA_INIT, None, ALU.add).then_inc(lam_set, 1)
                    nc.vector.tensor_scalar(LAM[:, 5:6], col("subln"), 1.0 - LAMBDA_INIT, None, ALU.mult).then_inc(lam_set, 1)
                    dve.wait_ge(lam_set, 3)
                elif kind == "gated":
                    h = what[1]
                    dve.wait_ge(gn_out, gns["o0"][5] + h + 1)
                    dve.wait_ge(sg_done, h + 1)
                    nc.vector.tensor_tensor(O2R[:, h, :], O2R[:, h, :], U[:, 12 + h, :], ALU.mult).then_inc(og_gated, 1)
                    if h:
                        y_low(0, h - 1)
                elif kind == "ret" and what[1] < RET_H * TT:
                    k = what[1]
                    h, j = k // TT, k % TT
                    w = S - P * j
                    if k == 0:
                        dve.wait_ge(tab_in, 16)
                        dve.wait_ge(p_turned, atts["mem0"].s0 + 16)
                    dve.wait_ge(ret_qk, k + 1)
                    if k >= 3:
                        dve.wait_ge(ret_pv, k - 2)
                    nc.vector.tensor_tensor(SB2[:, k % 3, 0:w], bank[2 + k % 2][:, 0:w], TAB[:, h, 0:w], ALU.mult).then_inc(ret_decayed, 1)
                elif kind == "ln_sum" and what[1] == CH - 1:
                    dve.wait_ge(ln_sum, 1)
                    for t in range(CH):
                        nc.vector.scalar_tensor_tensor(out=CO[:, t, :], in0=bank[7][:, :], scalar=-1.0 / 512, in1=CO[:, t, :],
                                                       op0=ALU.mult, op1=ALU.add).then_inc(ln_cent, 1)
                elif kind == "ln_root":
                    dve.wait_ge(ln_root, 1)
                    nc.vector.reciprocal(ACC[:, :], ACC[:, :]).then_inc(ln_rstd, 1)
                elif kind == "ln_norm":
                    dve.wait_ge(ln_rstd, 1)
                    for t in range(CH):
                        nc.vector.tensor_tensor(CO[:, t, :], CO[:, t, :], ACC[:, :], ALU.mult).then_inc(ln_norm, 1)
                elif kind == "ln_hi":
                    t = what[1]
                    dve.wait_ge(ln_hi, t + 1)
                    nc.vector.tensor_tensor(CNL[:, t, :], CO[:, t, :], view(CNH[:, t, :]), ALU.subtract).then_inc(ln_lo, 1)

            for n in range(ND):
                if n == 2:
                    lo(0)
                    lo(1)
                    dve.wait_ge(col_in, 16)
                dve.wait_ge(xT_done, n + 1)
                nc.vector.tensor_copy(H[:, n, :], bank[n][:, :]).then_inc(h_new, 1)
                if n >= 2:
                    site_dve(0, n - 2)
                if n == 7:
                    lo(2)
            site_dve(0, ND - 2)
            site_dve(0, ND - 1)
            nc.vector.tensor_tensor(PG[:, 0:1], col("mq0"), col("mk0"), ALU.mult).then_inc(gains_set, 1)
            nc.vector.tensor_tensor(PG[:, 1:2], col("mq1"), col("mk1"), ALU.mult).then_inc(gains_set, 1)
            dve.wait_ge(gains_set, 2)
            nc.vector.tensor_tensor(LAM[0:64, 0:1], col("lq1", 0, slice(0, 64)), col("lk1", 0, slice(0, 64)), ALU.mult).then_inc(lam_prod, 1)
            nc.vector.tensor_tensor(LAM[0:64, 1:2], col("lq2", 0, slice(0, 64)), col("lk2", 0, slice(0, 64)), ALU.mult).then_inc(lam_prod, 1)
            dve.wait_ge(const_in, 16)
            ffn_dve(0, 0, F1_GU, last=NF - 1)
            post_ffn(0, "f1_post")
            post_update(0, 1, (MX_IN + AHEAD - 1, MX_IN + AHEAD))

            def evacuate(phase, s, u_in, k, order):
                last = SPREAD_SLOT[phase]
                if k < last:
                    return
                if k == last:
                    dve.wait_ge(rstd_done, s + 1)
                for j in (range(last + 1) if k == last else [k]):
                    dve.wait_ge(unit_done, u_in + j + 1)
                    nc.vector.tensor_tensor(U[:, order[j], :], bank[unit_bank(j)][:, :], R[:, :], ALU.mult).then_inc(ev, 1)

            def taps(a, b):
                for j in range(a, b):
                    tap, t = j // 3, j % 3
                    w = col("dw_w", t * TAPS + tap)
                    if tap == 0:
                        nc.vector.tensor_scalar(CO[:, t, :], C[:, t, 0:S], w, col("dw_b", t), ALU.mult, ALU.add).then_inc(tap_done, 1)
                        continue
                    dve.wait_ge(tap_done, j - 2)
                    nc.vector.scalar_tensor_tensor(out=CO[:, t, :], in0=C[:, t, tap:tap + S], scalar=w, in1=CO[:, t, :],
                                                   op0=ALU.mult, op1=ALU.add).then_inc(tap_done, 1)

            tap_at = 0
            for k in range(N_IN1):
                if k:
                    lo(MX_IN + k + AHEAD)
                if k == 8:
                    for a in range(CH):
                        dve.wait_ge(glu_sig, a + 1)
                        nc.vector.scalar_tensor_tensor(out=C[:, a, PAD:PAD + S], in0=U[:, a, :], scalar=col("glu_bias", a), in1=U[:, 4 + a, :],
                                                       op0=ALU.add, op1=ALU.mult).then_inc(c_done, 1)
                    dve.wait_ge(pad_zero, 1)
                    dve.wait_ge(c_done, CH)
                if k == 14:
                    dve.wait_ge(bias_in, 16)
                    nc.vector.memset(BIAS1[0:64, :, 192:256], NEG).then_inc(bias_masked, 1)
                n_taps = min(5 if k < 17 else 4, 3 * TAPS - tap_at) if k > 8 else 0
                end = tap_at + n_taps
                for what in PLAN1[k]:
                    stage(0, what)
                    n = min(2, end - tap_at)
                    taps(tap_at, tap_at + n)
                    tap_at += n
                taps(tap_at, end)
                tap_at = end
                if k == SPREAD_SLOT[0] - 1:
                    site_inverse(1)
                evacuate(0, 1, MX_IN, k, ORDER1)
            assert tap_at == 3 * TAPS
            for j in range(4):
                lo(MX_CO + j + AHEAD)
                dve.wait_ge(unit_done, MX_CO + j + 1)
                for n in (2 * j, 2 * j + 1):
                    dve.wait_ge(gate_done, n + 1)
                    nc.vector.tensor_tensor(U[:, 28 + n, :], bank[n % 4][:, :], U[:, 28 + n, :], ALU.mult).then_inc(yb_done, 1)

            def m_lo(n):
                dve.wait_ge(mh_done, n + 1)
                nc.vector.tensor_tensor(XL[:, n, :], U[:, 20 + n, :], view(XH[:, n, :]), ALU.subtract).then_inc(mx_ready, 1)

            for j in range(4):
                lo(MX_AO + j + AHEAD)
                dve.wait_ge(unit_done, MX_AO + j + 1)
                for n in (2 * j, 2 * j + 1):
                    dve.wait_ge(gate_done, ND + n + 1)
                    nc.vector.tensor_tensor(U[:, 20 + n, :], bank[n % 4][:, :], U[:, 20 + n, :], ALU.mult).then_inc(ya_done, 1)
                    dve.wait_ge(ya_done, n + 1)
                    dve.wait_ge(yb_done, n + 1)
                    nc.vector.tensor_tensor(U[:, 20 + n, :], U[:, 20 + n, :], U[:, 28 + n, :], ALU.add).then_inc(m_done, 1)
                    if n:
                        m_lo(n - 1)
            m_lo(ND - 1)
            for n in range(ND):
                lo(MX_OUT + n + AHEAD)
                if n:
                    post_sum(1, n)
                post_gain(1, n, "mx_post")
            inverse("p1", froot_done, 2)
            post_update(1, 2)

            def mem_scale(layer):
                dve.wait_ge(mem_root, layer + 1)
                nc.vector.reciprocal(LAM[:, 6:8], LAM[:, 6:8]).then_inc(mem_rec, 1)
                dve.wait_ge(mem_rec, layer + 1)
                for t in range(NMT):
                    nc.vector.tensor_scalar(MTOK[:, t, :], MTOK[:, t, :], LAM[:, 6 + t:7 + t], None, ALU.mult).then_inc(mem_norm, 1)

            ffn_dve(1, 2, F2_GU, lambda: mem_scale(0), NF - 1)

            for layer in range(2):
                u0 = LAYER0 + layer * LAYER_UNITS
                s = 3 + 2 * layer
                if layer == 0:
                    post_ffn(2, "f2_post")
                else:
                    ready = down_ready(u0, 2)
                    for n in range(ND):
                        ready(n)
                        nc.vector.tensor_tensor(H[:, n, :], H[:, n, :], bank[n][:, :], ALU.add).then_inc(h_new, 1)
                if layer == 0:
                    lo(u0 + AHEAD - 1)
                    lo(u0 + AHEAD)
                for k in range(ND):
                    dve.wait_ge(memh_done, ND * layer + k + 1)
                    nc.vector.scalar_tensor_tensor(out=ML[:, k, :], in0=bank[turn_bank(layer, k)][:, 0:MEM], scalar=col("mem", k), in1=view(MH[:, k, :]),
                                                   op0=ALU.mult, op1=ALU.subtract).then_inc(meml_done, 1)
                if layer:
                    lo(u0 + AHEAD)
                if layer == 0:
                    post_update(2, 3, (u0 + 1 + AHEAD, u0 + 2 + AHEAD))
                else:
                    for n in range(ND):
                        site_dve(s, n)
                        if n == 3:
                            lo(u0 + 1 + AHEAD)
                        if n == 5:
                            lo(u0 + 2 + AHEAD)
                for m in range(4):
                    dve.wait_ge(unit_done, u0 + m + 1)
                    dst = MKT[:, m, :] if m < NMT else MVT[:, m - NMT, :]
                    nc.vector.tensor_copy(dst, bank[MEM_BANK[layer][m]][:, 0:MEM]).then_inc(mem_ev, 1)
                lo(u0 + 3 + AHEAD)

                for k in range(N_IN2):
                    lo(u0 + 4 + k + AHEAD)
                    for what in PLAN2[layer][k]:
                        stage(1 + layer, what)
                    if k == SPREAD_SLOT[1 + layer] - 1:
                        site_inverse(s)
                    evacuate(1 + layer, s, u0 + 4, k, ORDER2[layer])
                w0 = u0 + 4 + N_IN2
                lo(w0 + AHEAD)
                for what in TAIL[layer]:
                    stage(1 + layer, what)
                for n in range(ND):
                    if n:
                        lo(w0 + n + AHEAD)
                    dve.wait_ge(unit_done, w0 + n + 1)
                    nc.vector.tensor_tensor(H[:, n, :], H[:, n, :], bank[out_bank(n)][:, :], ALU.add).then_inc(h_new, 1)
                    if n:
                        site_dve(s + 1, n - 1)
                site_dve(s + 1, ND - 1)
                ffn_dve(2 + layer, s + 1, w0 + ND, (lambda: mem_scale(1)) if layer == 0 else None)
            ready = down_ready(UNITS, 3)
            for n in range(ND):
                ready(n)
                nc.vector.tensor_tensor(H[:, n, :], H[:, n, :], bank[n][:, :], ALU.add).then_inc(h_new, 1)

        @block.tensor
        def _(pe):
            def split_product(j, at, rhs_hi, rhs_lo, dst, start, stop):
                w = slice(at, at + P)
                nc.tensor.matmul(dst, WHI[:, j, w], rhs_hi, start=start, stop=False)
                nc.tensor.matmul(dst, WHI[:, j, w], rhs_lo, start=False, stop=False)
                return nc.tensor.matmul(dst, WLO[:, j, w], rhs_hi, start=False, stop=stop)

            def tile_unit(u, j, dst, xh, xl, before=None, plan=(), phase=0):
                pe.wait_ge(lo_ready, u + 1)
                for k in range(ND):
                    if before:
                        before(k)
                    mm = split_product(j, P * k, xh[:, k, :], xl[:, k, :], dst, k == 0, k == ND - 1)
                    if k == ND - 1:
                        mm.then_inc(unit_done, 1)
                    for n, what in enumerate(plan):
                        if max(1, (n + 1) * ND // (len(plan) + 1)) == k:
                            stage(phase, what)

            def pair(u, banks, xh, xl, before):
                for k in range(ND):
                    before(k)
                    for m in range(2):
                        if k == 0:
                            pe.wait_ge(lo_ready, u + m + 1)
                        mm = split_product((u + m) % RING, P * k, xh[:, k, :], xl[:, k, :], bank[banks[m]][:, :], k == 0, k == ND - 1)
                        if k == ND - 1:
                            mm.then_inc(unit_done, 1)

            def site_stat(s):
                pe.wait_ge(acc_done, (ND - 1) * (s + 1))
                for t in range(TT):
                    mm = nc.tensor.matmul(bank[7][:, t:t + 1], ACC[:, P * t:P * t + P], ONES[:, 0:1], start=True, stop=True)
                mm.then_inc(stat_done, 1)

            def spread(norm, b):
                k = NORMS.index(norm)
                pe.wait_ge(diag_done, TT * (k + 1))
                nc.tensor.matmul(bank[b][:, :], ONES, ACC[:, :], start=True, stop=True).then_inc(spread_done, 1)

            def ffn_pe(f, s, u0, p=None, turn_x=None):
                T0 = NF * f

                def body(i):
                    for k in range(4):
                        pe.wait_ge(g_scaled if k % 2 == 0 else u_scaled, i * 2 + (T0 + k // 2 - 1))
                        tile_unit(i * 4 + (u0 + k), (u0 + k) % RING, bank[k][:, :], XH, XL)

                def arrived(k):
                    if turn_x and k in (1, 3):
                        turn_x(k + 3)
                        turn_x(k + 4)
                    pe.wait_ge(x_ready, ND * s + k + 1)
                    if k == 0:
                        pe.wait_ge(h_new, ND * s + 2)
                pair(u0, (0, 1), XH, XL, arrived)
                if turn_x:
                    pe.wait_ge(h_new, ND)
                tile_unit(u0 + 2, (u0 + 2) % RING, bank[2][:, :], XH, XL)
                site_stat(s)
                tile_unit(u0 + 3, (u0 + 3) % RING, bank[3][:, :], XH, XL, None, [("spread", f"s{s}")])
                with pe.Fori(1, NF // 2) as i:
                    body(i)
                v0 = u0 + GU

                def down(k, j, order, start, stop, tiles):
                    pe.wait_ge(lo_ready, v0 + k + 1)
                    for n in order:
                        mm = split_product(j, P * n, AH[:, k, :], AL[:, k, :], bank[n][:, :], start, stop)
                        if tiles and n < ND - 1:
                            mm.then_inc(tile_ready, 1)
                        if n == ND - 1:
                            mm.then_inc(unit_done, 1)
                    if tiles and p is not None:
                        post_stat(p)

                pe.wait_ge(al_ready, T0 + NF - 2)
                pe.wait_ge(rstd_done, s + 1)
                pe.wait_ge(lo_ready, v0 + 1)
                for n in (4, 5, 6, 7, 0, 1, 2, 3):
                    if n == 0:
                        pe.wait_ge(g_scaled, T0 + NF)
                        pe.wait_ge(u_scaled, T0 + NF)
                    mm = split_product(v0 % RING, P * n, AH[:, 0, :], AL[:, 0, :], bank[n][:, :], True, False)
                mm.then_inc(unit_done, 1)
                down(1, (v0 + 1) % RING, range(ND), False, False, False)
                with pe.Fori(0, (NF - 6) // 4) as i:
                    for k in range(2, 6):
                        pe.wait_ge(lo_ready, i * 4 + (v0 + k + 1))
                        for n in range(ND):
                            mm = split_product((v0 + k) % RING, P * n, AH[:, i * 4 + k, :], AL[:, i * 4 + k, :], bank[n][:, :], False, False)
                        mm.then_inc(unit_done, 1)
                pe.wait_ge(al_ready, T0 + NF)
                for k in range(NF - 4, NF):
                    down(k, (v0 + k) % RING, range(ND), False, k == NF - 1, k == NF - 1)

            def post_stat(p):
                b = 7 if p == 1 else 0
                pe.wait_ge(fsum_done, (ND - 1) * (p + 1))
                if p != 1:
                    pe.wait_ge(fg_done, FG0[p] + 1)
                for t in range(TT):
                    mm = nc.tensor.matmul(bank[b][:, t:t + 1], ACC[:, P * t:P * t + P], ONES[:, 0:1], start=True, stop=True)
                mm.then_inc(fstat_done, 1)
                if p != 2:
                    spread(f"p{p}", b)

            def attention_pe(A, it):
                n = len(A.steps)
                if it == 0 and A.name != "b1":
                    name = "k1" if A.name == "diff" else "mk" + A.name[3]
                    pe.wait_ge(gn_out, gns[name][5] + gns[name][0])
                if it < n:
                    h, i = A.steps[it]
                    w = att_width(A, it)
                    if i == 0 and A.name == "diff":
                        pe.wait_ge(gn_out, gns["q1"][5] + h + 1)
                    if i == 0:
                        pe.wait_ge(ev, {"b1": 16 + h // 2, "mem0": E0[1] + 3, "mem1": E0[2] + 7, "diff": E0[2] + 8 + h}[A.name] + 1)
                    for c in range(A.maps):
                        m = A.m0 + it * A.maps + c
                        k = it * A.maps + c
                        if k >= 2:
                            pe.wait_ge(exp_done if A.name.startswith("mem") else sb_done, m - 1)
                        elif m >= 2:
                            pe.wait_ge(exp_done, A.m0)
                        nc.tensor.matmul(bank[2 + k % 2][:, 0:w], att_q(A, it, c), att_k(A, it, c), start=True, stop=True).then_inc(qk_done, 1)
                s = it - 3
                if 0 <= s < n:
                    w = att_width(A, s)
                    pe.wait_ge(p_done, A.s0 + s + 1)
                    if A.s0 + s >= 2:
                        pe.wait_ge(pt_ready, A.s0 + s - 1)
                    for j in range(w // P):
                        mm = nc.tensor.transpose(bank[4 + s % 2][:, P * j:P * j + P], att_sb(A, s, 0)[:, P * j:P * j + P], IDENT)
                    mm.then_inc(p_turned, 1)
                s = it - LAG
                if 0 <= s < n:
                    h, i = A.steps[s]
                    g = s // A.per_group
                    if s % A.per_group == 0 and A.g0 + g > 0:
                        pe.wait_ge(oh_done if A.name == "diff" and g else ol_done, A.g0 + g)
                    if i == 0 and not A.name.startswith("mem"):
                        pe.wait_ge(v_ready, 4 if A.name == "b1" else V_TILES[2][2] + h + 1)
                    if s == 0 and A.name.startswith("mem"):
                        pe.wait_ge(mv_ready, NMT * (int(A.name[3]) + 1))
                    w = att_width(A, s)
                    pe.wait_ge(pt_ready, A.s0 + s + 1)
                    for j in range(w // P):
                        mm = nc.tensor.matmul(bank[6][att_group_rows(A, s), P * i:P * i + P], att_v(A, s, j),
                                              att_pt(A, s)[:, P * j:P * j + P], start=j == 0, stop=j == w // P - 1)
                    mm.then_inc(pv_done, 1)

            def stage(phase, what):
                kind = what[0]
                if kind in atts:
                    attention_pe(atts[kind], what[1])
                elif kind == "turn":
                    a = what[1]
                    tile, unit, before = V_TILES[phase]
                    pe.wait_ge(ev, E0[phase] + unit + a + 1)
                    for t in range(TT):
                        mm = nc.tensor.transpose(bank[unit_bank(unit + a)][:, P * t:P * t + P], U[:, tile + a, P * t:P * t + P], IDENT)
                    mm.then_inc(v_turned, 1)
                elif kind == "spread":
                    spread(what[1], 7)
                elif kind == "mv":
                    b = what[1]
                    pe.wait_ge(mem_ev, 4 * (phase - 1) + NMT + b + 1)
                    for t in range(NMT):
                        mm = nc.tensor.transpose(bank[4 + b][:, P * t:P * t + P], MVT[:, b, P * t:P * t + P], IDENT)
                    mm.then_inc(mv_turned, 1)
                elif kind == "stat":
                    name, i = what[1:]
                    n, size, width, t0, k, q0 = gns[name]
                    if i == 0:
                        pe.wait_ge(rstd_done, 4 if phase == 1 else 6)
                        if k:
                            pe.wait_ge(gn_root, k)
                            pe.wait_ge(gn_out, q0)
                        if name == "qc1":
                            pe.wait_ge(lam_exp, 1)
                    pe.wait_ge(gn_sq, t0 + i + 1)
                    ones = CONST[:, SEL64_AT:SEL64_AT + 2] if size == 64 else ONES[:, 0:2]
                    for t in range(width // P):
                        at = t * 2 * n + 2 * i
                        mm = nc.tensor.matmul(bank[7][:, at:at + 2], SQ[:, (t0 + i) % 2, P * t:P * t + P], ones, start=True, stop=True)
                    mm.then_inc(gn_stat, 1)
                elif kind == "rows":
                    n, size, width, t0, k, q0 = gns[what[1]]
                    pe.wait_ge(gn_rec, k + 1)
                    for t in range(width // P):
                        mm = nc.tensor.transpose(bank[7][0:2 * n, P * t:P * t + P], GR[:, t * 2 * n:(t + 1) * 2 * n], IDENT)
                    mm.then_inc(gn_rows, 1)
                elif kind == "out":
                    name, i = what[1:]
                    n, size, width, t0, k, q0 = gns[name]
                    if i == 0:
                        pe.wait_ge(spread_set, phase)
                        pe.wait_ge(gn_row_out, ROWED.index(name) + 1)
                    else:
                        pe.wait_ge(gn_out, q0 + i)
                    nc.tensor.matmul(bank[7][:, 0:width], SPREAD_R[0:2 * n, i, :], ROWS[0:2 * n, 0, 0:width], start=True, stop=False)
                    nc.tensor.matmul(bank[7][:, 0:width], SPREAD_R[0:2 * n, i, :], ROWS[0:2 * n, 1, 0:width],
                                     start=False, stop=True).then_inc(gn_spread, 1)
                elif kind == "lam":
                    pe.wait_ge(lam_prod, 2)
                    pe.wait_ge(gn_out, gns["k1"][5] + 6)
                    nc.tensor.matmul(bank[7][:, 0:2], ONES[0:64, :], LAM[0:64, 0:2], start=True, stop=True).then_inc(lam_sum, 1)
                elif kind == "ret":
                    it = what[1]
                    if it < RET_H * TT:
                        h, j = it // TT, it % TT
                        w = S - P * j
                        rows = slice(64 * (h % 2), 64 * (h % 2) + 64)
                        if it == 0:
                            pe.wait_ge(ev, E0[1] + 8)
                            pe.wait_ge(exp_done, atts["mem1"].m0)
                        if it >= 2:
                            pe.wait_ge(ret_decayed, it - 1)
                        nc.tensor.matmul(bank[2 + it % 2][:, 0:w], U[rows, 3 + h // 2, P * j:P * j + P], U[rows, h // 2, P * j:S],
                                         start=True, stop=True).then_inc(ret_qk, 1)
                    k = it - 2
                    if k >= 0:
                        h, j = k // TT, k % TT
                        w = S - P * j
                        if j == 0:
                            pe.wait_ge(v_ready, V_TILES[1][2] + h + 1)
                            if h >= 2:
                                pe.wait_ge(ret_ev, h - 1)
                            else:
                                pe.wait_ge(pt_ready, atts["mem1"].s0)
                        pe.wait_ge(ret_decayed, k + 1)
                        nc.tensor.matmul(bank[4 + h % 2][:, P * j:S], V2[:, j, P * h:P * h + P], SB2[:, k % 3, 0:w],
                                         start=j == 0, stop=j == TT - 1).then_inc(ret_pv, 1)
                elif kind == "ln_sum":
                    t = what[1]
                    if t == 0:
                        pe.wait_ge(tap_done, 3 * TAPS)
                        pe.wait_ge(ptap_done, TAPS)
                    mm = nc.tensor.matmul(bank[7][:, :], ONES, CO[:, t, :], start=t == 0, stop=t == CH - 1)
                    if t == CH - 1:
                        mm.then_inc(ln_sum, 1)
                elif kind == "ln_var":
                    t = what[1]
                    if t == 0:
                        pe.wait_ge(ln_cent, CH)
                    pe.wait_ge(ln_sq, t + 1)
                    nc.tensor.matmul(bank[7][:, :], ONES, SQ[:, t % 2, :], start=t == 0, stop=t == CH - 1).then_inc(ln_var, 1)
                elif kind == "block":
                    n, k = what[1:]
                    layer = phase - 1
                    w0 = LAYER0 + layer * LAYER_UNITS + 4 + N_IN2
                    if k == 6:
                        pe.wait_ge(lo_ready, w0 + n + 1)
                        pe.wait_ge(ev, E0[phase] + N_IN2 - (n == 0))
                        pe.wait_ge(v_ready, V_TILES[phase][2] + (5 if n == 0 and layer else 6))
                        if n >= 2 and layer:
                            pe.wait_ge(sb_done, atts["diff"].m0 + 2 * DIFF_H * TT)
                        elif n >= 2:
                            pe.wait_ge(ret_decayed, RET_H * TT)
                        if n == 0:
                            pe.wait_ge(ol_done, 4 + 2 * (layer + 1))
                    elif k < 6:
                        pe.wait_ge(mx_ready, ND + 6 * layer + k + 1)
                    mm = split_product((w0 + n) % RING, P * k, y_hi(layer, k), y_lo(layer, k), bank[out_bank(n)][:, :], k == 6, k == 5)
                    if k == 5:
                        mm.then_inc(unit_done, 1)

            pe.wait_ge(const_in, 16)
            def turn_x(n):
                if n % 2 == 0:
                    pe.wait_ge(x_in[n // 2], 16)
                for t in range(TT):
                    mm = nc.tensor.transpose(bank[n][:, P * t:P * t + P], XTOK[:, t, P * n:P * n + P], IDENT)
                mm.then_inc(xT_done, 1)

            turn_x(0)
            turn_x(1)
            turn_x(2)
            turn_x(3)
            ffn_pe(0, 0, F1_GU, 0, turn_x)

            def projection(phase, s, u_in, plan, v_unit, n_v):
                last = {}
                for k in range(len(plan)):
                    b = unit_bank(k)
                    if b in last:
                        pe.wait_ge(ev, E0[phase] + last[b] + 1)
                        if v_unit <= last[b] < v_unit + n_v:
                            pe.wait_ge(v_ready, V_TILES[phase][2] + last[b] - v_unit + 1)
                    last[b] = k
                    if k == 0:
                        pair(u_in, (unit_bank(0), unit_bank(1)), XH, XL, lambda kk: pe.wait_ge(x_ready, ND * s + kk + 1))
                    elif k > 1:
                        if k == 2 and phase:
                            pe.wait_ge(mem_ev, 4 * phase)
                        own = [("spread", f"s{s}")] if k == SPREAD_SLOT[phase] else []
                        tile_unit(u_in + k, (u_in + k) % RING, bank[b][:, :], XH, XL, None, own + plan[k], phase)
                    if k == SPREAD_SLOT[phase] - 1:
                        site_stat(s)

            projection(0, 1, MX_IN, PLAN1, 12, 4)

            def half_unit(u, j, xh, xl, wait):
                pe.wait_ge(lo_ready, u + 1)
                for n in range(2):
                    for k in range(4):
                        if wait:
                            wait(k)
                        mm = split_product(u % RING, 256 * k + P * n, xh[:, k, :], xl[:, k, :], bank[(2 * j + n) % 4][:, :],
                                           k == 0, k == 3)
                mm.then_inc(unit_done, 1)

            pe.wait_ge(ev, N_IN1)
            for j in range(4):
                if j >= 2:
                    pe.wait_ge(yb_done, 2 * (j - 1))
                half_unit(MX_CO + j, j, CNH, CNL, (lambda k: pe.wait_ge(ln_lo, k + 1)) if j == 0 else None)
            pe.wait_ge(ol_done, 4)
            for j in range(4):
                if j < 2:
                    pe.wait_ge(yb_done, 4 + 2 * (j + 1))
                else:
                    pe.wait_ge(ya_done, 2 * (j - 1))
                half_unit(MX_AO + j, j, OH1, OL1, None)
            pair(MX_OUT, MIX_BANK, XH, XL, lambda kk: pe.wait_ge(mx_ready, kk + 1))
            pe.wait_ge(ya_done, ND)
            for n in range(2, ND):
                if n == ND - 1:
                    pe.wait_ge(fg_done, FG0[1] + 1)
                tile_unit(MX_OUT + n, (MX_OUT + n) % RING, bank[MIX_BANK[n]][:, :], XH, XL)
            post_stat(1)
            ffn_pe(1, 2, F2_GU, 2)

            for layer in range(2):
                u0 = LAYER0 + layer * LAYER_UNITS
                s = 3 + 2 * layer
                pe.wait_ge(mem_norm, NMT * (layer + 1))
                for k in range(ND):
                    if layer:
                        pe.wait_ge(h_new, ND * s + min(k, 3) + 1)
                    elif k < 4:
                        pe.wait_ge(fg_done, FG0[2] + k + 2)
                    if k == 3 and layer == 0:
                        spread("p2", 0)
                    if k >= 4:
                        pe.wait_ge(meml_done, ND * layer + k - 3)
                    for t in range(NMT):
                        mm = nc.tensor.transpose(bank[turn_bank(layer, k)][:, P * t:P * t + P], MTOK[:, t, P * k:P * k + P], IDENT)
                    mm.then_inc(mem_turned, 1)
                pe.wait_ge(h_new, ND * (s + layer))
                if layer == 0:
                    pe.wait_ge(fg_done, FG0[2] + 6)
                for m in range(4):
                    u = u0 + m
                    if layer == 0 and m == 3:
                        pe.wait_ge(fga_done, 3)
                    if m == 1:
                        pe.wait_ge(meml_done, ND * (layer + 1))
                    tile_unit(u, u % RING, bank[MEM_BANK[layer][m]][:, 0:MEM], MH, ML,
                              (lambda kk: pe.wait_ge(meml_done, ND * layer + kk + 1)) if m == 0 else None)
                projection(1 + layer, s, u0 + 4, PLAN2[layer], V_TILES[1 + layer][1], 6)
                for what in TAIL[layer]:
                    stage(1 + layer, what)
                w0 = u0 + 4 + N_IN2
                if layer:
                    pe.wait_ge(oh_done, atts["diff"].g0 + DIFF_H)
                    pe.wait_ge(gn_out, gns["o1c"][5] + 1)
                for n in range(4, ND):
                    pe.wait_ge(lo_ready, w0 + n + 1)
                    for k in range(ND):
                        mm = split_product((w0 + n) % RING, P * k, y_hi(layer, k), y_lo(layer, k), bank[n][:, :], k == 0, k == ND - 1)
                    mm.then_inc(unit_done, 1)
                ffn_pe(2 + layer, s + 1, w0 + ND)
            for n in range(ND):
                pe.wait_ge(h_new, ND * 7 + n + 1)
                for t in range(TT):
                    mm = nc.tensor.transpose(bank[n][:, P * t:P * t + P], H[:, n, P * t:P * t + P], IDENT)
                mm.then_inc(y_turned, 1)


FENCE_AT = 16512


def pack_columns(inputs):
    def tiles(a):
        return np.asarray(a, np.float32).reshape(-1, P).T

    def halves(a):
        a = np.asarray(a, np.float32).reshape(64, 1)
        return np.concatenate([a, a], 0)

    parts = {
        "f1_pre": tiles(inputs["ffn1_norm_pre"]), "f1_post": tiles(inputs["ffn1_norm_post"]),
        "mx_pre": tiles(inputs["mix_norm_pre"]), "gate_bias": tiles(inputs["gate_bias"]),
        "glu_bias": tiles(inputs["conv_glu_bias"]), "dw_b": tiles(inputs["conv_dw_b"]),
        "ln_g": tiles(inputs["conv_ln_g"]), "ln_b": tiles(inputs["conv_ln_b"]),
        "mx_post": tiles(inputs["mix_norm_post"]), "f2_pre": tiles(inputs["ffn2_norm_pre"]),
        "f2_post": tiles(inputs["ffn2_norm_post"]),
        "dw_w": np.asarray(inputs["conv_dw_w"], np.float32).reshape(TAPS, CH, P).transpose(2, 1, 0).reshape(P, CH * TAPS),
        "attn0": tiles(inputs["attn_norm_w_2"][0]), "attn1": tiles(inputs["attn_norm_w_2"][1]),
        "mem": tiles(inputs["mem_norm_w_2"]),
        "mq0": halves(inputs["mem_q_norm_w_2"][0]), "mq1": halves(inputs["mem_q_norm_w_2"][1]),
        "mk0": halves(inputs["mem_k_norm_w_2"][0]), "mk1": halves(inputs["mem_k_norm_w_2"][1]),
        "ret_gn": tiles(inputs["ret_gn_w_2"]), "dq": halves(inputs["diff_q_norm_w_2"]),
        "dk": halves(inputs["diff_k_norm_w_2"]), "subln": tiles(inputs["diff_subln_w_2"]),
        "ffn0": tiles(inputs["ffn_norm_w_2"][0]), "ffn1": tiles(inputs["ffn_norm_w_2"][1]),
        "lq1": halves(inputs["diff_lambda_q1_2"]), "lk1": halves(inputs["diff_lambda_k1_2"]),
        "lq2": halves(inputs["diff_lambda_q2_2"]), "lk2": halves(inputs["diff_lambda_k2_2"]),
    }
    return np.ascontiguousarray(np.concatenate([parts[name] for name in COLS], 1))


def relative_rows(table):
    p, u = np.arange(P)[:, None], np.arange(256)[None, :]
    return np.ascontiguousarray(np.asarray(table)[0][:, np.minimum(p - u + 256, 256)].transpose(1, 0, 2))


def kernel(**inputs):
    import concourse.bacc as bacc
    from concourse.bass_utils import run_bass_kernel_spmd

    arrays = {"cols": pack_columns(inputs), "rel": relative_rows(inputs["rel_table"]), **shape_constants()}
    for name in ("x", "mem_2", "w_mem_kv_2", "w_in_2", "w_out_2", "w_gate_up_2", "w_down_2"):
        arrays[name] = np.ascontiguousarray(inputs[name])
    for name in ("ffn1_w_gate", "ffn1_w_up", "ffn1_w_down", "w_in", "w_attn_out", "conv_w_out", "w_out",
                 "ffn2_w_gate", "ffn2_w_up", "ffn2_w_down"):
        arrays[name] = np.ascontiguousarray(inputs[name])[0]
    nc = bacc.Bacc("TRN2", target_bir_lowering=False, num_devices=1)
    aps = {name: nc.dram_tensor(f"in_{name}", a.shape, F32, kind="ExternalInput").ap() for name, a in arrays.items()}
    out = nc.dram_tensor("out_y", (1, S, D), F32, kind="ExternalOutput").ap()
    build(nc, aps, out)
    r = run_bass_kernel_spmd(nc, [{f"in_{name}": a for name, a in arrays.items()}], core_ids=[0])
    return r.results[0]["out_y"]
```
